# Optimizing a Trainium2 kernel written in Bass

```python
import jax
import jax.numpy as jnp
from jax import lax
import numpy as np

D_MODEL = 1024
BATCH = 1
SEQ = 1024
DEPTH = 1
DEC_BATCH = 8
DEC_SEQ = 4
PAST_LEN = 8192
PAGE_SIZE = 128

HEAD_DIM = 64
N_ATT_HEADS = 8
N_KV_HEADS = 2
KV_GROUP = N_ATT_HEADS // N_KV_HEADS
WINDOW = 128
ATT_BLOCK = WINDOW
N_RET_HEADS = 4
RET_QK_DIM = 64
RET_V_DIM = 128
RET_CHUNK = 128
N_MEM = 256
N_X_HEADS = 4
X_HEAD_DIM = D_MODEL // N_X_HEADS
X_WIDTH = N_X_HEADS * X_HEAD_DIM
D_FF = 4 * D_MODEL

RMS_EPS = 1e-6
GN_EPS = 1e-5

ATT_Q_W = N_ATT_HEADS * HEAD_DIM
ATT_KV_W = N_KV_HEADS * HEAD_DIM
RET_QK_W = N_RET_HEADS * RET_QK_DIM
RET_V_W = N_RET_HEADS * RET_V_DIM
MIX_OUT = ATT_Q_W + RET_V_W
IN_SIZES = (ATT_Q_W, ATT_KV_W, ATT_KV_W, RET_QK_W, RET_QK_W, RET_V_W, RET_V_W)
D_IN = sum(IN_SIZES)

kernel_name = "hymba_swa_sink_retention_step"

F32 = jnp.float32

def rms_norm(x, g):
    xf = x.astype(F32)
    y = xf * lax.rsqrt(jnp.mean(xf * xf, axis=-1, keepdims=True) + RMS_EPS)
    return (y * g.astype(F32)).astype(x.dtype)

def alibi_slopes():
    s = 2.0 ** (-8.0 * np.arange(1, N_ATT_HEADS + 1) / N_ATT_HEADS)
    return jnp.asarray(s.astype(np.float32)).reshape(N_KV_HEADS, KV_GROUP)

def retention_log_decay():
    g = 1.0 - 2.0 ** (-5.0 - np.arange(N_RET_HEADS))
    return jnp.asarray(np.log(g).astype(np.float32))

def split_projection(z):
    offs = [int(o) for o in np.cumsum(IN_SIZES)[:-1]]
    return jnp.split(z, offs, axis=-1)

def mixer_project(xn, w_in):
    B, L = xn.shape[:2]
    qa, ka, va, qr, kr, vr, gr = split_projection(xn @ w_in)
    ka = ka.reshape(B, L, N_KV_HEADS, HEAD_DIM)
    va = va.reshape(B, L, N_KV_HEADS, HEAD_DIM)
    qr = qr.reshape(B, L, N_RET_HEADS, RET_QK_DIM).astype(F32)
    kr = kr.reshape(B, L, N_RET_HEADS, RET_QK_DIM).astype(F32) * (RET_QK_DIM ** -0.5)
    vr = vr.reshape(B, L, N_RET_HEADS, RET_V_DIM).astype(F32)
    return qa, ka, va, qr, kr, vr, gr

def sink_attention(q, k, v, dist, valid, sinks):
    s = jnp.einsum('bnqhgd,bnkhd->bnhgqk', q, k).astype(F32) * (HEAD_DIM ** -0.5)
    s = s - alibi_slopes()[None, None, :, :, None, None] * dist.astype(F32)[None, None, None, None]
    s = jnp.where(valid[None, :, None, None], s, -jnp.inf)
    sink = sinks.astype(F32).reshape(N_KV_HEADS, KV_GROUP)[None, None, :, :, None, None]
    m = jnp.maximum(jnp.max(s, axis=-1, keepdims=True), sink)
    p = jnp.exp(s - m)
    p = p / (jnp.sum(p, axis=-1, keepdims=True) + jnp.exp(sink - m))
    return jnp.einsum('bnhgqk,bnkhd->bnqhgd', p.astype(v.dtype), v)

def window_attention_prompt(q, k, v, sinks):
    B, S = q.shape[:2]
    nb = S // ATT_BLOCK
    qb = q.reshape(B, nb, ATT_BLOCK, N_KV_HEADS, KV_GROUP, HEAD_DIM)
    kb = k.reshape(B, nb, ATT_BLOCK, N_KV_HEADS, HEAD_DIM)
    vb = v.reshape(B, nb, ATT_BLOCK, N_KV_HEADS, HEAD_DIM)
    pad = ((0, 0), (1, 0), (0, 0), (0, 0), (0, 0))
    kk = jnp.concatenate([jnp.pad(kb[:, :-1], pad), kb], axis=2)
    vv = jnp.concatenate([jnp.pad(vb[:, :-1], pad), vb], axis=2)
    qi = jnp.arange(ATT_BLOCK)[:, None]
    kj = jnp.arange(2 * ATT_BLOCK)[None, :]
    dist = qi + ATT_BLOCK - kj
    key_pos = jnp.arange(nb)[:, None, None] * ATT_BLOCK - ATT_BLOCK + kj[None]
    valid = (dist >= 0)[None] & (dist < WINDOW)[None] & (key_pos >= 0)
    o = sink_attention(qb, kk, vv, dist, valid, sinks)
    return o.reshape(B, S, ATT_Q_W), k[:, -WINDOW:], v[:, -WINDOW:]

def window_attention_sample(q, k, v, buf_k, buf_v, sinks):
    B, L = q.shape[:2]
    kk = jnp.concatenate([buf_k.astype(k.dtype), k], axis=1)
    vv = jnp.concatenate([buf_v.astype(v.dtype), v], axis=1)
    qb = q.reshape(B, 1, L, N_KV_HEADS, KV_GROUP, HEAD_DIM)
    dist = jnp.arange(L)[:, None] + WINDOW - jnp.arange(WINDOW + L)[None, :]
    valid = ((dist >= 0) & (dist < WINDOW))[None]
    o = sink_attention(qb, kk[:, None], vv[:, None], dist, valid, sinks)
    return o.reshape(B, L, ATT_Q_W), kk[:, -WINDOW:], vv[:, -WINDOW:]

def retention_chunk(state, q, k, v, log_g):
    L = q.shape[1]
    idx = jnp.arange(L, dtype=F32)
    diff = idx[:, None] - idx[None, :]
    decay = jnp.where(diff >= 0, jnp.exp(log_g[:, None, None] * jnp.maximum(diff, 0.0)), 0.0)
    inner = jnp.einsum('blhd,bshd->bhls', q, k) * decay[None]
    o = jnp.einsum('bhls,bshe->blhe', inner, v)
    xi = jnp.exp((idx[:, None] + 1.0) * log_g[None, :])
    o = o + jnp.einsum('blhd,bhde->blhe', q, state) * xi[None, :, :, None]
    zeta = jnp.exp((L - 1.0 - idx)[:, None] * log_g[None, :])
    new_state = jnp.exp(log_g * L)[None, :, None, None] * state + jnp.einsum('bshd,sh,bshe->bhde', k, zeta, v)
    return o, new_state

def retention_prompt(q, k, v):
    B, S = q.shape[:2]
    nc = S // RET_CHUNK
    log_g = retention_log_decay()

    def to_chunks(t):
        return jnp.moveaxis(t.reshape(B, nc, RET_CHUNK, *t.shape[2:]), 1, 0)

    def step(state, qkv):
        o, new_state = retention_chunk(state, qkv[0], qkv[1], qkv[2], log_g)
        return new_state, o

    s0 = jnp.zeros((B, N_RET_HEADS, RET_QK_DIM, RET_V_DIM), F32)
    final, o = lax.scan(step, s0, (to_chunks(q), to_chunks(k), to_chunks(v)))
    return jnp.moveaxis(o, 0, 1).reshape(B, S, N_RET_HEADS, RET_V_DIM), final

def mixer_merge(att_o, ret_o, gate, gn_g, gn_b, w_out):
    B, L = att_o.shape[:2]
    mu = jnp.mean(ret_o, axis=-1, keepdims=True)
    var = jnp.mean(jnp.square(ret_o - mu), axis=-1, keepdims=True)
    r = (ret_o - mu) * lax.rsqrt(var + GN_EPS) * gn_g.astype(F32) + gn_b.astype(F32)
    r = r.reshape(B, L, RET_V_W).astype(gate.dtype) * jax.nn.silu(gate)
    return jnp.concatenate([att_o, r.astype(att_o.dtype)], axis=-1) @ w_out

def memory_kv(mem, g_mem, w_xk, w_xv):
    B = mem.shape[0]
    mn = rms_norm(mem, g_mem)
    mk = (mn @ w_xk).reshape(B, N_MEM, N_X_HEADS, X_HEAD_DIM)
    mv = (mn @ w_xv).reshape(B, N_MEM, N_X_HEADS, X_HEAD_DIM)
    return mk, mv

def cross_attend(xn, mk, mv, w_xq, w_xo):
    B, L = xn.shape[:2]
    q = (xn @ w_xq).reshape(B, L, N_X_HEADS, X_HEAD_DIM)
    s = jnp.einsum('bqhd,bkhd->bhqk', q, mk.astype(q.dtype)).astype(F32) * (X_HEAD_DIM ** -0.5)
    p = jax.nn.softmax(s, axis=-1).astype(q.dtype)
    o = jnp.einsum('bhqk,bkhd->bqhd', p, mv.astype(q.dtype))
    return o.reshape(B, L, X_WIDTH) @ w_xo

def sqrelu_mlp(xn, w_up, w_down):
    return jnp.square(jax.nn.relu(xn @ w_up)) @ w_down

def setup_inputs(seed: int = 0) -> dict:
    key = jax.random.key(seed)
    ks = jax.random.split(key, 32)

    def nrm(k, shape, scale):
        return jax.random.normal(k, shape, F32) * scale

    d = DEPTH
    return {
        'x_prompt': nrm(ks[0], (BATCH, SEQ, D_MODEL), 1.0),
        'x_sample': nrm(ks[1], (DEC_BATCH, DEC_SEQ, D_MODEL), 1.0),
        'mem_prompt': nrm(ks[2], (BATCH, N_MEM, D_MODEL), 1.0),
        'cache_win_k': nrm(ks[3], (d, DEC_BATCH, WINDOW, N_KV_HEADS, HEAD_DIM), 1.0),
        'cache_win_v': nrm(ks[4], (d, DEC_BATCH, WINDOW, N_KV_HEADS, HEAD_DIM), 1.0),
        'state_ret': nrm(ks[5], (d, DEC_BATCH, N_RET_HEADS, RET_QK_DIM, RET_V_DIM), 1.0),
        'cache_mem_k': nrm(ks[6], (d, DEC_BATCH, N_MEM, N_X_HEADS, X_HEAD_DIM), 1.0),
        'cache_mem_v': nrm(ks[7], (d, DEC_BATCH, N_MEM, N_X_HEADS, X_HEAD_DIM), 1.0),
        'g_mix': 1.0 + nrm(ks[8], (d, D_MODEL), 0.05),
        'w_in': nrm(ks[9], (d, D_MODEL, D_IN), D_MODEL ** -0.5),
        'attn_sinks': nrm(ks[10], (d, N_ATT_HEADS), 1.0),
        'ret_gn_g': 1.0 + nrm(ks[11], (d, N_RET_HEADS, RET_V_DIM), 0.05),
        'ret_gn_b': nrm(ks[12], (d, N_RET_HEADS, RET_V_DIM), 0.02),
        'w_out': nrm(ks[13], (d, MIX_OUT, D_MODEL), MIX_OUT ** -0.5),
        'g_xattn': 1.0 + nrm(ks[14], (d, D_MODEL), 0.05),
        'g_mem': 1.0 + nrm(ks[15], (d, D_MODEL), 0.05),
        'w_xq': nrm(ks[16], (d, D_MODEL, X_WIDTH), D_MODEL ** -0.5),
        'w_xk': nrm(ks[17], (d, D_MODEL, X_WIDTH), D_MODEL ** -0.5),
        'w_xv': nrm(ks[18], (d, D_MODEL, X_WIDTH), D_MODEL ** -0.5),
        'w_xo': nrm(ks[19], (d, X_WIDTH, D_MODEL), X_WIDTH ** -0.5),
        'g_mlp': 1.0 + nrm(ks[20], (d, D_MODEL), 0.05),
        'w_up': nrm(ks[21], (d, D_MODEL, D_FF), D_MODEL ** -0.5),
        'w_down': nrm(ks[22], (d, D_FF, D_MODEL), D_FF ** -0.5),
        'g_final': 1.0 + nrm(ks[23], (D_MODEL,), 0.05),
    }

def reference(x_prompt, x_sample, mem_prompt, cache_win_k, cache_win_v, state_ret, cache_mem_k, cache_mem_v,
              g_mix, w_in, attn_sinks, ret_gn_g, ret_gn_b, w_out, g_xattn, g_mem, w_xq, w_xk, w_xv, w_xo,
              g_mlp, w_up, w_down, g_final):
    hp, hs = x_prompt, x_sample
    p_wk, p_wv, p_rs, p_mk, p_mv, s_wk, s_wv, s_rs = [], [], [], [], [], [], [], []
    log_g = retention_log_decay()
    for l in range(DEPTH):
        qa, ka, va, qr, kr, vr, gr = mixer_project(rms_norm(hp, g_mix[l]), w_in[l])
        att_o, wk, wv = window_attention_prompt(qa, ka, va, attn_sinks[l])
        ret_o, rs = retention_prompt(qr, kr, vr)
        hp = hp + mixer_merge(att_o, ret_o, gr, ret_gn_g[l], ret_gn_b[l], w_out[l])
        mk, mv = memory_kv(mem_prompt, g_mem[l], w_xk[l], w_xv[l])
        hp = hp + cross_attend(rms_norm(hp, g_xattn[l]), mk, mv, w_xq[l], w_xo[l])
        hp = hp + sqrelu_mlp(rms_norm(hp, g_mlp[l]), w_up[l], w_down[l])
        p_wk.append(wk); p_wv.append(wv); p_rs.append(rs); p_mk.append(mk); p_mv.append(mv)

        qa, ka, va, qr, kr, vr, gr = mixer_project(rms_norm(hs, g_mix[l]), w_in[l])
        att_o, wk, wv = window_attention_sample(qa, ka, va, cache_win_k[l], cache_win_v[l], attn_sinks[l])
        ret_o, rs = retention_chunk(state_ret[l].astype(F32), qr, kr, vr, log_g)
        hs = hs + mixer_merge(att_o, ret_o, gr, ret_gn_g[l], ret_gn_b[l], w_out[l])
        hs = hs + cross_attend(rms_norm(hs, g_xattn[l]), cache_mem_k[l], cache_mem_v[l], w_xq[l], w_xo[l])
        hs = hs + sqrelu_mlp(rms_norm(hs, g_mlp[l]), w_up[l], w_down[l])
        s_wk.append(wk); s_wv.append(wv); s_rs.append(rs)

    y_prompt = rms_norm(hp, g_final)
    y_sample = rms_norm(hs, g_final)
    return (y_prompt, y_sample,
            jnp.stack(p_wk), jnp.stack(p_wv), jnp.stack(p_rs), jnp.stack(p_mk), jnp.stack(p_mv),
            jnp.stack(s_wk), jnp.stack(s_wv), jnp.stack(s_rs))


_drawn_inputs = setup_inputs


def setup_inputs(seed=0):
    import zlib

    import numpy as np

    out = dict(_drawn_inputs(seed))
    spreads = {}
    factors = {'ret_gn_b': 6.893, 'g_xattn': 8.0}
    for name, (base, spread) in spreads.items():
        noise = np.random.default_rng([zlib.crc32(name.encode()), seed]).standard_normal(out[name].shape)
        drawn = base * np.exp(spread * noise) if base else spread * noise
        out[name] = jnp.asarray(drawn.astype(out[name].dtype))
    for name, factor in factors.items():
        out[name] = (out[name] * factor).astype(out[name].dtype)
    return out
```

```python
from contextlib import ExitStack

import numpy as np
import concourse.bass as bass
from concourse import mybir
from concourse.alu_op_type import AluOpType as ALU

ACT = mybir.ActivationFunctionType
AX = mybir.AxisListType
F32 = mybir.dt.float32
F32R = mybir.dt.float32r
ds = bass.ds

P = 128
D = 1024
KB = D // P
TP = 1024
NB = 8
DT = 4
TS = NB * DT
T = TP + TS
NCH = 3
CW = T // NCH
NQ = TP // P
WIN = 128
NH, NKV, G, HD = 8, 2, 4, 64
RH, RQ, RV = 4, 64, 128
NM = 256
XH = 4
DFF = 4096
FC = 4
RMS_EPS, GN_EPS = 1e-6, 1e-5
MASKED = -1e37

U_MEM = 0
U_IN = U_MEM + 16
U_OUT = U_IN + 18
U_XQ = U_OUT + 8
U_XO = U_XQ + 8
U_MLP = U_XO + 8
U_END = U_MLP + FC * 16
LOAD = 48

_T = {}
_at = 0
for _n, _w in (("ident", P), ("ones", P), ("dist", 2 * 256), ("decay", RH * P), ("xi", 2 * P), ("zeta", RH * RQ), ("gl", 2)):
    _T[_n] = (_at, _w)
    _at += _w
N_TAB = _at
_S = {}
_at = 0
for _n, _w in (("bias", NKV * 160), ("decay", RH * TS), ("xi", 2 * TS), ("zeta", RH * RQ), ("own", NB), ("sel", G), ("gl", 2)):
    _S[_n] = (_at, _w)
    _at += _w
N_STAB = _at

SLOPES = [2.0 ** (-8.0 * (i + 1) / NH) for i in range(NH)]


def tables():
    lg = np.log(1.0 - 2.0 ** (-5.0 - np.arange(RH))).astype(np.float32).astype(np.float64)
    t = np.zeros((P, N_TAB), np.float64)
    r = np.arange(P)

    def put(a, m, n, v):
        a[: v.shape[0], m[n][0]:m[n][0] + m[n][1]] = v.reshape(v.shape[0], -1)

    put(t, _T, "ident", np.eye(P))
    put(t, _T, "ones", np.ones((P, P)))
    dist = r[:, None] + WIN - np.arange(2 * WIN)[None]
    later = np.where((dist >= 0) & (dist < WIN), -dist, MASKED)
    first = np.where(np.arange(2 * WIN)[None] < WIN, MASKED, later)
    put(t, _T, "dist", np.stack([first, later], 1))
    d = r[None, :] - r[:, None]
    put(t, _T, "decay", np.stack([np.where(d >= 0, 0.125 * np.exp(lg[h] * np.maximum(d, 0)), 0.0) for h in range(RH)], 1))
    half = r // RQ
    put(t, _T, "xi", np.stack([np.exp((r[None, :] + 1.0) * lg[2 * j + half][:, None]) for j in range(2)], 1))
    put(t, _T, "zeta", np.repeat(0.125 * np.exp((P - 1.0 - r)[:, None] * lg[None]), RQ, 1))
    put(t, _T, "gl", np.stack([np.exp(P * lg[2 * j + half]) for j in range(2)], 1))

    s = np.zeros((P, N_STAB), np.float64)
    b, g, q = r // 16, (r // 4) % 4, r % 4
    bias = np.full((P, NKV, 160), MASKED)
    for kv in range(NKV):
        slope = 8.0 * np.array(SLOPES)[kv * G + g]
        c = np.arange(WIN)[None]
        dist = q[:, None] + WIN - c
        bias[:, kv, :WIN] = np.where((dist >= 0) & (dist < WIN), -slope[:, None] * dist, MASKED)
        c = np.arange(TS)[None]
        dist = q[:, None] - c % DT
        bias[:, kv, WIN:] = np.where((c // DT == b[:, None]) & (dist >= 0), -slope[:, None] * dist, MASKED)
    put(s, _S, "bias", bias)
    w = np.arange(TS)
    d = w[None, :] - w[:, None]
    same = (w[None, :] // DT == w[:, None] // DT) & (d >= 0)
    put(s, _S, "decay", np.stack([np.where(same, 0.125 * np.exp(lg[h] * np.maximum(d, 0)), 0.0) for h in range(RH)], 1))
    put(s, _S, "xi", np.stack([np.exp((w[None, :] % DT + 1.0) * lg[2 * j + half][:, None]) for j in range(2)], 1))
    put(s, _S, "zeta", np.repeat(0.125 * np.exp((DT - 1.0 - w % DT)[:, None] * lg[None]), RQ, 1))
    put(s, _S, "own", (w[:, None] // DT == np.arange(NB)[None]).astype(float))
    put(s, _S, "sel", (g[:, None] == np.arange(G)[None]).astype(float))
    put(s, _S, "gl", np.stack([np.exp(DT * lg[2 * j + half]) for j in range(2)], 1))
    return t.astype(np.float32), s.astype(np.float32)


def chunks_before(u, memory=False):
    if memory or (isinstance(u, int) and u <= U_IN):
        return u
    return u * 3 - 2 * U_IN


def wait(eng, sem, value):
    if isinstance(value, int) and value <= 0:
        return
    eng.wait_ge(sem, value)


class Steps:

    def __init__(self, eng, sem):
        self.eng, self.sem, self.n, self.more = eng, sem, 0, 0

    def did(self, ins):
        ins.then_inc(self.sem, 1)
        self.n += 1

    def settle(self):
        wait(self.eng, self.sem, self.n + self.more)

    def loop(self, first, last, body):
        before = self.n
        body(first)
        steps = self.n - before
        if last - first > 1:
            with self.eng.Fori(first + 1, last) as i:
                if steps:
                    self.more = i * steps - (first + 1) * steps
                body(i)
            self.more = 0
            self.n = before + steps * (last - first)


def layer(nc, io):
    with ExitStack() as ctx:
        start = (nc.sbuf_base + 31) // 32 * 32
        top = [start]

        def place(name, shape, dt=F32, at=None):
            size = 4 * int(np.prod(shape[1:]))
            if at is None:
                at = top[0]
                top[0] = at + (size + 31) // 32 * 32
            t = nc.alloc_sbuf_tensor_at(name, shape, dt, offset=at)
            return t, at

        BLK = T * 4
        hT, at_h = place("hT", [P, KB, T])
        xhi, at_x = place("xhi", [P, KB, T], F32R)
        xlo, at_xl = place("xlo", [P, KB, T], F32R)
        yhi, at_y = place("yhi", [P, KB, T], F32R)
        ylo, _ = place("ylo", [P, KB, T], F32R)
        raw, _ = place("raw", [P, 2, KB, P])
        whi, _ = place("whi", [P, 2, KB, P], F32R)
        wlo, _ = place("wlo", [P, 2, KB, P], F32R)
        tab, at_tab = place("tab", [P, N_TAB])
        ss, at_ss = place("ss", [P, T])
        sq, at_sq = place("sq", [P, T // 2])
        rstd, _ = place("rstd", [P, T])
        gains, _ = place("gains", [P, 5, KB])
        gn, _ = place("gn", [P, 2, RH])
        sink8, _ = place("sink8", [P, NH])
        small, _ = place("small", [P, 96])
        assert top[0] <= nc.sbuf_usable_end, top[0]

        ident = tab[:, _T["ident"][0]:_T["ident"][0] + P]
        ones = tab[:, _T["ones"][0]:_T["ones"][0] + P]

        def table(n):
            a, w = _T[n]
            return tab[:, a:a + w]

        G_MIX, G_X, G_MLP, G_FIN, G_MEM = range(5)

        memx, _ = place("memx", [P, 2, D], at=at_y)
        mnhi, _ = place("mnhi", [P, KB, NM], F32R, at=at_y + 8192)
        mnlo, _ = place("mnlo", [P, KB, NM], F32R, at=at_y + 16384)
        mkvT, _ = place("mkvT", [P, 16, NM], at=at_y + 24576)
        mkv, _ = place("mkv", [P, 2, 2 * D], at=at_y + 40960)
        xin, _ = place("xin", [P, 2, D], at=at_y + 57344)

        za, _ = place("za", [P, 10, T], at=at_y)
        zb, _ = place("zb", [P, 8, T], at=at_h)
        at_m = at_y + 10 * BLK
        stq, _ = place("stq", [P, 2, G, P], at=at_m)
        stk, _ = place("stk", [P, 2, 2 * P], at=at_m + 4096)
        stv, _ = place("stv", [P, 2, 2 * P], at=at_m + 6144)
        sc, _ = place("sc", [P, 2, G, 2 * P], at=at_m + 8192)
        pT, _ = place("pT", [P, 2, G * P], at=at_m + 16384)
        vtok, _ = place("vtok", [P, 2, P], at=at_m + 20480)
        rq, _ = place("rq", [P, 2, 2, P], at=at_m)
        rqx, _ = place("rqx", [P, 2, 2, P], at=at_m + 2048)
        rk, _ = place("rk", [P, 2, 2, P], at=at_m + 4096)
        rv, _ = place("rv", [P, 2, RH, P], at=at_m + 6144)
        krz, _ = place("krz", [P, RH * RQ], at=at_m + 10240)
        vrt, _ = place("vrt", [P, RH * RV], at=at_m + 11264)
        inner, _ = place("inner", [P, RH, P], at=at_m + 13312)
        onrm, _ = place("onrm", [P, RH, RV], at=at_m + 15360)
        rf, _ = place("rf", [P, RH, P], at=at_m + 17408)
        state, _ = place("state", [P, 2, 2, RV], at=at_m + 19456)
        at_s = at_x
        off = [at_s]

        def scratch(name, shape):
            t, a = place(name, shape, at=off[0])
            off[0] += (4 * int(np.prod(shape[1:])) + 31) // 32 * 32
            return t

        stab = scratch("stab", [P, N_STAB])
        kc = scratch("kc", [P, NB, P])
        vc = scratch("vc", [P, NB, P])
        kcT = scratch("kcT", [P, NB, P])
        sT = scratch("sT", [P, NKV * P])
        snT = scratch("snT", [TS, NKV * P])
        ssc = scratch("ssc", [P, NKV, 160])
        psT = scratch("psT", [P, NKV * P])
        pnT = scratch("pnT", [TS, NKV * P])
        kzs = scratch("kzs", [TS, RH * RQ])
        kzm = scratch("kzm", [TS, NB, RH * RQ])
        vrs = scratch("vrs", [TS, RH * RV])
        ins_ = scratch("ins_", [TS, RH, TS])
        oTs = scratch("oTs", [P, RH, TS])
        ons = scratch("ons", [TS, RH, RV])
        rfs = scratch("rfs", [P, RH, TS])
        qxs = scratch("qxs", [P, 2, TS])
        sst, _ = place("sst", [P, NB, 2, RV], at=at_y - 4 * NB * 2 * RV)
        assert off[0] <= at_y - 4 * NB * 2 * RV
        kvtok, _ = place("kvtok", [TS, 2 * P], at=at_ss)
        pw, _ = place("pw", [P, 2 * P], at=at_ss + 1024)

        xq, _ = place("xq", [P, KB, T], at=at_x)
        mkT, _ = place("mkT", [P, KB, NM], at=at_xl)
        mv, _ = place("mv", [P, 2, D], at=at_xl + 8192)
        stx, _ = place("stx", [P, 2, KB, P], at=at_xl + 16384)
        xp, _ = place("xp", [P, XH, NM], at=at_xl + 24576)
        xpT, _ = place("xpT", [P, 2, XH * P], at=at_xl + 28672)
        kx, _ = place("kx", [P, 2, D], at=at_xl + 16384)
        kxT, _ = place("kxT", [P, 2, KB, P], at=at_xl + 24576)
        sxT, _ = place("sxT", [P, 2, P], at=at_xl)
        sxp, _ = place("sxp", [P, NM], at=at_xl + 1024)
        pxT, _ = place("pxT", [P, 2, P], at=at_xl + 2048)
        at_t = at_tab + 4 * 2 * P
        relu, _ = place("relu", [P, 2, CW], at=at_t)
        hsq, _ = place("hsq", [P, 2, CW], at=at_t + 2 * 4 * CW)
        ytok, _ = place("ytok", [P, 4, D], at=at_y)

        ps = ctx.enter_context(nc.psum_tensor("ps", [P, 8, 512], F32))

        def bank(b, n=1):
            return ps[:, b:b + n, :].rearrange("p b c -> p (b c)")

        spill = nc.dram_tensor("spill", [KB, P, T], F32, kind="Internal").ap()
        mkT_d = nc.dram_tensor("mkT_d", [P, KB * NM], F32, kind="Internal").ap()

        sem = {}

        def S(name):
            if name not in sem:
                sem[name] = ctx.enter_context(nc.semaphore(name))
            return sem[name]

        block = ctx.enter_context(nc.Block())

        s_raw = [S("raw_loaded_even"), S("raw_loaded_odd")]
        s_whi, s_wlo = S("w_hi_made"), S("w_lo_made")
        s_mm, s_ev = S("chunk_multiplied"), S("chunk_evacuated")

        def kpn(w):
            return w.rearrange("(k p) n -> p k n", p=P)

        def load_unit(sp, u, q, pieces):
            wait(sp, s_wlo, u - 1)
            for n, (dst, src) in enumerate(pieces):
                last = n == len(pieces) - 1
                sp.dma_start(dst, src).then_inc(s_raw[q], LOAD - 16 * n if last else 16)

        def split_hi(act, u, q, memory=False):
            act.wait_ge(s_raw[q], LOAD // 2 * (u - q) + LOAD)
            wait(act, s_mm, chunks_before(u - 1, memory))
            act.activation(whi[:, q], raw[:, q], ACT.Copy).then_inc(s_whi, 1)

        def split_lo(dve, u, q):
            dve.wait_ge(s_whi, u + 1)
            dve.tensor_tensor(wlo[:, q], raw[:, q], whi[:, q].bitcast(F32), ALU.subtract).then_inc(s_wlo, 1)

        def product(pe, u, q, c, hi, lo, w, memory=False):
            wait(pe, s_ev, chunks_before(u, memory) + c - 1)
            out = ps[:, (q + c) % 2, 0:w]
            for k in range(KB):
                x1, x2 = hi[:, k, c * w:c * w + w], lo[:, k, c * w:c * w + w]
                pe.matmul(out, whi[:, q, k, :], x1, start=k == 0, stop=False)
                pe.matmul(out, whi[:, q, k, :], x2, start=False, stop=False)
                mm = pe.matmul(out, wlo[:, q, k, :], x1, start=False, stop=k == KB - 1)
            mm.then_inc(s_mm, 1)

        def unit(pe, u, q, hi, lo):
            pe.wait_ge(s_wlo, u + 1)
            for c in range(NCH):
                product(pe, u, q, c, hi, lo, CW)

        def pairs(eng, first, n_units, body):
            body(first)
            if n_units > 2:
                with eng.Fori(1, n_units // 2) as i:
                    body(i * 2 + first)

        def chunk(t, m, c):
            return t[:, ds(m, 1), c * CW:(c + 1) * CW].rearrange("p a t -> p (a t)")

        def row(t, m):
            return t[:, ds(m, 1), :].rearrange("p a t -> p (a t)")

        def cols(t, a, b, n):
            return t[:, a:b, ds(n * P, P)]

        s_tab, s_mem, s_x = S("tables_loaded"), S("memory_loaded"), [S("x_loaded_even"), S("x_loaded_odd")]
        s_msq, s_mvar, s_mpow, s_mn = S("memory_squares"), S("memory_variance"), S("memory_rstd"), S("memory_scaled")
        s_mnT, s_mhi, s_mlo = S("memory_turned"), S("memory_hi"), S("memory_lo")
        s_xT, s_xea, s_xed = S("x_turned"), S("x_evacuated_act"), S("x_evacuated_dve")
        s_mt, s_mta, s_mtd, s_mout = S("kv_turned"), S("kv_evacuated_act"), S("kv_evacuated_dve"), S("kv_stored")
        s_hi, s_lo, s_ss = S("operand_hi"), S("operand_lo"), S("squares_summed")
        s_nmm, s_root, s_rstd = S("norm_summed"), S("root_made"), S("rstd_made")
        s_pool, s_dve, s_act = S("pool_steps"), S("dve_steps"), S("act_steps")
        s_spill, s_back = S("residual_spilled"), [S("residual_back_0"), S("residual_back_1")]
        s_silu = S("gate_silu")
        s_wst, s_vT, s_vt = S("win_staged"), S("win_v_turned"), S("win_v_ready")
        s_ws, s_wsb, s_wm, s_we = S("win_scores"), S("win_biased"), S("win_max"), S("win_exp")
        s_wp, s_wpT, s_wpe, s_wo, s_woe = S("win_probs"), S("win_p_turned"), S("win_pT_ready"), S("win_out"), S("win_out_kept")
        s_rst, s_rT, s_krz, s_vrt = S("ret_staged"), S("ret_turned"), S("ret_kz"), S("ret_v")
        s_ri, s_rin, s_ro, s_rs, s_rstate = S("ret_inner"), S("ret_decayed"), S("ret_out"), S("ret_state_sum"), S("ret_state")
        s_rvar, s_rrs, s_ron, s_roT, s_rf, s_rg = S("ret_var"), S("ret_rstd"), S("ret_normed"), S("ret_o_turned"), S("ret_affine"), S("ret_gated")
        s_pwT, s_pwe, s_pret = S("last_window_turned"), S("last_window_ready"), S("ret_state_stored")
        s_sld, s_sst, s_out = S("sample_loaded"), S("sample_state_loaded"), S("stored")
        s_xld, s_xst = S("cross_kv_loaded"), S("cross_staged")
        s_xs, s_xm, s_xe, s_xp = S("cross_scores"), S("cross_max"), S("cross_exp"), S("cross_probs")
        s_xpT, s_xpe, s_xo, s_xoh, s_xol = S("cross_p_turned"), S("cross_pT_ready"), S("cross_out"), S("cross_hi"), S("cross_lo")
        s_kl = [S("sx_loaded_0"), S("sx_loaded_1")]
        s_kT, s_kea, s_ked, s_ksc, s_vx = S("sx_k_turned"), S("sx_k_act"), S("sx_k_dve"), S("sx_scores"), S("sx_values")
        s_relu, s_sqr, s_hhi, s_hlo = S("relu_made"), S("square_made"), S("hidden_hi"), S("hidden_lo")
        s_yT, s_yt, s_yea, s_yed = S("y_scaled"), S("y_turned"), S("y_evac_act"), S("y_evac_dve")
        s_yout = [S(f"y_stored_{i}") for i in range(4)]
        N_TABS = 9
        N_SLD = 3
        XT = NQ + 1
        N_OUT = 2 * (NB + 1) + 2

        half = T // 2
        EPS_N, EPS_G = RMS_EPS, GN_EPS
        msq, mvar, mrs, mhalf = small[:, 8:10], small[:, 10:12], small[:, 12:14], small[:, 16:24]
        wmax, wneg, wdif = small[:, 24:28], small[:, 28:36], small[:, 36:44]
        wsum, wsink, wrec = small[:, 44:52], small[:, 52:60], small[:, 60:68]
        gst, gmv = small[:, 68:92], small[:, 8:16]
        gvar, grs = small[:, 92:96], small[:, 0:4]

        @block.sync
        def _(sp):
            def stream(src, u0, n_units):
                def body(u):
                    for q in range(2):
                        load_unit(sp, u + q, q, [(raw[:, q], src[:, :, ds((u - u0 + q) * P, P)])])
                pairs(sp, u0, n_units, body)

            stream(kpn(io["w_xk"][0]), U_MEM, 8)
            stream(kpn(io["w_xv"][0]), U_MEM + 8, 8)
            wi = kpn(io["w_in"][0])

            def in_q(u):
                for q in range(2):
                    m = u - U_IN + q
                    load_unit(sp, u + q, q, [(raw[:, q, :, 0:HD], wi[:, :, ds(m * HD, HD)]),
                                             (raw[:, q, :, HD:P], wi[:, :, ds(m * HD + G * HD, HD)])])

            pairs(sp, U_IN, 4, in_q)
            stream(wi[:, :, 4 * P:], U_IN + 4, 14)
            wo = io["w_out"][0]
            wo_0, wo_1 = (wo[j * G * HD:(j + 1) * G * HD, :].rearrange("(k p) n -> p k n", p=HD) for j in range(2))
            wo_r = kpn(wo[2 * G * HD:, :])

            def out_units(u):
                for q in range(2):
                    c = ds((u - U_OUT + q) * P, P)
                    load_unit(sp, u + q, q, [(raw[0:HD, q, 0:4, :], wo_0[:, :, c]), (raw[HD:P, q, 0:4, :], wo_1[:, :, c]),
                                             (raw[:, q, 4:8, :], wo_r[:, :, c])])

            pairs(sp, U_OUT, 8, out_units)
            stream(kpn(io["w_xq"][0]), U_XQ, 8)
            stream(kpn(io["w_xo"][0]), U_XO, 8)
            for c in range(FC):
                u0 = U_MLP + 16 * c
                stream(kpn(io["w_up"][0])[:, :, c * D:(c + 1) * D], u0, 8)
                stream(kpn(io["w_down"][0][c * D:(c + 1) * D, :]), u0 + 8, 8)
            yp, ys = io["y_prompt"][0], io["y_sample"].rearrange("b t d -> (b t) d")
            for t in range(XT):
                sp.wait_ge(s_yea, t + 1)
                sp.wait_ge(s_yed, t + 1)
                if t < NQ:
                    sp.dma_start(yp[t * P:(t + 1) * P, :], ytok[:, t % 4, :]).then_inc(s_yout[t % 4], 16)
                else:
                    sp.dma_start(ys, ytok[0:TS, t % 4, :]).then_inc(s_yout[t % 4], 16)
            for i in range(4):
                sp.wait_ge(s_yout[i], 16 * len(range(i, XT, 4)))
            sp.wait_ge(s_out, 16 * N_OUT)
            sp.wait_ge(s_pret, 32)
            sp.wait_ge(s_mout, 48)
            sp.wait_ge(S("smp_state_stored"), 16 * NB)

        @block.gpsimd
        def _(pool):
            st = Steps(pool, s_pool)

            def squares(m, done):
                pool.wait_ge(*done)
                for j in range(2):
                    c = slice(j * half, (j + 1) * half)
                    h = row(hT, m)[:, c]
                    if isinstance(m, int) and m == 0:
                        last = pool.tensor_tensor(ss[:, c], h, h, ALU.mult)
                        if j == 0:
                            st.did(last)
                        continue
                    st.settle()
                    st.did(pool.tensor_tensor(sq[:], h, h, ALU.mult))
                    st.settle()
                    last = pool.tensor_tensor(ss[:, c], ss[:, c], sq[:], ALU.add)
                    if j == 0:
                        st.did(last)
                last.then_inc(s_ss, 1)

            def later_squares(m, done, n_before):
                pool.wait_ge(s_ss, n_before)
                squares(m, done)

            pool.dma_start(memx[:], io["mem_prompt"][0].rearrange("(t p) d -> p t d", p=P)).then_inc(s_mem, 16)
            pool.dma_start(tab[:], io["tables"]).then_inc(s_tab, 16)
            with nc.allow_non_contiguous_dma(reason="vectors of 1024 or 512 onto the partitions"):
                for n, g in ((G_MEM, io["g_mem"][0]), (G_MIX, io["g_mix"][0]), (G_X, io["g_xattn"][0]), (G_MLP, io["g_mlp"][0]), (G_FIN, io["g_final"])):
                    pool.dma_start(gains[:, n, :], g.rearrange("(k p) -> p k", p=P)).then_inc(s_tab, 16)
                pool.dma_start(gn[:, 0, :], io["ret_gn_g"][0].rearrange("h p -> p h")).then_inc(s_tab, 16)
                pool.dma_start(gn[:, 1, :], io["ret_gn_b"][0].rearrange("h p -> p h")).then_inc(s_tab, 16)
                pool.dma_start(sink8[:], io["attn_sinks"][0].partition_broadcast(P)).then_inc(s_tab, 16)
            pool.wait_ge(s_mvar, 1)
            pool.tensor_tensor(mrs, mvar, mhalf[:, 0:2], ALU.pow).then_inc(s_mpow, 1)

            for t in range(XT):
                wait(pool, s_xT, t - 1)
                if t < NQ:
                    pool.dma_start(xin[:, t % 2, :], io["x_prompt"][0, t * P:(t + 1) * P, :]).then_inc(s_x[t % 2], 16)
                else:
                    pool.dma_start(xin[0:TS, t % 2, :], io["x_sample"].rearrange("b t d -> (b t) d")).then_inc(s_x[t % 2], 16)
            pool.wait_ge(s_xea, XT)
            pool.wait_ge(s_xed, XT)
            for k in range(KB):
                pool.dma_start(spill[k], hT[:, k, :]).then_inc(s_spill, 16)
            for k in range(KB):
                if k:
                    pool.wait_ge(s_ss, k)
                squares(k, (s_xed, XT))
            pool.wait_ge(s_ev, 16)
            pool.dma_start(mkT_d, mkvT[:, 0:KB, :].rearrange("p k t -> p (k t)")).then_inc(s_mout, 16)
            pool.wait_ge(s_mta, 4)
            pool.wait_ge(s_mtd, 4)
            pool.dma_start(io["p_mem_k"].rearrange("l b (t p) h d -> p (l b t) (h d)", p=P), mkv[:, :, 0:D]).then_inc(s_mout, 16)
            pool.dma_start(io["p_mem_v"].rearrange("l b (t p) h d -> p (l b t) (h d)", p=P), mkv[:, :, D:]).then_inc(s_mout, 16)

            pool.wait_ge(s_ev, chunks_before(U_IN + 6))

            def win_stage(n2):
                for p in range(2):
                    n = n2 * 2 + p
                    wait(pool, s_wo, n * 2 - 2)
                    prev = n if isinstance(n, int) and n == 0 else n - 1
                    pool.tensor_copy(stq[:, p], cols(za, 0, G, n)).then_inc(s_wst, 1)
                    for dst, b in ((stk, 4), (stv, 5)):
                        pool.tensor_copy(dst[:, p, 0:P], cols(za, b, b + 1, prev).rearrange("p a t -> p (a t)")).then_inc(s_wst, 1)
                        pool.tensor_copy(dst[:, p, P:2 * P], cols(za, b, b + 1, n).rearrange("p a t -> p (a t)")).then_inc(s_wst, 1)

            st.loop(0, NQ // 2, win_stage)

            pool.wait_ge(s_woe, NQ)
            pool.wait_ge(s_silu, 4)

            def ret_stage(n2):
                for p in range(2):
                    n = n2 * 2 + p
                    wait(pool, s_rs, n - 1)
                    pool.tensor_copy(rq[:, p], cols(za, 6, 8, n)).then_inc(s_rst, 1)
                    pool.tensor_tensor(rqx[:, p], cols(za, 6, 8, n), table("xi").rearrange("p (j t) -> p j t", j=2), ALU.mult).then_inc(s_rst, 1)
                    pool.tensor_copy(rk[:, p], cols(za, 8, 10, n)).then_inc(s_rst, 1)
                    pool.tensor_copy(rv[:, p], cols(zb, 4, 8, n)).then_inc(s_rst, 1)
                    pool.wait_ge(s_rvar, n + 1)
                    pool.tensor_tensor(grs, gvar, mhalf[:, 0:4], ALU.pow).then_inc(s_rrs, 1)
                    pool.wait_ge(s_rf, 4 * n + 4)
                    pool.tensor_tensor(cols(zb, 4, 8, n), rf[:], cols(zb, 0, 4, n), ALU.mult).then_inc(s_rg, 1)

            st.loop(0, NQ // 2, ret_stage)
            pool.wait_ge(s_rstate, RH * NQ)
            for e in range(2):
                pool.dma_start(io["p_ret"][0, 0].rearrange("(j h) d e -> h d j e", h=2)[e], state[e * RQ:(e + 1) * RQ, :, e, :]).then_inc(s_pret, 16)

            pool.wait_ge(s_mm, chunks_before(U_OUT))
            pool.dma_start(stab[:], io["sample_tables"]).then_inc(s_sld, 16)
            pool.dma_start(kc[:], io["cache_win_k"][0].rearrange("b k h d -> k b (h d)")).then_inc(s_sld, 16)
            pool.dma_start(vc[:], io["cache_win_v"][0].rearrange("b k h d -> k b (h d)")).then_inc(s_sld, 16)
            for b in range(NB):
                pool.dma_start(sst[:, b], io["state_ret"][0, b].rearrange("(j h) d e -> (h d) j e", h=2)).then_inc(s_sst, 16)
            pool.wait_ge(S("smp_var"), 1)
            pool.tensor_tensor(grs[0:TS], gvar[0:TS], mhalf[0:TS, 0:4], ALU.pow).then_inc(S("smp_rstd"), 1)
            pool.wait_ge(S("smp_affine"), 4)
            pool.tensor_tensor(zb[:, 4:8, TP:T], rfs[:], zb[:, 0:4, TP:T], ALU.mult).then_inc(S("smp_gated"), 1)
            pool.wait_ge(S("smp_gated"), 1)
            pool.wait_ge(s_spill, 16 * KB)
            for k in range(4):
                pool.dma_start(hT[:, k, :], spill[k]).then_inc(s_back[0], 16)
            pool.wait_ge(S("smp_state"), 2)
            for b in range(NB):
                pool.dma_start(io["s_ret"][0, b].rearrange("(j h) d e -> (h d) j e", h=2), sst[:, b]).then_inc(S("smp_state_stored"), 16)
            pool.wait_ge(S("smp_kv_ready"), 1)
            pool.wait_ge(s_pwe, 1)
            for name, cache, j in (("s_win_k", "cache_win_k", 0), ("s_win_v", "cache_win_v", 1)):
                pool.dma_start(io[name][0, :, 0:WIN - DT].rearrange("b k h d -> b (k h d)"),
                               io[cache][0, :, DT:WIN].rearrange("b k h d -> b (k h d)")).then_inc(s_out, 16)
                for b in range(NB):
                    pool.dma_start(io[name][0, b, WIN - DT:WIN].rearrange("t h d -> t (h d)"),
                                   kvtok[b * DT:b * DT + DT, j * P:j * P + P]).then_inc(s_out, 16)
            pool.dma_start(io["p_win_k"].rearrange("l b k h d -> (l b k) (h d)"), pw[:, 0:P]).then_inc(s_out, 16)
            pool.dma_start(io["p_win_v"].rearrange("l b k h d -> (l b k) (h d)"), pw[:, P:2 * P]).then_inc(s_out, 16)
            pool.wait_ge(s_lo, 2 * KB)
            for k in range(4, KB):
                pool.dma_start(hT[:, k, :], spill[k]).then_inc(s_back[1], 16)

            def residual_squares(u0, before):
                def body(u):
                    for q in range(2):
                        if not (isinstance(u, int) and u == u0 and q == 0):
                            pool.wait_ge(s_ss, before + (u - u0) + q)
                        squares(u - u0 + q, (s_ev, chunks_before(u + q + 1)))
                before_n = st.n
                body(u0)
                first_n = st.n - before_n
                n1 = st.n
                pool_body = lambda i: body(i * 2 + u0)
                st.loop(1, 4, pool_body)

            pool.wait_ge(s_out, 16 * N_OUT)
            residual_squares(U_OUT, KB)

            def x_stage(n2):
                for p in range(2):
                    n = n2 * 2 + p
                    wait(pool, s_xs, n - 1)
                    pool.tensor_copy(stx[:, p], cols(xq, 0, KB, n)).then_inc(s_xst, 1)

            pool.wait_ge(s_mm, chunks_before(U_XQ))
            pool.wait_ge(s_mout, 48)
            pool.dma_start(mkT[:].rearrange("p k t -> p (k t)"), mkT_d).then_inc(s_xld, 16)
            pool.dma_start(mv[:], io["p_mem_v"].rearrange("l b (t p) h d -> p (l b t) (h d)", p=P)).then_inc(s_xld, 16)
            pool.wait_ge(s_ev, chunks_before(U_XO))
            st.loop(0, NQ // 2, x_stage)

            pool.wait_ge(s_xs, NQ)

            def sx(b, cache, room):
                for kb in range(2):
                    room(b, kb)
                    pool.dma_start(kx[:, kb, :], io[cache][0, ds(b, 1), kb * P:(kb + 1) * P].rearrange("b k h d -> (b k) (h d)")).then_inc(s_kl[kb], 16)

            st.loop(0, NB, lambda b: sx(b, "cache_mem_k", lambda b, kb: wait(pool, s_kT, b * 2 + kb - 1)))
            pool.wait_ge(s_kT, 2 * NB)
            st.loop(0, NB, lambda b: sx(b, "cache_mem_v", lambda b, kb: wait(pool, s_vx, b)))
            residual_squares(U_XO, 2 * KB)
            residual_squares(U_END - 8, 3 * KB)

        @block.scalar
        def _(act):
            def copy(out, in_):
                return act.activation(out, in_, ACT.Copy)

            def prep_hi(m, dst, g, done):
                act.wait_ge(*done)
                act.activation(row(dst, m), row(hT, m), ACT.Copy, scale=gains[:, g, ds(m, 1)]).then_inc(s_hi, 1)

            def root(n, free):
                wait(act, s_ev, free)
                for c in range(NCH):
                    act.wait_ge(s_nmm, 3 * (n - 1) + c + 1)
                    act.activation(rstd[:, c * CW:(c + 1) * CW], ps[:, 2 + c, 0:CW], ACT.Sqrt, scale=1.0 / D, bias=small[:, 4:5]).then_inc(s_root, 1)

            def ahead(u, q, memory=False):
                split_hi(act, u + q + 1, 1 - q, memory)

            act.wait_ge(s_mem, 16)
            for t in range(2):
                act.activation(mkv[:, t, 0:D], memx[:, t, :], ACT.Square, accum_out=msq[:, t:t + 1]).then_inc(s_msq, 1)
            split_hi(act, 0, 0)
            act.wait_ge(s_mnT, 1)
            for k in range(KB):
                act.activation(mnhi[:, k, :], ps[:, 2 + k // 2, (k % 2) * NM:(k % 2) * NM + NM], ACT.Copy, scale=gains[:, G_MEM, k:k + 1]).then_inc(s_mhi, 1)

            def mem_body(i):
                for r in range(2):
                    for q in range(2):
                        ahead(i * 4 + 2 * r, q, memory=True)
                    t = i * 2 + r
                    act.wait_ge(s_xT, t + 1)
                    copy(hT[:, 0:4, ds(t * P, P)], ps[:, 2 + 2 * r, :].rearrange("p (k t) -> p k t", k=4)).then_inc(s_xea, 1)

            Steps(act, s_act).loop(0, 4, mem_body)
            act.wait_ge(s_xT, XT)
            copy(hT[:, 0:4, TP:T], ps[:, 2, :].rearrange("p (k t) -> p k t", k=4)[:, :, 0:TS]).then_inc(s_xea, 1)
            for k in range(KB):
                prep_hi(k, xhi, G_MIX, (s_xea, XT) if k < 4 else (s_xed, XT))
            for s in range(0, 8, 2):
                act.wait_ge(s_mt, s + 1)
                copy(mkv[:, s // 4, (s % 4) * 512:(s % 4) * 512 + 512], ps[:, 2 + s % 4, :]).then_inc(s_mta, 1)
            root(1, 0)

            def plain_in(u):
                for q in range(2):
                    ahead(u, q)

            pairs(act, U_IN, 14, plain_in)

            def gate_in(u):
                for q in range(2):
                    ahead(u, q)
                    act.wait_ge(s_ev, chunks_before(u + q + 1))
                    act.activation(row(zb, u - (U_IN + 14) + q), row(zb, u - (U_IN + 14) + q), ACT.Silu).then_inc(s_silu, 1)

            pairs(act, U_IN + 14, 4, gate_in)

            def win(n2):
                for p in range(2):
                    n = n2 * 2 + p
                    act.wait_ge(s_vT, n + 1)
                    copy(vtok[:].rearrange("p a d -> p (a d)"), ps[:, 7, 0:2 * P]).then_inc(s_vt, 1)
                    for kv in range(2):
                        j = n * 2 + kv
                        act.wait_ge(s_wm, j + 1)
                        for g in range(G):
                            c = kv * G + g
                            act.activation(sc[:, kv, g, :], sc[:, kv, g, :], ACT.Exp, scale=0.125, bias=wneg[:, c:c + 1],
                                           accum_out=wsum[:, c:c + 1]).then_inc(s_we, 1)
                        act.activation(wsink[:, kv * G:kv * G + G], wdif[:, kv * G:kv * G + G], ACT.Exp, scale=0.125).then_inc(s_we, 1)
                        act.wait_ge(s_wpT, j + 1)
                        copy(pT[:].rearrange("p a t -> p (a t)"), bank(4, 2)).then_inc(s_wpe, 1)
                    act.wait_ge(s_wo, 2 * n + 2)
                    copy(cols(za, 0, G, n), ps[:, 6, :].rearrange("p (g t) -> p g t", g=G)).then_inc(s_woe, 1)

            Steps(act, s_act).loop(0, NQ // 2, win)
            act.wait_ge(s_pwT, 1)
            copy(pw[:], ps[:, 2, 0:2 * P]).then_inc(s_pwe, 1)

            def ret(n):
                act.wait_ge(s_rT, 2 * n + 2)
                copy(vrt[:], ps[:, 3, :]).then_inc(s_vrt, 1)
                act.wait_ge(s_roT, n + 1)
                wait(act, s_rg, n)
                for h in range(RH):
                    act.activation(rf[:, h, :], ps[:, 7, h * P:(h + 1) * P], ACT.Identity, scale=gn[:, 0, h:h + 1], bias=gn[:, 1, h:h + 1]).then_inc(s_rf, 1)

            Steps(act, s_act).loop(0, NQ, ret)

            act.wait_ge(S("smp_k_turned"), 1)
            copy(kcT[:].rearrange("p b k -> p (b k)"), bank(2, 2)).then_inc(S("smp_kT_ready"), 1)
            act.wait_ge(S("smp_max"), 1)
            for kv in range(NKV):
                act.activation(ssc[:, kv, :], ssc[:, kv, :], ACT.Exp, scale=0.125, bias=wneg[:, kv:kv + 1], accum_out=wsum[:, kv:kv + 1]).then_inc(S("smp_exp"), 1)
            act.activation(wsink[:, 0:NKV], wdif[:, 0:NKV], ACT.Exp, scale=0.125).then_inc(S("smp_exp"), 1)
            act.wait_ge(S("smp_p_turned"), 1)
            copy(psT[:], ps[:, 5, 0:2 * P]).then_inc(S("smp_pT_ready"), 1)
            act.wait_ge(S("smp_out"), 1)
            copy(za[:, 0:G, TP:T].rearrange("p g (b t) -> p b g t", t=DT), ps[:, 4, 0:P].rearrange("p (b g t) -> p b g t", g=G, t=DT)).then_inc(S("smp_out_kept"), 1)
            act.wait_ge(S("smp_r_turned"), 1)
            copy(vrs[:], ps[0:TS, 3, :]).then_inc(S("smp_v_ready"), 1)
            act.wait_ge(S("smp_ret_out"), 1)
            copy(oTs[:].rearrange("p (j e) t -> p e j t", e=2), ps[:, 5:7, 0:2 * TS].rearrange("p e (j t) -> p e j t", j=2)).then_inc(S("smp_oT_ready"), 1)
            act.wait_ge(S("smp_on_turned"), 1)
            for h in range(RH):
                act.activation(rfs[:, h, :], ps[:, 7, h * TS:(h + 1) * TS], ACT.Identity, scale=gn[:, 0, h:h + 1], bias=gn[:, 1, h:h + 1]).then_inc(S("smp_affine"), 1)

            act.wait_ge(S("smp_out_kept"), 1)
            act.wait_ge(S("smp_gated"), 1)
            act.wait_ge(s_woe, NQ)
            act.wait_ge(s_rg, NQ)
            act.wait_ge(S("smp_state"), 2)
            for k in range(KB):
                if k == 6:
                    act.wait_ge(S("smp_state_stored"), 16 * NB)
                copy(xhi[:, k, :], za[:, k, :] if k < 4 else zb[:, k, :]).then_inc(s_hi, 1)

            def residual(u0, dst, g):
                def body(u):
                    for q in range(2):
                        ahead(u, q)
                        prep_hi(u - u0 + q, dst, g, (s_ev, chunks_before(u + q + 1)))
                pairs(act, u0, 8, body)

            residual(U_OUT, yhi, G_X)
            root(2, chunks_before(U_OUT))
            pairs(act, U_XQ, 8, plain_in)

            def cross(n2):
                for p in range(2):
                    n = n2 * 2 + p
                    act.wait_ge(s_xm, n + 1)
                    wait(act, s_xpT, n)
                    for h in range(XH):
                        act.activation(xp[:, h, :], ps[:, 2 + h // 2, (h % 2) * NM:(h % 2) * NM + NM], ACT.Exp, scale=1.0 / 16, bias=wneg[:, h:h + 1],
                                       accum_out=wsum[:, h:h + 1]).then_inc(s_xe, 1)
                    act.wait_ge(s_xpT, n + 1)
                    wait(act, s_xo, n)
                    copy(xpT[:].rearrange("p a t -> p (a t)"), bank(4, 2)).then_inc(s_xpe, 1)
                    act.wait_ge(s_xo, n + 1)
                    copy(cols(yhi, 0, KB, n), bank(6, 2).rearrange("p (k t) -> p k t", k=KB)).then_inc(s_xoh, 1)

            Steps(act, s_act).loop(0, NQ // 2, cross)

            def kx_evac(b):
                for kb in range(2):
                    t = b * 2 + kb
                    act.wait_ge(s_kT, t + 1)
                    wait(act, s_ksc, t - 1)
                    copy(kxT[:, kb, 0:4, :].rearrange("p k t -> p (k t)"), ps[:, 2 + 2 * kb, :]).then_inc(s_kea, 1)

            Steps(act, s_act).loop(0, NB, kx_evac)
            act.wait_ge(S("sx_max"), 1)
            act.activation(sxp[:], ps[:, 7, 0:NM], ACT.Exp, scale=1.0 / 16, bias=wneg[:, 0:1], accum_out=wsum[:, 0:1]).then_inc(S("sx_exp"), 1)
            act.wait_ge(S("sx_p_turned"), 1)
            copy(pxT[:].rearrange("p a r -> p (a r)"), ps[:, 6, 0:2 * P]).then_inc(S("sx_pT_ready"), 1)
            act.wait_ge(s_vx, NB)
            copy(yhi[:, :, TP:T], ps[:, 2, 0:KB * TS].rearrange("p (k t) -> p k t", k=KB)).then_inc(s_xoh, 1)
            residual(U_XO, xhi, G_MLP)
            root(3, chunks_before(U_XO))

            for f in range(FC):
                u0 = U_MLP + 16 * f

                def up(u):
                    for q in range(2):
                        ahead(u, q)
                        for c in range(NCH):
                            b = (q + c) % 2
                            hc = (u - u0 + q + 8 * f) * 3 + c
                            act.wait_ge(s_relu, hc + 1)
                            wait(act, s_hlo, hc - 1)
                            act.activation(hsq[:, b, :], relu[:, b, :], ACT.Square).then_inc(s_sqr, 1)
                            act.wait_ge(s_sqr, hc + 1)
                            copy(chunk(yhi, u - u0 + q, c), hsq[:, b, :]).then_inc(s_hhi, 1)

                pairs(act, u0, 8, up)
                if f < FC - 1:
                    pairs(act, u0 + 8, 8, plain_in)
                else:
                    pairs(act, u0 + 8, 6, plain_in)
                    ahead(u0 + 14, 0)
            root(4, chunks_before(U_END - 8))
            for t in range(XT):
                act.wait_ge(s_yt, t + 1)
                if t >= 4:
                    act.wait_ge(s_yout[t % 4], 16 * (t // 4))
                w = P if t < NQ else TS
                copy(ytok[0:w, t % 4, 0:512], ps[0:w, 2 + 2 * (t % 2), :]).then_inc(s_yea, 1)

        @block.tensor
        def _(pe):
            def norm_sum(n):
                pe.wait_ge(s_ss, KB * n)
                for c in range(NCH):
                    pe.matmul(ps[:, 2 + c, 0:CW], ones, ss[:, c * CW:(c + 1) * CW], start=True, stop=True).then_inc(s_nmm, 1)

            def units(u0, n_units, hi, lo):
                def body(u):
                    for q in range(2):
                        unit(pe, u + q, q, hi, lo)
                pairs(pe, u0, n_units, body)

            def turn(out, in_):
                n = in_.shape[0]
                return pe.transpose(out, in_, ident[0:n, 0:n])

            pe.wait_ge(s_tab, 16 * N_TABS)
            pe.wait_ge(s_mn, 2)
            for k in range(KB):
                for t in range(2):
                    mm = turn(ps[:, 2 + k // 2, (k % 2) * NM + t * P:(k % 2) * NM + (t + 1) * P], memx[:, t, k * P:(k + 1) * P])
            mm.then_inc(s_mnT, 1)
            pe.wait_ge(s_mlo, KB)

            def turn_x(t, r, w):
                wait(pe, s_xea, t - 1)
                wait(pe, s_xed, t - 1)
                pe.wait_ge(s_x[r], (t - r) * 8 + 16)
                for k in range(KB):
                    mm = turn(ps[:, 2 + 2 * r + k // 4, (k % 4) * P:(k % 4) * P + w], xin[0:w, r, k * P:(k + 1) * P])
                mm.then_inc(s_xT, 1)

            def mem_body(i):
                for r in range(2):
                    for q in range(2):
                        u = i * 4 + 2 * r + q
                        pe.wait_ge(s_wlo, u + 1)
                        product(pe, u, q, 0, mnhi, mnlo, NM, memory=True)
                    turn_x(i * 2 + r, r, P)

            Steps(pe, s_act).loop(0, 4, mem_body)
            turn_x(NQ, 0, TS)
            pe.wait_ge(s_ev, 16)
            pe.wait_ge(s_xea, XT)
            pe.wait_ge(s_xed, XT)
            for s in range(8):
                if s >= 4:
                    pe.wait_ge(s_mta if s % 2 == 0 else s_mtd, (s - 4) // 2 + 1)
                for j in range(4):
                    mm = turn(ps[:, 2 + s % 4, j * P:(j + 1) * P], mkvT[:, (s % 4) * 4 + j, (s // 4) * P:(s // 4 + 1) * P])
                mm.then_inc(s_mt, 1)
            pe.wait_ge(s_mta, 4)
            pe.wait_ge(s_mtd, 4)
            pe.wait_ge(s_lo, KB)
            norm_sum(1)
            units(U_IN, 18, xhi, xlo)
            pe.wait_ge(s_root, 3)

            def win(n2):
                for p in range(2):
                    n = n2 * 2 + p
                    pe.wait_ge(s_wst, 5 * n + 5)
                    wait(pe, s_vt, n)
                    for a in range(2):
                        mm = turn(ps[:, 7, a * P:(a + 1) * P], stv[:, p, a * P:(a + 1) * P])
                    mm.then_inc(s_vT, 1)
                    for kv in range(NKV):
                        j = n * 2 + kv
                        r = slice(kv * HD, (kv + 1) * HD)
                        wait(pe, s_wsb, 4 * j)
                        for g in range(G):
                            mm = pe.matmul(ps[:, 2 + g // 2, (g % 2) * 256:(g % 2) * 256 + 256], stq[r, p, g, :], stk[r, p, :], start=True, stop=True)
                        mm.then_inc(s_ws, 1)
                        pe.wait_ge(s_wp, 4 * j + 4)
                        wait(pe, s_wpe, j)
                        for a in range(2):
                            for g in range(G):
                                mm = turn(ps[:, 4 + a, g * P:(g + 1) * P], sc[:, kv, g, a * P:(a + 1) * P])
                        mm.then_inc(s_wpT, 1)
                        pe.wait_ge(s_wpe, j + 1)
                        pe.wait_ge(s_vt, n + 1)
                        wait(pe, s_woe, n)
                        for a in range(2):
                            mm = pe.matmul(ps[r, 6, :], vtok[:, a, r], pT[:, a, :], start=a == 0, stop=a == 1)
                        mm.then_inc(s_wo, 1)

            Steps(pe, s_act).loop(0, NQ // 2, win)
            for a in range(2):
                mm = turn(ps[:, 2, a * P:(a + 1) * P], za[:, 4 + a, TP - WIN:TP])
            mm.then_inc(s_pwT, 1)
            pe.wait_ge(s_pwe, 1)
            pe.wait_ge(s_woe, NQ)

            def ret(n2):
                for p in range(2):
                    n = n2 * 2 + p
                    pe.wait_ge(s_rst, 4 * n + 4)
                    wait(pe, s_rin, 2 * n)
                    for a in range(2):
                        mm = turn(ps[:, 2, a * P:(a + 1) * P], rk[:, p, a, :])
                    mm.then_inc(s_rT, 1)
                    wait(pe, s_vrt, n)
                    for h in range(RH):
                        mm = turn(ps[:, 3, h * P:(h + 1) * P], rv[:, p, h, :])
                    mm.then_inc(s_rT, 1)
                    wait(pe, s_rin, 2 * n)
                    pe.wait_ge(s_krz, n + 1)
                    for h in range(RH):
                        r = slice((h % 2) * RQ, (h % 2 + 1) * RQ)
                        mm = pe.matmul(ps[:, 4 if h % 2 == 0 else 2, (h // 2) * P:(h // 2 + 1) * P], rk[r, p, h // 2, :], rq[r, p, h // 2, :], start=True, stop=True)
                    mm.then_inc(s_ri, 1)
                    pe.wait_ge(s_rin, 2 * n + 2)
                    pe.wait_ge(s_vrt, n + 1)
                    wait(pe, s_rstate, RH * n)
                    pe.wait_ge(S("ret_state_zeroed"), 1)
                    wait(pe, s_ron, 4 * n)
                    for j in range(2):
                        pe.matmul(ps[:, 5, j * 2 * RV:(j + 1) * 2 * RV], rqx[:, p, j, :], state[:, j].rearrange("p e v -> p (e v)"), start=True, stop=False, skip_group_check=True)
                        for h in (2 * j, 2 * j + 1):
                            mm = pe.matmul(ps[:, 5, h * RV:(h + 1) * RV], inner[:, h, :], vrt[:, h * RV:(h + 1) * RV], start=False, stop=True, skip_group_check=True)
                    mm.then_inc(s_ro, 1)
                    pe.wait_ge(s_krz, n + 1)
                    for h in range(RH):
                        r = slice((h % 2) * RQ, (h % 2 + 1) * RQ)
                        mm = pe.matmul(ps[r, 6, (h // 2) * RV:(h // 2 + 1) * RV], krz[:, h * RQ:(h + 1) * RQ], vrt[:, h * RV:(h + 1) * RV], start=True, stop=True)
                    mm.then_inc(s_rs, 1)
                    pe.wait_ge(s_ron, 4 * n + 4)
                    wait(pe, s_rf, 4 * n)
                    for h in range(RH):
                        mm = turn(ps[:, 7, h * P:(h + 1) * P], onrm[:, h, :])
                    mm.then_inc(s_roT, 1)

            Steps(pe, s_act).loop(0, NQ // 2, ret)

            pe.wait_ge(s_rf, 4 * NQ)
            pe.wait_ge(s_rstate, RH * NQ)
            pe.wait_ge(s_sld, 16 * N_SLD)
            for b in range(NB):
                mm = turn(ps[:, 2 + b // 4, (b % 4) * P:(b % 4 + 1) * P], kc[:, b, :])
            mm.then_inc(S("smp_k_turned"), 1)
            for a in range(2):
                mm = turn(ps[0:TS, 4, a * P:(a + 1) * P], za[:, 4 + a, TP:T])
            mm.then_inc(S("smp_kv_turned"), 1)
            pe.wait_ge(S("smp_kT_ready"), 1)
            for kv in range(NKV):
                r = slice(kv * HD, (kv + 1) * HD)
                for b in range(NB):
                    mm = pe.matmul(ps[:, 5 + kv, b * 16:b * 16 + 16].rearrange("p (g t) -> p g t", t=DT), kcT[r, b, :],
                                   za[r, 0:G, TP + b * DT:TP + b * DT + DT], start=True, stop=True)
            mm.then_inc(S("smp_scores"), 1)
            for kv in range(NKV):
                r = slice(kv * HD, (kv + 1) * HD)
                mm = pe.matmul(ps[0:TS, 5 + kv, P:2 * P].rearrange("p (b g t) -> p b g t", g=G, t=DT), za[r, 4, TP:T],
                               za[r, 0:G, TP:T].rearrange("p g (b t) -> p b g t", t=DT), start=True, stop=True)
            mm.then_inc(S("smp_scores"), 1)
            pe.wait_ge(S("smp_s_ready"), 2)
            for kv in range(NKV):
                turn(ps[:, 7, kv * 160:kv * 160 + WIN], sT[:, kv * P:(kv + 1) * P])
                mm = turn(ps[:, 7, kv * 160 + WIN:kv * 160 + 160], snT[:, kv * P:(kv + 1) * P])
            mm.then_inc(S("smp_s_turned"), 1)
            pe.wait_ge(S("smp_probs"), 2)
            for kv in range(NKV):
                turn(ps[:, 5, kv * P:(kv + 1) * P], ssc[:, kv, 0:WIN])
                mm = turn(ps[0:TS, 6, kv * P:(kv + 1) * P], ssc[:, kv, WIN:160])
            mm.then_inc(S("smp_p_turned"), 1)
            pe.wait_ge(S("smp_pT_ready"), 1)
            pe.wait_ge(S("smp_pn_ready"), 1)
            pe.wait_ge(S("smp_kv_ready"), 1)
            for kv in range(NKV):
                r = slice(kv * HD, (kv + 1) * HD)
                pe.matmul(ps[r, 4, 0:P], kvtok[:, P + kv * HD:P + (kv + 1) * HD], pnT[:, kv * P:(kv + 1) * P], start=True, stop=False, skip_group_check=True)
                for b in range(NB):
                    mm = pe.matmul(ps[r, 4, b * 16:(b + 1) * 16], vc[:, b, r], psT[:, kv * P + b * 16:kv * P + (b + 1) * 16],
                                   start=False, stop=b == NB - 1, skip_group_check=True)
            mm.then_inc(S("smp_out"), 1)
            for a in range(2):
                turn(ps[0:TS, 2, a * P:(a + 1) * P], za[:, 8 + a, TP:T])
            for h in range(RH):
                mm = turn(ps[0:TS, 3, h * P:(h + 1) * P], zb[:, 4 + h, TP:T])
            mm.then_inc(S("smp_r_turned"), 1)
            for h in range(RH):
                r = slice((h % 2) * RQ, (h % 2 + 1) * RQ)
                mm = pe.matmul(ps[0:TS, 7 - h % 2, (h // 2) * TS:(h // 2 + 1) * TS], za[r, 8 + h // 2, TP:T], za[r, 6 + h // 2, TP:T], start=True, stop=True)
            mm.then_inc(S("smp_inner"), 1)
            pe.wait_ge(S("smp_decayed"), 2)
            pe.wait_ge(S("smp_v_ready"), 1)
            pe.wait_ge(S("smp_qx"), 1)
            pe.wait_ge(s_sst, 16 * NB)
            for h in range(RH):
                r = slice((h % 2) * RQ, (h % 2 + 1) * RQ)
                o = ps[:, 5 + h % 2, (h // 2) * TS:(h // 2 + 1) * TS]
                pe.matmul(o, vrs[:, h * RV:(h + 1) * RV], ins_[:, h, :], start=True, stop=False, skip_group_check=True)
                for b in range(NB):
                    mm = pe.matmul(o[:, b * DT:b * DT + DT], sst[r, b, h // 2, :], qxs[r, h // 2, b * DT:(b + 1) * DT],
                                   start=False, stop=b == NB - 1, skip_group_check=True)
            mm.then_inc(S("smp_ret_out"), 1)
            pe.wait_ge(S("smp_oT_ready"), 1)
            pe.wait_ge(S("smp_out_kept"), 1)
            for h in range(RH):
                mm = turn(ps[0:TS, 4, h * RV:(h + 1) * RV], oTs[:, h, :])
            mm.then_inc(S("smp_o_turned"), 1)
            pe.wait_ge(S("smp_normed"), RH)
            for h in range(RH):
                mm = turn(ps[:, 7, h * TS:(h + 1) * TS], ons[:, h, :])
            mm.then_inc(S("smp_on_turned"), 1)
            pe.wait_ge(S("smp_kz_masked"), NB)
            pe.wait_ge(S("smp_out_kept"), 1)
            for b in range(NB):
                for h in range(RH):
                    r, s = slice((h % 2) * RQ, (h % 2 + 1) * RQ), b * 2 + h // 2
                    mm = pe.matmul(ps[r, 2 + s // 4, (s % 4) * RV:(s % 4 + 1) * RV], kzm[:, b, h * RQ:(h + 1) * RQ], vrs[:, h * RV:(h + 1) * RV], start=True, stop=True)
            mm.then_inc(S("smp_state_sum"), 1)

            pe.wait_ge(s_lo, 2 * KB)
            units(U_OUT, 8, xhi, xlo)
            pe.wait_ge(s_lo, 3 * KB)
            norm_sum(2)
            units(U_XQ, 8, yhi, ylo)
            pe.wait_ge(s_root, 6)

            pe.wait_ge(s_xld, 32)

            def cross(n2):
                for p in range(2):
                    n = n2 * 2 + p
                    pe.wait_ge(s_xst, n + 1)
                    wait(pe, s_xe, 4 * n)
                    for h in range(XH):
                        for dd in range(2):
                            mm = pe.matmul(ps[:, 2 + h // 2, (h % 2) * NM:(h % 2) * NM + NM], stx[:, p, 2 * h + dd, :], mkT[:, 2 * h + dd, :], start=dd == 0, stop=dd == 1)
                    mm.then_inc(s_xs, 1)
                    pe.wait_ge(s_xp, 4 * n + 4)
                    wait(pe, s_xpe, n)
                    for a in range(2):
                        for h in range(XH):
                            mm = turn(ps[:, 4 + a, h * P:(h + 1) * P], xp[:, h, a * P:(a + 1) * P])
                    mm.then_inc(s_xpT, 1)
                    pe.wait_ge(s_xpe, n + 1)
                    wait(pe, s_xol, n)
                    for k in range(KB):
                        for a in range(2):
                            mm = pe.matmul(ps[:, 6 + k // 4, (k % 4) * P:(k % 4 + 1) * P], mv[:, a, k * P:(k + 1) * P], xpT[:, a, (k // 2) * P:(k // 2 + 1) * P], start=a == 0, stop=a == 1)
                    mm.then_inc(s_xo, 1)

            Steps(pe, s_act).loop(0, NQ // 2, cross)
            pe.wait_ge(s_xpe, NQ)
            pe.wait_ge(s_xe, 4 * NQ)
            pe.wait_ge(s_xol, NQ)

            def sxk(b):
                for kb in range(2):
                    t = b * 2 + kb
                    pe.wait_ge(s_kl[kb], b * 16 + 16)
                    wait(pe, s_kea, t - 1)
                    wait(pe, s_ked, t - 1)
                    for k in range(KB):
                        mm = turn(ps[:, 2 + 2 * kb + k // 4, (k % 4) * P:(k % 4 + 1) * P], kx[:, kb, k * P:(k + 1) * P])
                    mm.then_inc(s_kT, 1)
                for kb in range(2):
                    t = b * 2 + kb
                    pe.wait_ge(s_kea, t + 1)
                    pe.wait_ge(s_ked, t + 1)
                    for h in range(XH):
                        for dd in range(2):
                            mm = pe.matmul(ps[:, 6, ds(b * 16 + (kb * P + h * DT), DT)], kxT[:, kb, 2 * h + dd, :], xq[:, 2 * h + dd, ds(b * DT + TP, DT)], start=dd == 0, stop=dd == 1)
                    mm.then_inc(s_ksc, 1)

            Steps(pe, s_act).loop(0, NB, sxk)
            pe.wait_ge(S("sx_s_ready"), 1)
            for kb in range(2):
                mm = turn(ps[:, 7, kb * P:(kb + 1) * P], sxT[:, kb, :])
            mm.then_inc(S("sx_s_turned"), 1)
            pe.wait_ge(S("sx_probs"), 1)
            for kb in range(2):
                mm = turn(ps[:, 6, kb * P:(kb + 1) * P], sxp[:, kb * P:(kb + 1) * P])
            mm.then_inc(S("sx_p_turned"), 1)
            pe.wait_ge(S("sx_pT_ready"), 1)

            def sxv(b):
                for kb in range(2):
                    pe.wait_ge(s_kl[kb], b * 16 + 16 * (NB + 1))
                for k in range(KB):
                    for kb in range(2):
                        mm = pe.matmul(ps[:, 2, ds(b * DT + k * TS, DT)], kx[:, kb, k * P:(k + 1) * P], pxT[:, kb, ds(b * 16 + (k // 2) * DT, DT)], start=kb == 0, stop=kb == 1)
                mm.then_inc(s_vx, 1)

            Steps(pe, s_act).loop(0, NB, sxv)
            pe.wait_ge(s_xol, NQ + 1)
            units(U_XO, 8, yhi, ylo)
            pe.wait_ge(s_lo, 4 * KB)
            norm_sum(3)
            for f in range(FC):
                u0 = U_MLP + 16 * f
                units(u0, 8, xhi, xlo)
                pe.wait_ge(s_hlo, 24 * (f + 1))
                units(u0 + 8, 8, yhi, ylo)
            pe.wait_ge(s_root, 9)
            norm_sum(4)
            pe.wait_ge(s_yT, KB)
            for t in range(XT):
                w = P if t < NQ else TS
                if t >= 2:
                    pe.wait_ge(s_yea, t - 1)
                    pe.wait_ge(s_yed, t - 1)
                for k in range(KB):
                    mm = turn(ps[0:w, 2 + 2 * (t % 2) + k // 4, (k % 4) * P:(k % 4 + 1) * P], hT[:, k, t * P:t * P + w])
                mm.then_inc(s_yt, 1)

        @block.vector
        def _(dve):
            st = Steps(dve, s_dve)

            def prep_lo(m, n, hi, lo, g):
                dve.wait_ge(s_hi, n + 1)
                dve.scalar_tensor_tensor(row(lo, m), row(hT, m), gains[:, g, ds(m, 1)], row(hi, m).bitcast(F32), ALU.mult, ALU.subtract).then_inc(s_lo, 1)

            def invert(n):
                for c in range(NCH):
                    dve.wait_ge(s_root, 3 * (n - 1) + c + 1)
                    dve.reciprocal(rstd[:, c * CW:(c + 1) * CW], rstd[:, c * CW:(c + 1) * CW]).then_inc(s_rstd, 1)
                dve.wait_ge(s_rstd, 3 * n)

            def evac(u, q, dst_of, last=False):
                if not last:
                    split_lo(dve, u + 1, 1 - q)
                for c in range(NCH):
                    dve.wait_ge(s_mm, chunks_before(u) + c + 1)
                    dst_of(u, q, c).then_inc(s_ev, 1)

            def scaled(t, m0):
                def f(u, q, c):
                    return dve.tensor_tensor(chunk(t, u - m0, c), ps[:, (q + c) % 2, 0:CW], rstd[:, c * CW:(c + 1) * CW], ALU.mult)
                return f

            def added(m0):
                def f(u, q, c):
                    return dve.tensor_tensor(chunk(hT, u - m0, c), ps[:, (q + c) % 2, 0:CW], chunk(hT, u - m0, c), ALU.add)
                return f

            def run(u0, n_units, f, after=None, last=False):
                def body(u):
                    for q in range(2):
                        evac(u + q, q, f)
                        if after is not None:
                            after(u + q)
                if not last:
                    pairs(dve, u0, n_units, body)
                    return
                pairs(dve, u0, n_units - 2, body)
                for q in range(2):
                    evac(u0 + n_units - 2 + q, q, f, last=q == 1)

            dve.memset(mhalf, -0.5).then_inc(S("dve_constants"), 1)
            dve.memset(small[:, 4:5], EPS_N).then_inc(S("dve_constants"), 1)
            dve.wait_ge(s_msq, 2)
            dve.wait_ge(S("dve_constants"), 2)
            dve.tensor_scalar(mvar, msq, 1.0 / D, EPS_N, ALU.mult, ALU.add).then_inc(s_mvar, 1)
            dve.wait_ge(s_mpow, 1)
            for t in range(2):
                dve.tensor_scalar(memx[:, t, :], memx[:, t, :], mrs[:, t:t + 1], None, ALU.mult).then_inc(s_mn, 1)
            dve.wait_ge(s_tab, 16 * N_TABS)
            st.did(dve.tensor_scalar(sink8[:], sink8[:], 8.0, None, ALU.mult))
            split_lo(dve, 0, 0)
            for k in range(KB):
                dve.wait_ge(s_mhi, k // 2 * 2 + 2)
                dve.scalar_tensor_tensor(mnlo[:, k, :], ps[:, 2 + k // 2, (k % 2) * NM:(k % 2) * NM + NM], gains[:, G_MEM, k:k + 1], mnhi[:, k, :].bitcast(F32),
                                         ALU.mult, ALU.subtract).then_inc(s_mlo, 1)

            def mem_body(i):
                for r in range(2):
                    for q in range(2):
                        u = i * 4 + 2 * r + q
                        split_lo(dve, u + 1, 1 - q)
                        dve.wait_ge(s_mm, u + 1)
                        dve.tensor_copy(mkvT[:, ds(u, 1), :].rearrange("p a t -> p (a t)"), ps[:, q, 0:NM]).then_inc(s_ev, 1)
                    t = i * 2 + r
                    dve.wait_ge(s_xT, t + 1)
                    dve.tensor_copy(hT[:, 4:8, ds(t * P, P)], ps[:, 3 + 2 * r, :].rearrange("p (k t) -> p k t", k=4)).then_inc(s_xed, 1)

            st.loop(0, 4, mem_body)
            dve.wait_ge(s_xT, XT)
            dve.tensor_copy(hT[:, 4:8, TP:T], ps[:, 3, :].rearrange("p (k t) -> p k t", k=4)[:, :, 0:TS]).then_inc(s_xed, 1)
            for k in range(KB):
                prep_lo(k, k, xhi, xlo, G_MIX)
            for s in range(1, 8, 2):
                dve.wait_ge(s_mt, s + 1)
                dve.tensor_copy(mkv[:, s // 4, (s % 4) * 512:(s % 4) * 512 + 512], ps[:, 2 + s % 4, :]).then_inc(s_mtd, 1)
            invert(1)
            dve.wait_ge(s_mout, 48)
            run(U_IN, 10, scaled(za, U_IN))
            dve.wait_ge(s_spill, 16 * KB)
            dve.wait_ge(s_ss, KB)
            run(U_IN + 10, 4, scaled(zb, U_IN + 10 - 4))
            run(U_IN + 14, 4, scaled(zb, U_IN + 14))

            def softmax_tail(c0, n, probs, exp_sem, exp_n, out_sem, sink=True):
                dve.wait_ge(exp_sem, exp_n)
                if sink:
                    st.did(dve.tensor_tensor(wsum[:, c0:c0 + n], wsum[:, c0:c0 + n], wsink[:, c0:c0 + n], ALU.add))
                    st.settle()
                st.did(dve.reciprocal(wrec[:, c0:c0 + n], wsum[:, c0:c0 + n]))
                st.settle()
                for g in range(n):
                    dve.tensor_scalar(probs(g), probs(g), wrec[:, c0 + g:c0 + g + 1], None, ALU.mult).then_inc(out_sem, 1)

            dist = table("dist").rearrange("p (v c) -> p v c", v=2)

            def win(n2):
                for p in range(2):
                    n = n2 * 2 + p
                    for kv in range(NKV):
                        j = n * 2 + kv
                        c0 = kv * G
                        dve.wait_ge(s_ws, j + 1)
                        wait(dve, s_wpT, j - 1)
                        which = 0 if isinstance(n, int) and n == 0 else 1
                        for g in range(G):
                            dve.scalar_tensor_tensor(sc[:, kv, g, :], dist[:, which, :], 8.0 * SLOPES[c0 + g], ps[:, 2 + g // 2, (g % 2) * 256:(g % 2) * 256 + 256],
                                                     ALU.mult, ALU.add).then_inc(s_wsb, 1)
                        dve.wait_ge(s_wsb, 4 * j + 4)
                        st.did(dve.tensor_reduce(wmax, sc[:, kv], AX.X, ALU.max))
                        st.settle()
                        st.did(dve.tensor_tensor(wmax, wmax, sink8[:, c0:c0 + G], ALU.max))
                        st.settle()
                        st.did(dve.tensor_scalar(wneg[:, c0:c0 + G], wmax, -0.125, None, ALU.mult))
                        st.settle()
                        dve.tensor_tensor(wdif[:, c0:c0 + G], sink8[:, c0:c0 + G], wmax, ALU.subtract).then_inc(s_wm, 1)
                        softmax_tail(c0, G, lambda g: sc[:, kv, g, :], s_we, 5 * j + 5, s_wp)

            st.loop(0, NQ // 2, win)

            dve.wait_ge(s_woe, NQ)
            dve.wait_ge(s_wpe, 2 * NQ)
            dve.memset(state[:], 0.0).then_inc(S("ret_state_zeroed"), 1)
            dve.wait_ge(S("ret_state_zeroed"), 1)
            gl = table("gl")
            decay = table("decay").rearrange("p (h t) -> p h t", h=RH)

            def by_half(t):
                return t.rearrange("p (j e) t -> p e j t", e=2)

            def stats(w, o_of, var_sem, meanwhile=None):
                for h in range(RH):
                    st.did(dve.bn_stats(gst[0:w, h * 6:(h + 1) * 6], o_of(h)))
                st.settle()
                if meanwhile is not None:
                    meanwhile()
                for h in range(RH):
                    st.did(dve.bn_aggr(gmv[0:w, h * 2:(h + 1) * 2], gst[0:w, h * 6:(h + 1) * 6]))
                st.settle()
                dve.tensor_scalar(gvar[0:w], gmv[0:w].rearrange("p (h m) -> p h m", m=2)[:, :, 1], EPS_G, None, ALU.add).then_inc(var_sem, 1)

            def ret(n):
                dve.wait_ge(s_rT, 2 * n + 1)
                wait(dve, s_rs, n)
                dve.tensor_tensor(krz[:], ps[:, 2, 0:2 * P], table("zeta"), ALU.mult).then_inc(s_krz, 1)
                dve.wait_ge(s_ri, n + 1)
                for e, b in ((0, 4), (1, 2)):
                    dve.tensor_tensor(by_half(inner[:])[:, e], ps[:, b, 0:2 * P].rearrange("p (j t) -> p j t", j=2), by_half(decay)[:, e], ALU.mult).then_inc(s_rin, 1)
                dve.wait_ge(s_ro, n + 1)

                def update():
                    dve.wait_ge(s_rs, n + 1)
                    for h in range(RH):
                        e, j = h % 2, h // 2
                        r = slice(e * RQ, (e + 1) * RQ)
                        dve.scalar_tensor_tensor(state[r, j, e, :], state[r, j, e, :], gl[r, j:j + 1], ps[r, 6, j * RV:(j + 1) * RV], ALU.mult, ALU.add).then_inc(s_rstate, 1)

                stats(P, lambda h: ps[:, 5, h * RV:(h + 1) * RV], s_rvar, update)
                dve.wait_ge(s_rrs, n + 1)
                wait(dve, s_roT, n)
                for h in range(RH):
                    dve.tensor_scalar(onrm[:, h, :], ps[:, 5, h * RV:(h + 1) * RV], gmv[:, 2 * h:2 * h + 1], grs[:, h:h + 1], ALU.subtract, ALU.mult).then_inc(s_ron, 1)

            st.loop(0, NQ, ret)

            def stable(n, w=P):
                a, k = _S[n]
                return stab[0:w, a:a + k]

            dve.wait_ge(S("smp_kv_turned"), 1)
            dve.tensor_copy(kvtok[:], ps[0:TS, 4, 0:2 * P]).then_inc(S("smp_kv_ready"), 1)
            dve.wait_ge(S("smp_scores"), 2)
            dve.tensor_copy(sT[:].rearrange("p (k r) -> p k r", k=NKV), ps[:, 5:7, 0:P]).then_inc(S("smp_s_ready"), 1)
            dve.tensor_copy(snT[:].rearrange("p (k r) -> p k r", k=NKV), ps[0:TS, 5:7, P:2 * P]).then_inc(S("smp_s_ready"), 1)
            for kv in range(NKV):
                st.did(dve.tensor_tensor(wdif[:, kv * G:kv * G + G], sink8[:, kv * G:kv * G + G], stable("sel"), ALU.mult))
            st.settle()
            st.did(dve.tensor_reduce(wrec[:, 4:6], wdif.rearrange("p (k g) -> p k g", g=G), AX.X, ALU.add))
            dve.wait_ge(S("smp_s_turned"), 1)
            st.did(dve.tensor_tensor(ssc[:].rearrange("p k c -> p (k c)"), ps[:, 7, 0:320], stable("bias"), ALU.add))
            st.settle()
            st.did(dve.tensor_reduce(wmax[:, 0:2], ssc[:], AX.X, ALU.max))
            st.settle()
            st.did(dve.tensor_tensor(wmax[:, 0:2], wmax[:, 0:2], wrec[:, 4:6], ALU.max))
            st.settle()
            st.did(dve.tensor_scalar(wneg[:, 0:2], wmax[:, 0:2], -0.125, None, ALU.mult))
            st.settle()
            dve.tensor_tensor(wdif[:, 0:2], wrec[:, 4:6], wmax[:, 0:2], ALU.subtract).then_inc(S("smp_max"), 1)
            softmax_tail(0, 2, lambda kv: ssc[:, kv, :], S("smp_exp"), 3, S("smp_probs"))
            dve.wait_ge(S("smp_p_turned"), 1)
            dve.tensor_copy(pnT[:], ps[0:TS, 6, 0:2 * P]).then_inc(S("smp_pn_ready"), 1)
            dve.tensor_tensor(qxs[:], za[:, 6:8, TP:T], stable("xi").rearrange("p (j t) -> p j t", j=2), ALU.mult).then_inc(S("smp_qx"), 1)
            dve.wait_ge(S("smp_r_turned"), 1)
            dve.tensor_tensor(kzs[:], ps[0:TS, 2, 0:2 * P], stable("zeta", TS), ALU.mult).then_inc(S("smp_kz"), 1)
            dve.wait_ge(S("smp_inner"), 1)
            sdecay = stable("decay", TS).rearrange("p (h t) -> p h t", h=RH)
            for e in range(2):
                dve.tensor_tensor(by_half(ins_[:])[:, e], ps[0:TS, 7 - e, 0:2 * TS].rearrange("p (j t) -> p j t", j=2), by_half(sdecay)[:, e], ALU.mult).then_inc(S("smp_decayed"), 1)
            dve.wait_ge(S("smp_kz"), 1)
            for b in range(NB):
                dve.tensor_scalar(kzm[:, b, :], kzs[:], stable("own", TS)[:, b:b + 1], None, ALU.mult).then_inc(S("smp_kz_masked"), 1)
            dve.wait_ge(S("smp_o_turned"), 1)
            stats(TS, lambda h: ps[0:TS, 4, h * RV:(h + 1) * RV], S("smp_var"))
            dve.wait_ge(S("smp_rstd"), 1)
            for h in range(RH):
                dve.tensor_scalar(ons[:, h, :], ps[0:TS, 4, h * RV:(h + 1) * RV], gmv[0:TS, 2 * h:2 * h + 1], grs[0:TS, h:h + 1], ALU.subtract, ALU.mult).then_inc(S("smp_normed"), 1)
            dve.wait_ge(S("smp_state_sum"), 1)
            for j in range(2):
                dve.scalar_tensor_tensor(sst[:, :, j, :], sst[:, :, j, :], stable("gl")[:, j:j + 1], bank(2, 4).rearrange("p (b j e) -> p b j e", b=NB, j=2)[:, :, j, :],
                                         ALU.mult, ALU.add).then_inc(S("smp_state"), 1)

            for k in range(KB):
                dve.wait_ge(s_hi, KB + k + 1)
                dve.tensor_tensor(xlo[:, k, :], za[:, k, :] if k < 4 else zb[:, k, :], xhi[:, k, :].bitcast(F32), ALU.subtract).then_inc(s_lo, 1)
            dve.wait_ge(s_back[0], 64)

            def residual(u0, n0, hi, lo, g):
                return lambda u: prep_lo(u - u0, u - u0 + n0, hi, lo, g)

            run(U_OUT, 4, added(U_OUT), residual(U_OUT, 2 * KB, yhi, ylo, G_X))
            dve.wait_ge(s_back[1], 64)
            run(U_OUT + 4, 4, added(U_OUT), residual(U_OUT, 2 * KB, yhi, ylo, G_X))
            invert(2)
            run(U_XQ, 8, scaled(xq, U_XQ))

            def cross(n2):
                for p in range(2):
                    n = n2 * 2 + p
                    dve.wait_ge(s_xs, n + 1)
                    st.did(dve.tensor_reduce(wmax, bank(2, 2).rearrange("p (h c) -> p h c", h=XH), AX.X, ALU.max))
                    st.settle()
                    dve.tensor_scalar(wneg[:, 0:XH], wmax, -1.0 / 16, None, ALU.mult).then_inc(s_xm, 1)
                    softmax_tail(0, XH, lambda h: xp[:, h, :], s_xe, 4 * n + 4, s_xp, sink=False)
                    dve.wait_ge(s_xoh, n + 1)
                    dve.tensor_tensor(cols(ylo, 0, KB, n), bank(6, 2).rearrange("p (k t) -> p k t", k=KB), cols(yhi, 0, KB, n).bitcast(F32), ALU.subtract).then_inc(s_xol, 1)

            st.loop(0, NQ // 2, cross)

            def kx_evac(b):
                for kb in range(2):
                    t = b * 2 + kb
                    dve.wait_ge(s_kT, t + 1)
                    wait(dve, s_ksc, t - 1)
                    dve.tensor_copy(kxT[:, kb, 4:8, :].rearrange("p k t -> p (k t)"), ps[:, 3 + 2 * kb, :]).then_inc(s_ked, 1)

            st.loop(0, NB, kx_evac)
            dve.wait_ge(s_ksc, 2 * NB)
            dve.tensor_copy(sxT[:].rearrange("p a r -> p (a r)"), ps[:, 6, 0:2 * P]).then_inc(S("sx_s_ready"), 1)
            dve.wait_ge(S("sx_s_turned"), 1)
            st.did(dve.tensor_reduce(wmax[:, 0:1], ps[:, 7, 0:NM], AX.X, ALU.max))
            st.settle()
            dve.tensor_scalar(wneg[:, 0:1], wmax[:, 0:1], -1.0 / 16, None, ALU.mult).then_inc(S("sx_max"), 1)
            softmax_tail(0, 1, lambda h: sxp[:], S("sx_exp"), 1, S("sx_probs"), sink=False)
            dve.wait_ge(s_xoh, NQ + 1)
            dve.tensor_tensor(ylo[:, :, TP:T], ps[:, 2, 0:KB * TS].rearrange("p (k t) -> p k t", k=KB), yhi[:, :, TP:T].bitcast(F32), ALU.subtract).then_inc(s_xol, 1)
            run(U_XO, 8, added(U_XO), residual(U_XO, 3 * KB, xhi, xlo, G_MLP))
            invert(3)

            for f in range(FC):
                u0 = U_MLP + 16 * f

                def up(u):
                    for q in range(2):
                        split_lo(dve, u + q + 1, 1 - q)

                        def lo_part(c):
                            hc = (u - u0 + q + 8 * f) * 3 + c
                            dve.wait_ge(s_hhi, hc + 1)
                            dve.tensor_tensor(chunk(ylo, u - u0 + q, c), hsq[:, (q + c) % 2, :], chunk(yhi, u - u0 + q, c).bitcast(F32), ALU.subtract).then_inc(s_hlo, 1)

                        for c in range(NCH):
                            hc = (u - u0 + q + 8 * f) * 3 + c
                            dve.wait_ge(s_mm, chunks_before(u + q) + c + 1)
                            wait(dve, s_sqr, hc - 1)
                            dve.scalar_tensor_tensor(relu[:, (q + c) % 2, :], ps[:, (q + c) % 2, 0:CW], 0.0, rstd[:, c * CW:(c + 1) * CW], ALU.max, ALU.mult).then_inc(s_relu, 1)
                            dve.wait_ge(s_relu, hc + 1)
                            dve.sem_inc(s_ev, 1)
                            if c:
                                lo_part(c - 1)
                        lo_part(NCH - 1)

                pairs(dve, u0, 8, up)
                run(u0 + 8, 8, added(u0 + 8), last=f == FC - 1)
            invert(4)
            for k in range(KB):
                dve.scalar_tensor_tensor(hT[:, k, :], hT[:, k, :], gains[:, G_FIN, k:k + 1], rstd[:], ALU.mult, ALU.mult).then_inc(s_yT, 1)
            for t in range(XT):
                dve.wait_ge(s_yt, t + 1)
                if t >= 4:
                    dve.wait_ge(s_yout[t % 4], 16 * (t // 4))
                w = P if t < NQ else TS
                dve.tensor_copy(ytok[0:w, t % 4, 512:D], ps[0:w, 3 + 2 * (t % 2), :]).then_inc(s_yed, 1)


_INS = ["x_prompt", "x_sample", "mem_prompt", "cache_win_k", "cache_win_v", "state_ret", "cache_mem_k", "cache_mem_v", "g_mix", "w_in",
        "attn_sinks", "ret_gn_g", "ret_gn_b", "w_out", "g_xattn", "g_mem", "w_xq", "w_xk", "w_xv", "w_xo", "g_mlp", "w_up", "w_down", "g_final"]
_OUTS = [("y_prompt", (1, TP, D)), ("y_sample", (NB, DT, D)), ("p_win_k", (1, 1, WIN, NKV, HD)), ("p_win_v", (1, 1, WIN, NKV, HD)),
         ("p_ret", (1, 1, RH, RQ, RV)), ("p_mem_k", (1, 1, NM, XH, D // XH)), ("p_mem_v", (1, 1, NM, XH, D // XH)),
         ("s_win_k", (1, NB, WIN, NKV, HD)), ("s_win_v", (1, NB, WIN, NKV, HD)), ("s_ret", (1, NB, RH, RQ, RV))]


def kernel(**inputs):
    import concourse.bacc as bacc
    from concourse.bass_utils import run_bass_kernel_spmd

    nc = bacc.Bacc("TRN2", target_bir_lowering=False, num_devices=1)
    arrays, io = {}, {}
    given = {name: np.ascontiguousarray(inputs[name]) for name in _INS}
    given["tables"], given["sample_tables"] = tables()
    for name, a in given.items():
        arrays[f"in_{name}"] = a
        io[name] = nc.dram_tensor(f"in_{name}", a.shape, mybir.dt.from_np(a.dtype), kind="ExternalInput").ap()
    for name, shape in _OUTS:
        io[name] = nc.dram_tensor(f"out_{name}", shape, F32, kind="ExternalOutput").ap()
    layer(nc, io)
    r = run_bass_kernel_spmd(nc, [arrays], core_ids=[0])
    return tuple(r.results[0][f"out_{name}"] for name, _ in _OUTS)
```

```python
from contextlib import ExitStack

import numpy as np
import concourse.bass as bass
from concourse import mybir
from concourse.alu_op_type import AluOpType as ALU

ACT = mybir.ActivationFunctionType
AX = mybir.AxisListType
F32 = mybir.dt.float32
F32R = mybir.dt.float32r
ds = bass.ds

P = 128
D = 1024
KB = D // P
TP = 1024
NB = 8
DT = 4
TS = NB * DT
T = TP + TS
NCH = 3
CW = T // NCH
NQ = TP // P
WIN = 128
NH, NKV, G, HD = 8, 2, 4, 64
RH, RQ, RV = 4, 64, 128
NM = 256
XH = 4
DFF = 4096
FC = 4
RMS_EPS, GN_EPS = 1e-6, 1e-5
MASKED = -1e37

U_MEM = 0
U_IN = U_MEM + 16
U_RET = U_IN + 6
U_GATE = U_IN + 14
U_OUT = U_IN + 18
U_XQ = U_OUT + 8
U_XO = U_XQ + 8
U_MLP = U_XO + 8
U_END = U_MLP + FC * 16
LOAD = 48

_T = {}
_at = 0
for _n, _w in (("ident", P), ("ones", P), ("dist", 2 * 256), ("decay", RH * P), ("xi", 2 * P), ("zeta", RH * RQ), ("gl", 2)):
    _T[_n] = (_at, _w)
    _at += _w
N_TAB = _at
_S = {}
_at = 0
for _n, _w in (("bias", NKV * 160), ("decay", RH * TS), ("xi", 2 * TS), ("zeta", RH * RQ), ("own", NB), ("sel", G), ("gl", 2)):
    _S[_n] = (_at, _w)
    _at += _w
N_STAB = _at

SLOPES = [2.0 ** (-8.0 * (i + 1) / NH) for i in range(NH)]


def tables():
    lg = np.log(1.0 - 2.0 ** (-5.0 - np.arange(RH))).astype(np.float32).astype(np.float64)
    t = np.zeros((P, N_TAB), np.float64)
    r = np.arange(P)

    def put(a, m, n, v):
        a[: v.shape[0], m[n][0]:m[n][0] + m[n][1]] = v.reshape(v.shape[0], -1)

    put(t, _T, "ident", np.eye(P))
    put(t, _T, "ones", np.ones((P, P)))
    dist = r[:, None] + WIN - np.arange(2 * WIN)[None]
    later = np.where((dist >= 0) & (dist < WIN), -dist, MASKED)
    first = np.where(np.arange(2 * WIN)[None] < WIN, MASKED, later)
    put(t, _T, "dist", np.stack([first, later], 1))
    d = r[None, :] - r[:, None]
    put(t, _T, "decay", np.stack([np.where(d >= 0, 0.125 * np.exp(lg[h] * np.maximum(d, 0)), 0.0) for h in range(RH)], 1))
    half = r // RQ
    put(t, _T, "xi", np.stack([np.exp((r[None, :] + 1.0) * lg[2 * j + half][:, None]) for j in range(2)], 1))
    put(t, _T, "zeta", np.repeat(0.125 * np.exp((P - 1.0 - r)[:, None] * lg[None]), RQ, 1))
    put(t, _T, "gl", np.stack([np.exp(P * lg[2 * j + half]) for j in range(2)], 1))

    s = np.zeros((P, N_STAB), np.float64)
    b, g, q = r // 16, (r // 4) % 4, r % 4
    bias = np.full((P, NKV, 160), MASKED)
    for kv in range(NKV):
        slope = 8.0 * np.array(SLOPES)[kv * G + g]
        c = np.arange(WIN)[None]
        dist = q[:, None] + WIN - c
        bias[:, kv, :WIN] = np.where((dist >= 0) & (dist < WIN), -slope[:, None] * dist, MASKED)
        c = np.arange(TS)[None]
        dist = q[:, None] - c % DT
        bias[:, kv, WIN:] = np.where((c // DT == b[:, None]) & (dist >= 0), -slope[:, None] * dist, MASKED)
    put(s, _S, "bias", bias)
    w = np.arange(TS)
    d = w[None, :] - w[:, None]
    same = (w[None, :] // DT == w[:, None] // DT) & (d >= 0)
    put(s, _S, "decay", np.stack([np.where(same, 0.125 * np.exp(lg[h] * np.maximum(d, 0)), 0.0) for h in range(RH)], 1))
    put(s, _S, "xi", np.stack([np.exp((w[None, :] % DT + 1.0) * lg[2 * j + half][:, None]) for j in range(2)], 1))
    put(s, _S, "zeta", np.repeat(0.125 * np.exp((DT - 1.0 - w % DT)[:, None] * lg[None]), RQ, 1))
    put(s, _S, "own", (w[:, None] // DT == np.arange(NB)[None]).astype(float))
    put(s, _S, "sel", (g[:, None] == np.arange(G)[None]).astype(float))
    put(s, _S, "gl", np.stack([np.exp(DT * lg[2 * j + half]) for j in range(2)], 1))
    return t.astype(np.float32), s.astype(np.float32)


def chunks_before(u, memory=False):
    if memory or (isinstance(u, int) and u <= U_IN):
        return u
    return u * 3 - 2 * U_IN


def wait(eng, sem, value):
    if isinstance(value, int) and value <= 0:
        return
    eng.wait_ge(sem, value)


class Steps:

    def __init__(self, eng, sem):
        self.eng, self.sem, self.n, self.more = eng, sem, 0, 0

    def did(self, ins):
        ins.then_inc(self.sem, 1)
        self.n += 1

    def settle(self):
        wait(self.eng, self.sem, self.n + self.more)

    def loop(self, first, last, body):
        before = self.n
        body(first)
        steps = self.n - before
        if last - first > 1:
            with self.eng.Fori(first + 1, last) as i:
                if steps:
                    self.more = i * steps - (first + 1) * steps
                body(i)
            self.more = 0
            self.n = before + steps * (last - first)


def layer(nc, io):
    with ExitStack() as ctx:
        start = (nc.sbuf_base + 31) // 32 * 32
        top = [start]

        def place(name, shape, dt=F32, at=None):
            size = 4 * int(np.prod(shape[1:]))
            if at is None:
                at = top[0]
                top[0] = at + (size + 31) // 32 * 32
            t = nc.alloc_sbuf_tensor_at(name, shape, dt, offset=at)
            return t, at

        BLK = T * 4
        hT, at_h = place("hT", [P, KB, T])
        xhi, at_x = place("xhi", [P, KB, T], F32R)
        xlo, at_xl = place("xlo", [P, KB, T], F32R)
        yhi, at_y = place("yhi", [P, KB, T], F32R)
        ylo, _ = place("ylo", [P, KB, T], F32R)
        raw, _ = place("raw", [P, 2, KB, P])
        whi, _ = place("whi", [P, 2, KB, P], F32R)
        wlo, _ = place("wlo", [P, 2, KB, P], F32R)
        tab, at_tab = place("tab", [P, N_TAB])
        ss, at_ss = place("ss", [P, T])
        sq, at_sq = place("sq", [P, T // 2])
        rstd, _ = place("rstd", [P, T])
        gains, _ = place("gains", [P, 5, KB])
        gn, _ = place("gn", [P, 2, RH])
        sink8, _ = place("sink8", [P, NH])
        small, _ = place("small", [P, 96])
        assert top[0] <= nc.sbuf_usable_end, top[0]

        ident = tab[:, _T["ident"][0]:_T["ident"][0] + P]
        ones = tab[:, _T["ones"][0]:_T["ones"][0] + P]

        def table(n):
            a, w = _T[n]
            return tab[:, a:a + w]

        G_MIX, G_X, G_MLP, G_FIN, G_MEM = range(5)

        memx, _ = place("memx", [P, 2, D], at=at_y)
        mnhi, _ = place("mnhi", [P, KB, NM], F32R, at=at_y + 8192)
        mnlo, _ = place("mnlo", [P, KB, NM], F32R, at=at_y + 16384)
        mkvT, _ = place("mkvT", [P, 16, NM], at=at_y + 24576)
        mkv, _ = place("mkv", [P, 2, 2 * D], at=at_y + 40960)
        xin, _ = place("xin", [P, 2, D], at=at_y + 57344)
        diag, _ = place("diag", [P, NQ + 1, P], at=at_y)

        za, _ = place("za", [P, 10, T], at=at_y)
        zb, _ = place("zb", [P, 8, T], at=at_h)
        at_m = at_y + 10 * BLK
        stq, _ = place("stq", [P, 2, G, P], at=at_m)
        stk, _ = place("stk", [P, 2, 2 * P], at=at_m + 4096)
        stv, _ = place("stv", [P, 2, 2 * P], at=at_m + 6144)
        sc, _ = place("sc", [P, 2, G, 2 * P], at=at_m + 8192)
        pT, _ = place("pT", [P, 2, G * P], at=at_m + 16384)
        vtok, _ = place("vtok", [P, 2, P], at=at_m + 20480)
        rq, _ = place("rq", [P, 2, 2, P], at=at_m)
        rqx, _ = place("rqx", [P, 2, 2, P], at=at_m + 2048)
        rk, _ = place("rk", [P, 2, 2, P], at=at_m + 4096)
        rv, _ = place("rv", [P, 2, RH, P], at=at_m + 6144)
        krz, _ = place("krz", [P, RH * RQ], at=at_m + 10240)
        vrt, _ = place("vrt", [P, RH * RV], at=at_m + 11264)
        inner, _ = place("inner", [P, RH, P], at=at_m + 13312)
        onrm, _ = place("onrm", [P, RH, RV], at=at_m + 15360)
        state, _ = place("state", [P, 2, 2, RV], at=at_m + 19456)
        at_s = at_x
        off = [at_s]

        def scratch(name, shape):
            t, a = place(name, shape, at=off[0])
            off[0] += (4 * int(np.prod(shape[1:])) + 31) // 32 * 32
            return t

        stab = scratch("stab", [P, N_STAB])
        kc = scratch("kc", [P, NB, P])
        vc = scratch("vc", [P, NB, P])
        kcT = scratch("kcT", [P, NB, P])
        sT = scratch("sT", [P, NKV * P])
        snT = scratch("snT", [TS, NKV * P])
        ssc = scratch("ssc", [P, NKV, 160])
        psT = scratch("psT", [P, NKV * P])
        pnT = scratch("pnT", [TS, NKV * P])
        kzs = scratch("kzs", [TS, RH * RQ])
        kzm = scratch("kzm", [TS, NB, RH * RQ])
        vrs = scratch("vrs", [TS, RH * RV])
        ins_ = scratch("ins_", [TS, RH, TS])
        oTs = scratch("oTs", [P, RH, TS])
        ons = scratch("ons", [TS, RH, RV])
        rfs = scratch("rfs", [P, RH, TS])
        qxs = scratch("qxs", [P, 2, TS])
        sst, _ = place("sst", [P, NB, 2, RV], at=at_y - 4 * NB * 2 * RV)
        assert off[0] <= at_y - 4 * NB * 2 * RV
        kvtok, _ = place("kvtok", [TS, 2 * P], at=at_ss)
        pw, _ = place("pw", [P, 2 * P], at=at_ss + 1024)

        xq, _ = place("xq", [P, KB, T], at=at_x)
        mkT, _ = place("mkT", [P, KB, NM], at=at_xl)
        mv, _ = place("mv", [P, 2, D], at=at_xl + 8192)
        stx, _ = place("stx", [P, 2, KB, P], at=at_xl + 16384)
        xp, _ = place("xp", [P, XH, NM], at=at_xl + 24576)
        xpT, _ = place("xpT", [P, 2, XH * P], at=at_xl + 28672)
        kx, _ = place("kx", [P, 2, D], at=at_xl + 16384)
        kxT, _ = place("kxT", [P, 2, KB, P], at=at_xl + 24576)
        sxT, _ = place("sxT", [P, 2, P], at=at_xl)
        sxp, _ = place("sxp", [P, NM], at=at_xl + 1024)
        pxT, _ = place("pxT", [P, 2, P], at=at_xl + 2048)
        at_t = at_tab + 4 * 2 * P
        relu, _ = place("relu", [P, 2, CW], at=at_t)
        hsq, _ = place("hsq", [P, 2, CW], at=at_t + 2 * 4 * CW)
        ytok, _ = place("ytok", [P, 4, D], at=at_y)

        ps = ctx.enter_context(nc.psum_tensor("ps", [P, 8, 512], F32))

        def bank(b, n=1):
            return ps[:, b:b + n, :].rearrange("p b c -> p (b c)")

        spill = nc.dram_tensor("spill", [KB, P, T], F32, kind="Internal").ap()
        mkT_d = nc.dram_tensor("mkT_d", [P, KB * NM], F32, kind="Internal").ap()

        sem = {}

        def S(name):
            if name not in sem:
                sem[name] = ctx.enter_context(nc.semaphore(name))
            return sem[name]

        block = ctx.enter_context(nc.Block())

        s_raw = [S("raw_loaded_even"), S("raw_loaded_odd")]
        s_rawg = S("gate_raw_loaded")
        s_whi, s_wlo = S("w_hi_made"), S("w_lo_made")
        s_mm, s_ev = S("chunk_multiplied"), S("chunk_evacuated")

        def kpn(w):
            return w.rearrange("(k p) n -> p k n", p=P)

        def load_unit(sp, u, q, pieces):
            wait(sp, s_wlo, u - 1)
            for n, (dst, src) in enumerate(pieces):
                last = n == len(pieces) - 1
                sp.dma_start(dst, src).then_inc(s_raw[q], LOAD - 16 * n if last else 16)

        def split_hi(act, u, q, memory=False):
            act.wait_ge(s_raw[q], LOAD // 2 * (u - q) + LOAD)
            wait(act, s_mm, chunks_before(u - 1, memory))
            act.activation(whi[:, q], raw[:, q], ACT.Copy).then_inc(s_whi, 1)

        def load_gate(sp, u):
            wait(sp, s_wlo, u)
            sp.dma_start(raw[:, 0], kpn(io["w_in"][0])[:, :, ds((u - U_IN) * P, P)]).then_inc(s_rawg, 16)

        def split_gate(act, u):
            act.wait_ge(s_rawg, (u - U_GATE) * 16 + 16)
            act.wait_ge(s_mm, chunks_before(u))
            act.activation(whi[:, 0], raw[:, 0], ACT.Copy).then_inc(s_whi, 1)

        def split_lo(dve, u, q):
            dve.wait_ge(s_whi, u + 1)
            dve.tensor_tensor(wlo[:, q], raw[:, q], whi[:, q].bitcast(F32), ALU.subtract).then_inc(s_wlo, 1)

        def product(pe, u, q, c, hi, lo, w, memory=False, one_slot=False, last_block=None):
            before = c if one_slot and c == 0 else c - 1
            wait(pe, s_ev, chunks_before(u, memory) + before)
            out = ps[:, (q + c) % 2, 0:w]
            for k in range(KB):
                if k == KB - 1 and last_block is not None:
                    pe.wait_ge(*last_block)
                x1, x2 = hi[:, k, c * w:c * w + w], lo[:, k, c * w:c * w + w]
                pe.matmul(out, whi[:, q, k, :], x1, start=k == 0, stop=False)
                pe.matmul(out, whi[:, q, k, :], x2, start=False, stop=False)
                mm = pe.matmul(out, wlo[:, q, k, :], x1, start=False, stop=k == KB - 1)
            mm.then_inc(s_mm, 1)

        def unit(pe, u, q, hi, lo, last_block=None, before=None):
            pe.wait_ge(s_wlo, u + 1)
            for c in range(NCH):
                if before is not None:
                    before(c)
                product(pe, u, q, c, hi, lo, CW, last_block=last_block if c == 0 else None)

        def pairs(eng, first, n_units, body):
            body(first)
            if n_units > 2:
                with eng.Fori(1, n_units // 2) as i:
                    body(i * 2 + first)

        def chunk(t, m, c):
            return t[:, ds(m, 1), c * CW:(c + 1) * CW].rearrange("p a t -> p (a t)")

        def row(t, m):
            return t[:, ds(m, 1), :].rearrange("p a t -> p (a t)")

        def cols(t, a, b, n):
            return t[:, a:b, ds(n * P, P)]

        s_tab, s_mem, s_x = S("tables_loaded"), S("memory_loaded"), [S("x_loaded_even"), S("x_loaded_odd")]
        s_msq, s_mvar, s_mpow, s_mn = S("memory_squares"), S("memory_variance"), S("memory_rstd"), S("memory_scaled")
        s_mnT, s_mhi, s_mlo = S("memory_turned"), S("memory_hi"), S("memory_lo")
        s_xT, s_xea, s_xed = S("x_turned"), S("x_evacuated_act"), S("x_evacuated_dve")
        s_mt, s_mta, s_mtd, s_mout = S("kv_turned"), S("kv_evacuated_act"), S("kv_evacuated_dve"), S("kv_stored")
        s_hi, s_lo, s_ss = S("operand_hi"), S("operand_lo"), S("squares_summed")
        s_nmm, s_rstd = S("norm_summed"), S("rstd_made")
        s_pool, s_dve, s_act = S("pool_steps"), S("dve_steps"), S("act_steps")
        s_spill, s_back = S("residual_spilled"), [S("residual_back_0"), S("residual_back_1")]
        s_silu = S("gate_silu")
        s_wst, s_vT, s_vt = S("win_staged"), S("win_v_turned"), S("win_v_ready")
        s_ws, s_wsb, s_wm, s_we = S("win_scores"), S("win_biased"), S("win_max"), S("win_exp")
        s_wp, s_wpT, s_wpe, s_wo, s_woe = S("win_probs"), S("win_p_turned"), S("win_pT_ready"), S("win_out"), S("win_out_kept")
        s_rst, s_rT, s_krz, s_vrt = S("ret_staged"), S("ret_turned"), S("ret_kz"), S("ret_v")
        s_ri, s_rin, s_ro, s_rs, s_rstate = S("ret_inner"), S("ret_decayed"), S("ret_out"), S("ret_state_sum"), S("ret_state")
        s_rvar, s_rrs, s_ron, s_roT, s_rf, s_rg = S("ret_var"), S("ret_rstd"), S("ret_normed"), S("ret_o_turned"), S("ret_affine"), S("ret_gated")
        s_sqx, s_diag, s_root = S("x_squared"), S("x_diagonals"), S("root_made")
        s_pwT, s_pwe, s_pret = S("last_window_turned"), S("last_window_ready"), S("ret_state_stored")
        s_sld, s_sst, s_out = S("sample_loaded"), S("sample_state_loaded"), S("stored")
        s_xld, s_xst = S("cross_kv_loaded"), S("cross_staged")
        s_xs, s_xm, s_xe, s_xp = S("cross_scores"), S("cross_max"), S("cross_exp"), S("cross_probs")
        s_xpT, s_xpe, s_xo, s_xoh, s_xol = S("cross_p_turned"), S("cross_pT_ready"), S("cross_out"), S("cross_hi"), S("cross_lo")
        s_kl = [S("sx_loaded_0"), S("sx_loaded_1")]
        s_kT, s_kea, s_ked, s_ksc, s_vx = S("sx_k_turned"), S("sx_k_act"), S("sx_k_dve"), S("sx_scores"), S("sx_values")
        s_relu, s_sqr, s_hhi, s_hlo = S("relu_made"), S("square_made"), S("hidden_hi"), S("hidden_lo")
        s_yT, s_yt, s_yea, s_yed = S("y_scaled"), S("y_turned"), S("y_evac_act"), S("y_evac_dve")
        s_yout = [S(f"y_stored_{i}") for i in range(4)]
        N_TABS = 9
        N_SLD = 3
        XT = NQ + 1
        N_OUT = 2 * (NB + 1) + 2

        half = T // 2
        EPS_N, EPS_G = RMS_EPS, GN_EPS
        msq, mvar, mrs, mhalf = small[:, 8:10], small[:, 10:12], small[:, 12:14], small[:, 16:24]
        sqx = small[:, 24:24 + NQ + 1]
        wmax, wneg, wdif = small[:, 24:28], small[:, 28:36], small[:, 36:44]
        wsum, wsink, wrec = small[:, 44:52], small[:, 52:60], small[:, 60:68]
        gst, gmv = small[:, 68:92], small[:, 8:16]
        gvar, grs = small[:, 92:96], small[:, 0:4]

        @block.sync
        def _(sp):
            def stream(src, u0, n_units):
                def body(u):
                    for q in range(2):
                        load_unit(sp, u + q, q, [(raw[:, q], src[:, :, ds((u - u0 + q) * P, P)])])
                pairs(sp, u0, n_units, body)

            stream(kpn(io["w_xk"][0]), U_MEM, 8)
            stream(kpn(io["w_xv"][0]), U_MEM + 8, 8)
            wi = kpn(io["w_in"][0])

            def in_q(u):
                for q in range(2):
                    m = u - U_IN + q
                    load_unit(sp, u + q, q, [(raw[:, q, :, 0:HD], wi[:, :, ds(m * HD, HD)]),
                                             (raw[:, q, :, HD:P], wi[:, :, ds(m * HD + G * HD, HD)])])

            pairs(sp, U_IN, 4, in_q)
            stream(wi[:, :, 4 * P:], U_IN + 4, 10)
            load_gate(sp, U_GATE)
            with sp.Fori(1, 4) as i:
                load_gate(sp, i + U_GATE)
            for q in range(2):
                sp.sem_inc(s_raw[q], 2 * LOAD)
            sp.wait_ge(s_wlo, U_OUT)
            wo = io["w_out"][0]
            wo_0, wo_1 = (wo[j * G * HD:(j + 1) * G * HD, :].rearrange("(k p) n -> p k n", p=HD) for j in range(2))
            wo_r = kpn(wo[2 * G * HD:, :])

            def out_units(u):
                for q in range(2):
                    c = ds((u - U_OUT + q) * P, P)
                    load_unit(sp, u + q, q, [(raw[0:HD, q, 0:4, :], wo_0[:, :, c]), (raw[HD:P, q, 0:4, :], wo_1[:, :, c]),
                                             (raw[:, q, 4:8, :], wo_r[:, :, c])])

            pairs(sp, U_OUT, 8, out_units)
            stream(kpn(io["w_xq"][0]), U_XQ, 8)
            stream(kpn(io["w_xo"][0]), U_XO, 8)
            for c in range(FC):
                u0 = U_MLP + 16 * c
                stream(kpn(io["w_up"][0])[:, :, c * D:(c + 1) * D], u0, 8)
                stream(kpn(io["w_down"][0][c * D:(c + 1) * D, :]), u0 + 8, 8)
            yp, ys = io["y_prompt"][0], io["y_sample"].rearrange("b t d -> (b t) d")
            for t in range(XT):
                sp.wait_ge(s_yea, t + 1)
                sp.wait_ge(s_yed, t + 1)
                if t < NQ:
                    sp.dma_start(yp[t * P:(t + 1) * P, :], ytok[:, t % 4, :]).then_inc(s_yout[t % 4], 16)
                else:
                    sp.dma_start(ys, ytok[0:TS, t % 4, :]).then_inc(s_yout[t % 4], 16)
            for i in range(4):
                sp.wait_ge(s_yout[i], 16 * len(range(i, XT, 4)))
            sp.wait_ge(s_out, 16 * N_OUT)
            sp.wait_ge(s_pret, 32)
            sp.wait_ge(s_mout, 48)
            sp.wait_ge(S("smp_state_stored"), 16 * NB)

        @block.gpsimd
        def _(pool):
            st = Steps(pool, s_pool)

            def squares(m, done):
                pool.wait_ge(*done)
                for j in range(2):
                    c = slice(j * half, (j + 1) * half)
                    h = row(hT, m)[:, c]
                    if isinstance(m, int) and m == 0:
                        last = pool.tensor_tensor(ss[:, c], h, h, ALU.mult)
                        if j == 0:
                            st.did(last)
                        continue
                    st.settle()
                    st.did(pool.tensor_tensor(sq[:], h, h, ALU.mult))
                    st.settle()
                    last = pool.tensor_tensor(ss[:, c], ss[:, c], sq[:], ALU.add)
                    if j == 0:
                        st.did(last)
                last.then_inc(s_ss, 1)

            pool.dma_start(memx[:], io["mem_prompt"][0].rearrange("(t p) d -> p t d", p=P)).then_inc(s_mem, 16)
            pool.dma_start(tab[:], io["tables"]).then_inc(s_tab, 16)
            with nc.allow_non_contiguous_dma(reason="vectors of 1024 or 512 onto the partitions"):
                for n, g in ((G_MEM, io["g_mem"][0]), (G_MIX, io["g_mix"][0]), (G_X, io["g_xattn"][0]), (G_MLP, io["g_mlp"][0]), (G_FIN, io["g_final"])):
                    pool.dma_start(gains[:, n, :], g.rearrange("(k p) -> p k", p=P)).then_inc(s_tab, 16)
                pool.dma_start(gn[:, 0, :], io["ret_gn_g"][0].rearrange("h p -> p h")).then_inc(s_tab, 16)
                pool.dma_start(gn[:, 1, :], io["ret_gn_b"][0].rearrange("h p -> p h")).then_inc(s_tab, 16)
                pool.dma_start(sink8[:], io["attn_sinks"][0].partition_broadcast(P)).then_inc(s_tab, 16)
            pool.wait_ge(s_mvar, 1)
            pool.tensor_tensor(mrs, mvar, mhalf[:, 0:2], ALU.pow).then_inc(s_mpow, 1)

            for t in range(XT):
                wait(pool, s_xT, t - 1)
                wait(pool, s_sqx, t - 1)
                if t < NQ:
                    pool.dma_start(xin[:, t % 2, :], io["x_prompt"][0, t * P:(t + 1) * P, :]).then_inc(s_x[t % 2], 16)
                else:
                    pool.dma_start(xin[0:TS, t % 2, :], io["x_sample"].rearrange("b t d -> (b t) d")).then_inc(s_x[t % 2], 16)
            pool.wait_ge(s_xea, XT)
            pool.wait_ge(s_xed, XT)
            for k in range(KB):
                pool.dma_start(spill[k], hT[:, k, :]).then_inc(s_spill, 16)
            pool.wait_ge(s_ev, 16)
            pool.dma_start(mkT_d, mkvT[:, 0:KB, :].rearrange("p k t -> p (k t)")).then_inc(s_mout, 16)
            pool.wait_ge(s_mta, 4)
            pool.wait_ge(s_mtd, 4)
            pool.dma_start(io["p_mem_k"].rearrange("l b (t p) h d -> p (l b t) (h d)", p=P), mkv[:, :, 0:D]).then_inc(s_mout, 16)
            pool.dma_start(io["p_mem_v"].rearrange("l b (t p) h d -> p (l b t) (h d)", p=P), mkv[:, :, D:]).then_inc(s_mout, 16)

            pool.wait_ge(s_ev, chunks_before(U_IN + 6))

            def win_stage(n2):
                for p in range(2):
                    n = n2 * 2 + p
                    wait(pool, s_ws, n * 2 - 2)
                    prev = n if isinstance(n, int) and n == 0 else n - 1
                    pool.tensor_copy(stq[:, p], cols(za, 0, G, n)).then_inc(s_wst, 1)
                    for dst, b in ((stk, 4), (stv, 5)):
                        pool.tensor_copy(dst[:, p, 0:P], cols(za, b, b + 1, prev).rearrange("p a t -> p (a t)")).then_inc(s_wst, 1)
                        pool.tensor_copy(dst[:, p, P:2 * P], cols(za, b, b + 1, n).rearrange("p a t -> p (a t)")).then_inc(s_wst, 1)

            st.loop(0, NQ // 2, win_stage)

            pool.wait_ge(s_woe, NQ)
            pool.wait_ge(s_ev, chunks_before(U_GATE))

            def ret_stage(n, p):
                pool.tensor_copy(rk[:, p], cols(zb, 2, 4, n)).then_inc(s_rst, 1)
                pool.tensor_copy(rv[:, p], cols(zb, 4, 8, n)).then_inc(s_rst, 1)
                pool.tensor_copy(rq[:, p], cols(zb, 0, 2, n)).then_inc(s_rst, 1)
                pool.tensor_tensor(rqx[:, p], cols(zb, 0, 2, n), table("xi").rearrange("p (j t) -> p j t", j=2), ALU.mult).then_inc(s_rst, 1)

            def ret_norm(n2):
                for p in range(2):
                    n = n2 * 2 + p
                    pool.wait_ge(s_rvar, n + 1)
                    pool.tensor_tensor(grs, gvar, mhalf[:, 0:4], ALU.pow).then_inc(s_rrs, 1)
                    if not (isinstance(n2, int) and n2 == NQ // 2 - 1):
                        pool.wait_ge(s_ro, n + 1)
                        ret_stage(n + 2, p)

            ret_stage(0, 0)
            ret_stage(1, 1)
            st.loop(0, NQ // 2 - 1, ret_norm)
            ret_norm(NQ // 2 - 1)
            pool.wait_ge(s_rstate, RH * NQ)
            for e in range(2):
                pool.dma_start(io["p_ret"][0, 0].rearrange("(j h) d e -> h d j e", h=2)[e], state[e * RQ:(e + 1) * RQ, :, e, :]).then_inc(s_pret, 16)

            pool.wait_ge(s_mm, chunks_before(U_OUT))
            pool.dma_start(stab[:], io["sample_tables"]).then_inc(s_sld, 16)
            pool.dma_start(kc[:], io["cache_win_k"][0].rearrange("b k h d -> k b (h d)")).then_inc(s_sld, 16)
            pool.dma_start(vc[:], io["cache_win_v"][0].rearrange("b k h d -> k b (h d)")).then_inc(s_sld, 16)
            for b in range(NB):
                pool.dma_start(sst[:, b], io["state_ret"][0, b].rearrange("(j h) d e -> (h d) j e", h=2)).then_inc(s_sst, 16)
            pool.wait_ge(S("smp_var"), 1)
            pool.tensor_tensor(grs[0:TS], gvar[0:TS], mhalf[0:TS, 0:4], ALU.pow).then_inc(S("smp_rstd"), 1)
            pool.wait_ge(S("smp_inner"), 1)
            pool.wait_ge(S("smp_qx"), 1)
            pool.wait_ge(s_spill, 16 * KB)
            for k in range(4):
                pool.dma_start(hT[:, k, :], spill[k]).then_inc(s_back[0], 16)
            pool.wait_ge(S("smp_affine"), 4)
            pool.wait_ge(s_silu, 4)
            pool.tensor_tensor(zb[:, 4:8, TP:T], rfs[:], za[:, 6:10, TP:T], ALU.mult).then_inc(S("smp_gated"), 1)
            pool.wait_ge(S("smp_state"), 2)
            for b in range(NB):
                pool.dma_start(io["s_ret"][0, b].rearrange("(j h) d e -> (h d) j e", h=2), sst[:, b]).then_inc(S("smp_state_stored"), 16)
            pool.wait_ge(S("smp_kv_ready"), 1)
            pool.wait_ge(s_pwe, 1)
            for name, cache, j in (("s_win_k", "cache_win_k", 0), ("s_win_v", "cache_win_v", 1)):
                pool.dma_start(io[name][0, :, 0:WIN - DT].rearrange("b k h d -> b (k h d)"),
                               io[cache][0, :, DT:WIN].rearrange("b k h d -> b (k h d)")).then_inc(s_out, 16)
                for b in range(NB):
                    pool.dma_start(io[name][0, b, WIN - DT:WIN].rearrange("t h d -> t (h d)"),
                                   kvtok[b * DT:b * DT + DT, j * P:j * P + P]).then_inc(s_out, 16)
            pool.dma_start(io["p_win_k"].rearrange("l b k h d -> (l b k) (h d)"), pw[:, 0:P]).then_inc(s_out, 16)
            pool.dma_start(io["p_win_v"].rearrange("l b k h d -> (l b k) (h d)"), pw[:, P:2 * P]).then_inc(s_out, 16)
            pool.wait_ge(s_lo, 2 * KB)
            for k in range(4, KB):
                pool.dma_start(hT[:, k, :], spill[k]).then_inc(s_back[1], 16)

            def residual_squares(u0, before):
                def body(u):
                    for q in range(2):
                        if not (isinstance(u, int) and u == u0 and q == 0):
                            pool.wait_ge(s_ss, before + (u - u0) + q)
                        squares(u - u0 + q, (s_ev, chunks_before(u + q + 1)))
                body(u0)
                st.loop(1, 4, lambda i: body(i * 2 + u0))

            pool.wait_ge(s_out, 16 * N_OUT)
            residual_squares(U_OUT, 0)

            def x_stage(n2):
                for p in range(2):
                    n = n2 * 2 + p
                    wait(pool, s_xs, n - 1)
                    pool.tensor_copy(stx[:, p], cols(xq, 0, KB, n)).then_inc(s_xst, 1)

            pool.wait_ge(s_mm, chunks_before(U_XQ))
            pool.wait_ge(s_mout, 48)
            pool.dma_start(mkT[:].rearrange("p k t -> p (k t)"), mkT_d).then_inc(s_xld, 16)
            pool.dma_start(mv[:], io["p_mem_v"].rearrange("l b (t p) h d -> p (l b t) (h d)", p=P)).then_inc(s_xld, 16)
            pool.wait_ge(s_ev, chunks_before(U_XO))
            st.loop(0, NQ // 2, x_stage)

            pool.wait_ge(s_xs, NQ)

            def sx(b, cache, room):
                for kb in range(2):
                    room(b, kb)
                    pool.dma_start(kx[:, kb, :], io[cache][0, ds(b, 1), kb * P:(kb + 1) * P].rearrange("b k h d -> (b k) (h d)")).then_inc(s_kl[kb], 16)

            st.loop(0, NB, lambda b: sx(b, "cache_mem_k", lambda b, kb: wait(pool, s_kT, b * 2 + kb - 1)))
            pool.wait_ge(s_kT, 2 * NB)
            st.loop(0, NB, lambda b: sx(b, "cache_mem_v", lambda b, kb: wait(pool, s_vx, b)))
            residual_squares(U_XO, KB)
            residual_squares(U_END - 8, 2 * KB)

        @block.scalar
        def _(act):
            def copy(out, in_):
                return act.activation(out, in_, ACT.Copy)

            def prep_hi(m, dst, g, done):
                act.wait_ge(*done)
                act.activation(row(dst, m), row(hT, m), ACT.Copy, scale=gains[:, g, ds(m, 1)]).then_inc(s_hi, 1)

            def root(n):
                wait(act, s_ev, 16 if n == 1 else chunks_before({2: U_OUT, 3: U_XO, 4: U_END - 8}[n]))
                for c in range(NCH):
                    act.wait_ge(s_nmm, 3 * (n - 1) + c + 1)
                    a, b = (c * CW, (c + 1) * CW) if n > 1 else (c * 4 * P, min((c + 1) * 4 * P, T))
                    src = ps[:, 2 + c if n > 1 else (6, 7, 1)[c], 0:b - a]
                    act.activation(rstd[:, a:b], src, ACT.Sqrt, scale=1.0 / D, bias=small[:, 4:5]).then_inc(s_root, 1)

            def ahead(u, q, memory=False):
                split_hi(act, u + q + 1, 1 - q, memory)

            act.wait_ge(s_mem, 16)
            for t in range(2):
                act.activation(mkv[:, t, 0:D], memx[:, t, :], ACT.Square, accum_out=msq[:, t:t + 1]).then_inc(s_msq, 1)
            split_hi(act, 0, 0)
            act.wait_ge(s_mnT, 1)
            for k in range(KB):
                act.activation(mnhi[:, k, :], ps[:, 2 + k // 2, (k % 2) * NM:(k % 2) * NM + NM], ACT.Copy, scale=gains[:, G_MEM, k:k + 1]).then_inc(s_mhi, 1)

            def square_x(t, r, w):
                act.wait_ge(s_x[r], (t - r) * 8 + 16)
                wait(act, s_sqx, t)
                act.activation(ss[0:w, 0:D], xin[0:w, r, :], ACT.Square, accum_out=sqx[0:w, ds(t, 1)]).then_inc(s_sqx, 1)

            def mem_body(i):
                for r in range(2):
                    for q in range(2):
                        ahead(i * 4 + 2 * r, q, memory=True)
                    t = i * 2 + r
                    square_x(t, r, P)
                    act.wait_ge(s_xT, t + 1)
                    copy(hT[:, 0:4, ds(t * P, P)], ps[:, 2 + 2 * r, :].rearrange("p (k t) -> p k t", k=4)).then_inc(s_xea, 1)

            Steps(act, s_act).loop(0, 4, mem_body)
            square_x(NQ, 0, TS)
            act.wait_ge(s_xT, XT)
            copy(hT[:, 0:4, TP:T], ps[:, 2, :].rearrange("p (k t) -> p k t", k=4)[:, :, 0:TS]).then_inc(s_xea, 1)
            root(1)
            for k in range(KB):
                prep_hi(k, xhi, G_MIX, (s_xea, XT) if k < 4 else (s_xed, XT))
            for s in range(0, 8, 2):
                act.wait_ge(s_mt, s + 1)
                copy(mkv[:, s // 4, (s % 4) * 512:(s % 4) * 512 + 512], ps[:, 2 + s % 4, :]).then_inc(s_mta, 1)

            def plain_in(u):
                for q in range(2):
                    ahead(u, q)

            pairs(act, U_IN, 6, plain_in)

            def win_exp(n, kv):
                j = n * 2 + kv
                act.wait_ge(s_wm, j + 1)
                for g in range(G):
                    c = kv * G + g
                    act.activation(sc[:, kv, g, :], sc[:, kv, g, :], ACT.Exp, scale=0.125, bias=wneg[:, c:c + 1],
                                   accum_out=wsum[:, c:c + 1]).then_inc(s_we, 1)
                act.activation(wsink[:, kv * G:kv * G + G], wdif[:, kv * G:kv * G + G], ACT.Exp, scale=0.125).then_inc(s_we, 1)

            def win_v(n):
                act.wait_ge(s_vT, n + 1)
                copy(vtok[:].rearrange("p a d -> p (a d)"), ps[:, 7, 0:2 * P]).then_inc(s_vt, 1)

            def win_pT(n, kv):
                act.wait_ge(s_wpT, n * 2 + kv + 1)
                copy(pT[:].rearrange("p a t -> p (a t)"), bank(4, 2)).then_inc(s_wpe, 1)

            def win(n2):
                for p in range(2):
                    n = n2 * 2 + p
                    end = isinstance(n, int) and n == NQ - 1
                    if not end:
                        split_hi(act, n + U_RET + 1, 1 - p)
                    win_exp(n, 1)
                    win_pT(n, 0)
                    if not end:
                        win_exp(n + 1, 0)
                    win_pT(n, 1)
                    act.wait_ge(s_wo, n * 2 + 2)
                    copy(cols(za, 0, G, n), ps[:, 6, :].rearrange("p (g t) -> p g t", g=G)).then_inc(s_woe, 1)
                    if not end:
                        win_v(n + 1)

            win_v(0)
            win_exp(0, 0)
            Steps(act, s_act).loop(0, NQ // 2 - 1, win)
            win(NQ // 2 - 1)

            def ret_v(n):
                act.wait_ge(s_rT, n * 2 + 2)
                copy(vrt[:], ps[:, 3, :]).then_inc(s_vrt, 1)

            def silu(m):
                act.wait_ge(s_ev, chunks_before(m + U_GATE + 1))
                act.activation(row(za, m + 6), row(za, m + 6), ACT.Silu).then_inc(s_silu, 1)

            def ret(n2):
                for p in range(2):
                    n = n2 * 2 + p
                    if p == 0:
                        split_gate(act, n2 + U_GATE)
                    if not (isinstance(n, int) and n == NQ - 1):
                        ret_v(n + 1)
                    if p == 0 and not (isinstance(n, int) and n == 0):
                        silu(n2 - 1)
                    act.wait_ge(s_roT, n + 1)
                    for h in range(RH):
                        act.activation(cols(zb, 4 + h, 5 + h, n).rearrange("p a t -> p (a t)"), ps[:, 7, h * P:(h + 1) * P], ACT.Identity,
                                       scale=gn[:, 0, h:h + 1], bias=gn[:, 1, h:h + 1]).then_inc(s_rf, 1)

            ret_v(0)
            Steps(act, s_act).loop(0, NQ // 2 - 1, ret)
            ret(NQ // 2 - 1)
            silu(RH - 1)
            act.wait_ge(s_pwT, 1)
            copy(pw[:], ps[:, 2, 0:2 * P]).then_inc(s_pwe, 1)
            split_hi(act, U_OUT, 0)

            act.wait_ge(S("smp_k_turned"), 1)
            copy(kcT[:].rearrange("p b k -> p (b k)"), bank(2, 2)).then_inc(S("smp_kT_ready"), 1)
            act.wait_ge(S("smp_max"), 1)
            for kv in range(NKV):
                act.activation(ssc[:, kv, :], ssc[:, kv, :], ACT.Exp, scale=0.125, bias=wneg[:, kv:kv + 1], accum_out=wsum[:, kv:kv + 1]).then_inc(S("smp_exp"), 1)
            act.activation(wsink[:, 0:NKV], wdif[:, 0:NKV], ACT.Exp, scale=0.125).then_inc(S("smp_exp"), 1)
            act.wait_ge(S("smp_p_turned"), 1)
            copy(psT[:], ps[:, 5, 0:2 * P]).then_inc(S("smp_pT_ready"), 1)
            act.wait_ge(S("smp_out"), 1)
            copy(za[:, 0:G, TP:T].rearrange("p g (b t) -> p b g t", t=DT), ps[:, 4, 0:P].rearrange("p (b g t) -> p b g t", g=G, t=DT)).then_inc(S("smp_out_kept"), 1)
            act.wait_ge(S("smp_r_turned"), 1)
            copy(vrs[:], ps[0:TS, 3, :]).then_inc(S("smp_v_ready"), 1)
            act.wait_ge(S("smp_ret_out"), 1)
            copy(oTs[:].rearrange("p (j e) t -> p e j t", e=2), ps[:, 5:7, 0:2 * TS].rearrange("p e (j t) -> p e j t", j=2)).then_inc(S("smp_oT_ready"), 1)
            act.wait_ge(S("smp_on_turned"), 1)
            for h in range(RH):
                act.activation(rfs[:, h, :], ps[:, 7, h * TS:(h + 1) * TS], ACT.Identity, scale=gn[:, 0, h:h + 1], bias=gn[:, 1, h:h + 1]).then_inc(S("smp_affine"), 1)

            act.wait_ge(S("smp_out_kept"), 1)
            act.wait_ge(S("smp_gated"), 1)
            act.wait_ge(s_woe, NQ)
            act.wait_ge(s_rg, RH)
            act.wait_ge(S("smp_state"), 2)
            for k in range(KB):
                if k == 6:
                    act.wait_ge(S("smp_state_stored"), 16 * NB)
                copy(xhi[:, k, :], za[:, k, :] if k < 4 else zb[:, k, :]).then_inc(s_hi, 1)

            def residual(u0, dst, g):
                def body(u):
                    for q in range(2):
                        ahead(u, q)
                        prep_hi(u - u0 + q, dst, g, (s_ev, chunks_before(u + q + 1)))
                pairs(act, u0, 8, body)

            residual(U_OUT, yhi, G_X)
            root(2)
            pairs(act, U_XQ, 8, plain_in)

            def cross(n2):
                for p in range(2):
                    n = n2 * 2 + p
                    act.wait_ge(s_xm, n + 1)
                    wait(act, s_xpT, n)
                    for h in range(XH):
                        act.activation(xp[:, h, :], ps[:, 2 + h // 2, (h % 2) * NM:(h % 2) * NM + NM], ACT.Exp, scale=1.0 / 16, bias=wneg[:, h:h + 1],
                                       accum_out=wsum[:, h:h + 1]).then_inc(s_xe, 1)
                    act.wait_ge(s_xpT, n + 1)
                    wait(act, s_xo, n)
                    copy(xpT[:].rearrange("p a t -> p (a t)"), bank(4, 2)).then_inc(s_xpe, 1)
                    act.wait_ge(s_xo, n + 1)
                    copy(cols(yhi, 0, KB, n), bank(6, 2).rearrange("p (k t) -> p k t", k=KB)).then_inc(s_xoh, 1)

            Steps(act, s_act).loop(0, NQ // 2, cross)

            def kx_evac(b):
                for kb in range(2):
                    t = b * 2 + kb
                    act.wait_ge(s_kT, t + 1)
                    wait(act, s_ksc, t - 1)
                    copy(kxT[:, kb, 0:4, :].rearrange("p k t -> p (k t)"), ps[:, 2 + 2 * kb, :]).then_inc(s_kea, 1)

            Steps(act, s_act).loop(0, NB, kx_evac)
            act.wait_ge(S("sx_max"), 1)
            act.activation(sxp[:], ps[:, 7, 0:NM], ACT.Exp, scale=1.0 / 16, bias=wneg[:, 0:1], accum_out=wsum[:, 0:1]).then_inc(S("sx_exp"), 1)
            act.wait_ge(S("sx_p_turned"), 1)
            copy(pxT[:].rearrange("p a r -> p (a r)"), ps[:, 6, 0:2 * P]).then_inc(S("sx_pT_ready"), 1)
            act.wait_ge(s_vx, NB)
            copy(yhi[:, :, TP:T], ps[:, 2, 0:KB * TS].rearrange("p (k t) -> p k t", k=KB)).then_inc(s_xoh, 1)
            residual(U_XO, xhi, G_MLP)
            root(3)

            for f in range(FC):
                u0 = U_MLP + 16 * f

                def up(u):
                    for q in range(2):
                        ahead(u, q)
                        for c in range(NCH):
                            b = (q + c) % 2
                            hc = (u - u0 + q + 8 * f) * 3 + c
                            act.wait_ge(s_relu, hc + 1)
                            wait(act, s_hlo, hc - 1)
                            act.activation(hsq[:, b, :], relu[:, b, :], ACT.Square).then_inc(s_sqr, 1)
                            act.wait_ge(s_sqr, hc + 1)
                            copy(chunk(yhi, u - u0 + q, c), hsq[:, b, :]).then_inc(s_hhi, 1)

                pairs(act, u0, 8, up)
                if f < FC - 1:
                    pairs(act, u0 + 8, 8, plain_in)
                else:
                    pairs(act, u0 + 8, 6, plain_in)
                    ahead(u0 + 14, 0)
            root(4)
            for t in range(XT):
                act.wait_ge(s_yt, t + 1)
                if t >= 4:
                    act.wait_ge(s_yout[t % 4], 16 * (t // 4))
                w = P if t < NQ else TS
                copy(ytok[0:w, t % 4, 0:512], ps[0:w, 2 + 2 * (t % 2), :]).then_inc(s_yea, 1)

        @block.tensor
        def _(pe):
            def norm_sum(n):
                pe.wait_ge(s_ss, KB * (n - 1))
                for c in range(NCH):
                    pe.matmul(ps[:, 2 + c, 0:CW], ones, ss[:, c * CW:(c + 1) * CW], start=True, stop=True).then_inc(s_nmm, 1)

            def units(u0, n_units, hi, lo, last_block=None, before=None):
                def body(u):
                    for q in range(2):
                        first = isinstance(u, int) and q == 0
                        unit(pe, u + q, q, hi, lo, last_block if first else None, before if first else None)
                pairs(pe, u0, n_units, body)

            def turn(out, in_):
                n = in_.shape[0]
                return pe.transpose(out, in_, ident[0:n, 0:n])

            pe.wait_ge(s_tab, 16 * N_TABS)
            pe.wait_ge(s_mn, 2)
            for k in range(KB):
                for t in range(2):
                    mm = turn(ps[:, 2 + k // 2, (k % 2) * NM + t * P:(k % 2) * NM + (t + 1) * P], memx[:, t, k * P:(k + 1) * P])
            mm.then_inc(s_mnT, 1)
            pe.wait_ge(s_mlo, KB)

            def turn_x(t, r, w):
                wait(pe, s_xea, t - 1)
                wait(pe, s_xed, t - 1)
                pe.wait_ge(s_x[r], (t - r) * 8 + 16)
                for k in range(KB):
                    mm = turn(ps[:, 2 + 2 * r + k // 4, (k % 4) * P:(k % 4) * P + w], xin[0:w, r, k * P:(k + 1) * P])
                mm.then_inc(s_xT, 1)

            def mem_body(i):
                for r in range(2):
                    for q in range(2):
                        u = i * 4 + 2 * r + q
                        pe.wait_ge(s_wlo, u + 1)
                        product(pe, u, q, 0, mnhi, mnlo, NM, memory=True)
                    turn_x(i * 2 + r, r, P)

            Steps(pe, s_act).loop(0, 4, mem_body)
            turn_x(NQ, 0, TS)
            pe.wait_ge(s_ev, 16)
            pe.wait_ge(s_diag, XT)
            for t in range(XT):
                w = P if t < NQ else TS
                mm = pe.matmul(ps[:, (6, 7, 1)[t // 4], (t % 4) * P:(t % 4) * P + w], ones[0:w, :], diag[0:w, t, 0:w], start=True, stop=True)
                if t % 4 == 3 or t == NQ:
                    mm.then_inc(s_nmm, 1)
            pe.wait_ge(s_xea, XT)
            pe.wait_ge(s_xed, XT)
            for s in range(8):
                if s >= 4:
                    pe.wait_ge(s_mta if s % 2 == 0 else s_mtd, (s - 4) // 2 + 1)
                for j in range(4):
                    mm = turn(ps[:, 2 + s % 4, j * P:(j + 1) * P], mkvT[:, (s % 4) * 4 + j, (s // 4) * P:(s // 4 + 1) * P])
                mm.then_inc(s_mt, 1)
            pe.wait_ge(s_root, 3)
            pe.wait_ge(s_lo, KB - 1)
            units(U_IN, 6, xhi, xlo, last_block=(s_lo, KB))
            pe.wait_ge(s_mta, 4)
            pe.wait_ge(s_mtd, 4)

            def win_turn_v(n, p):
                pe.wait_ge(s_wst, n * 5 + 5)
                wait(pe, s_vt, n)
                for a in range(2):
                    mm = turn(ps[:, 7, a * P:(a + 1) * P], stv[:, p, a * P:(a + 1) * P])
                mm.then_inc(s_vT, 1)

            def win_scores(n, p, kv):
                r = slice(kv * HD, (kv + 1) * HD)
                pe.wait_ge(s_wst, n * 5 + 5)
                wait(pe, s_wsb, n * 8 + 4 * kv)
                for g in range(G):
                    mm = pe.matmul(ps[:, 2 + g // 2, (g % 2) * 256:(g % 2) * 256 + 256], stq[r, p, g, :], stk[r, p, :], start=True, stop=True)
                mm.then_inc(s_ws, 1)

            def win_turn_p(n, kv):
                pe.wait_ge(s_wp, n * 8 + 4 * kv + 4)
                wait(pe, s_wpe, n * 2 + kv)
                for a in range(2):
                    for g in range(G):
                        mm = turn(ps[:, 4 + a, g * P:(g + 1) * P], sc[:, kv, g, a * P:(a + 1) * P])
                mm.then_inc(s_wpT, 1)

            def win_values(n, kv):
                r = slice(kv * HD, (kv + 1) * HD)
                pe.wait_ge(s_wpe, n * 2 + kv + 1)
                pe.wait_ge(s_vt, n + 1)
                wait(pe, s_woe, n)
                for a in range(2):
                    mm = pe.matmul(ps[r, 6, :], vtok[:, a, r], pT[:, a, :], start=a == 0, stop=a == 1)
                mm.then_inc(s_wo, 1)

            def win(n2):
                for p in range(2):
                    n = n2 * 2 + p
                    u = n + U_RET
                    end = isinstance(n, int) and n == NQ - 1
                    win_scores(n, p, 1)
                    pe.wait_ge(s_wlo, u + 1)
                    product(pe, u, p, 0, xhi, xlo, CW)
                    win_turn_p(n, 0)
                    if not end:
                        win_scores(n + 1, 1 - p, 0)
                    win_values(n, 0)
                    product(pe, u, p, 1, xhi, xlo, CW)
                    win_turn_p(n, 1)
                    product(pe, u, p, 2, xhi, xlo, CW)
                    win_values(n, 1)
                    if not end:
                        win_turn_v(n + 1, 1 - p)

            win_turn_v(0, 0)
            win_scores(0, 0, 0)
            Steps(pe, s_act).loop(0, NQ // 2 - 1, win)
            win(NQ // 2 - 1)

            def ret_turn(n, p):
                pe.wait_ge(s_rst, n * 4 + 4)
                wait(pe, s_krz, n)
                wait(pe, s_vrt, n)
                for a in range(2):
                    mm = turn(ps[:, 2, a * P:(a + 1) * P], rk[:, p, a, :])
                mm.then_inc(s_rT, 1)
                for h in range(RH):
                    mm = turn(ps[:, 3, h * P:(h + 1) * P], rv[:, p, h, :])
                mm.then_inc(s_rT, 1)

            def ret_inner(n, p):
                wait(pe, s_rin, n * 2)
                wait(pe, s_rf, n * 4 - 4)
                for h in range(RH):
                    r = slice((h % 2) * RQ, (h % 2 + 1) * RQ)
                    mm = pe.matmul(ps[:, 4 if h % 2 == 0 else 7, (h // 2) * P:(h // 2 + 1) * P], rk[r, p, h // 2, :], rq[r, p, h // 2, :], start=True, stop=True)
                mm.then_inc(s_ri, 1)

            def ret(n2):
                u = n2 + U_GATE
                for p in range(2):
                    n = n2 * 2 + p
                    end = isinstance(n, int) and n == NQ - 1
                    pe.wait_ge(s_rin, n * 2 + 2)
                    pe.wait_ge(s_vrt, n + 1)
                    wait(pe, s_rstate, n * RH)
                    pe.wait_ge(S("ret_state_zeroed"), 1)
                    wait(pe, s_ron, n * 4)
                    for j in range(2):
                        pe.matmul(ps[:, 5, j * 2 * RV:(j + 1) * 2 * RV], rqx[:, p, j, :], state[:, j].rearrange("p e v -> p (e v)"), start=True, stop=False, skip_group_check=True)
                        for h in (2 * j, 2 * j + 1):
                            mm = pe.matmul(ps[:, 5, h * RV:(h + 1) * RV], inner[:, h, :], vrt[:, h * RV:(h + 1) * RV], start=False, stop=True, skip_group_check=True)
                    mm.then_inc(s_ro, 1)
                    pe.wait_ge(s_krz, n + 1)
                    for h in range(RH):
                        r = slice((h % 2) * RQ, (h % 2 + 1) * RQ)
                        mm = pe.matmul(ps[r, 6, (h // 2) * RV:(h // 2 + 1) * RV], krz[:, h * RQ:(h + 1) * RQ], vrt[:, h * RV:(h + 1) * RV], start=True, stop=True)
                    mm.then_inc(s_rs, 1)
                    if not end:
                        ret_turn(n + 1, 1 - p)
                        ret_inner(n + 1, 1 - p)
                    if p == 0:
                        pe.wait_ge(s_wlo, u + 1)
                    product(pe, u, 0, p, xhi, xlo, CW, one_slot=True)
                    pe.wait_ge(s_ron, n * 4 + 4)
                    wait(pe, s_rin, n * 2 + (2 if end else 4))
                    wait(pe, s_rf, n * 4)
                    for h in range(RH):
                        mm = turn(ps[:, 7, h * P:(h + 1) * P], onrm[:, h, :])
                    mm.then_inc(s_roT, 1)
                product(pe, u, 0, 2, xhi, xlo, CW)

            pe.wait_ge(s_woe, NQ)
            pe.wait_ge(s_vt, NQ)
            ret_turn(0, 0)
            ret_inner(0, 0)
            Steps(pe, s_act).loop(0, NQ // 2 - 1, ret)
            ret(NQ // 2 - 1)
            for a in range(2):
                mm = turn(ps[:, 2, a * P:(a + 1) * P], za[:, 4 + a, TP - WIN:TP])
            mm.then_inc(s_pwT, 1)
            pe.wait_ge(s_pwe, 1)

            pe.wait_ge(s_rf, 4 * NQ)
            pe.wait_ge(s_rstate, RH * NQ)
            pe.wait_ge(s_sld, 16 * N_SLD)
            for b in range(NB):
                mm = turn(ps[:, 2 + b // 4, (b % 4) * P:(b % 4 + 1) * P], kc[:, b, :])
            mm.then_inc(S("smp_k_turned"), 1)
            for a in range(2):
                mm = turn(ps[0:TS, 4, a * P:(a + 1) * P], za[:, 4 + a, TP:T])
            mm.then_inc(S("smp_kv_turned"), 1)
            pe.wait_ge(S("smp_kT_ready"), 1)
            for kv in range(NKV):
                r = slice(kv * HD, (kv + 1) * HD)
                for b in range(NB):
                    mm = pe.matmul(ps[:, 5 + kv, b * 16:b * 16 + 16].rearrange("p (g t) -> p g t", t=DT), kcT[r, b, :],
                                   za[r, 0:G, TP + b * DT:TP + b * DT + DT], start=True, stop=True)
            mm.then_inc(S("smp_scores"), 1)
            for kv in range(NKV):
                r = slice(kv * HD, (kv + 1) * HD)
                mm = pe.matmul(ps[0:TS, 5 + kv, P:2 * P].rearrange("p (b g t) -> p b g t", g=G, t=DT), za[r, 4, TP:T],
                               za[r, 0:G, TP:T].rearrange("p g (b t) -> p b g t", t=DT), start=True, stop=True)
            mm.then_inc(S("smp_scores"), 1)
            pe.wait_ge(S("smp_s_ready"), 2)
            for kv in range(NKV):
                turn(ps[:, 7, kv * 160:kv * 160 + WIN], sT[:, kv * P:(kv + 1) * P])
                mm = turn(ps[:, 7, kv * 160 + WIN:kv * 160 + 160], snT[:, kv * P:(kv + 1) * P])
            mm.then_inc(S("smp_s_turned"), 1)
            pe.wait_ge(S("smp_probs"), 2)
            for kv in range(NKV):
                turn(ps[:, 5, kv * P:(kv + 1) * P], ssc[:, kv, 0:WIN])
                mm = turn(ps[0:TS, 6, kv * P:(kv + 1) * P], ssc[:, kv, WIN:160])
            mm.then_inc(S("smp_p_turned"), 1)
            pe.wait_ge(S("smp_pT_ready"), 1)
            pe.wait_ge(S("smp_pn_ready"), 1)
            pe.wait_ge(S("smp_kv_ready"), 1)
            for kv in range(NKV):
                r = slice(kv * HD, (kv + 1) * HD)
                pe.matmul(ps[r, 4, 0:P], kvtok[:, P + kv * HD:P + (kv + 1) * HD], pnT[:, kv * P:(kv + 1) * P], start=True, stop=False, skip_group_check=True)
                for b in range(NB):
                    mm = pe.matmul(ps[r, 4, b * 16:(b + 1) * 16], vc[:, b, r], psT[:, kv * P + b * 16:kv * P + (b + 1) * 16],
                                   start=False, stop=b == NB - 1, skip_group_check=True)
            mm.then_inc(S("smp_out"), 1)
            for a in range(2):
                turn(ps[0:TS, 2, a * P:(a + 1) * P], zb[:, 2 + a, TP:T])
            for h in range(RH):
                mm = turn(ps[0:TS, 3, h * P:(h + 1) * P], zb[:, 4 + h, TP:T])
            mm.then_inc(S("smp_r_turned"), 1)
            for h in range(RH):
                r = slice((h % 2) * RQ, (h % 2 + 1) * RQ)
                mm = pe.matmul(ps[0:TS, 7 - h % 2, (h // 2) * TS:(h // 2 + 1) * TS], zb[r, 2 + h // 2, TP:T], zb[r, h // 2, TP:T], start=True, stop=True)
            mm.then_inc(S("smp_inner"), 1)
            pe.wait_ge(S("smp_decayed"), 2)
            pe.wait_ge(S("smp_v_ready"), 1)
            pe.wait_ge(S("smp_qx"), 1)
            pe.wait_ge(s_sst, 16 * NB)
            for h in range(RH):
                r = slice((h % 2) * RQ, (h % 2 + 1) * RQ)
                o = ps[:, 5 + h % 2, (h // 2) * TS:(h // 2 + 1) * TS]
                pe.matmul(o, vrs[:, h * RV:(h + 1) * RV], ins_[:, h, :], start=True, stop=False, skip_group_check=True)
                for b in range(NB):
                    mm = pe.matmul(o[:, b * DT:b * DT + DT], sst[r, b, h // 2, :], qxs[r, h // 2, b * DT:(b + 1) * DT],
                                   start=False, stop=b == NB - 1, skip_group_check=True)
            mm.then_inc(S("smp_ret_out"), 1)
            pe.wait_ge(S("smp_oT_ready"), 1)
            pe.wait_ge(S("smp_out_kept"), 1)
            for h in range(RH):
                mm = turn(ps[0:TS, 4, h * RV:(h + 1) * RV], oTs[:, h, :])
            mm.then_inc(S("smp_o_turned"), 1)
            pe.wait_ge(S("smp_normed"), RH)
            for h in range(RH):
                mm = turn(ps[:, 7, h * TS:(h + 1) * TS], ons[:, h, :])
            mm.then_inc(S("smp_on_turned"), 1)
            pe.wait_ge(S("smp_kz_masked"), NB)
            pe.wait_ge(S("smp_out_kept"), 1)
            for b in range(NB):
                for h in range(RH):
                    r, s = slice((h % 2) * RQ, (h % 2 + 1) * RQ), b * 2 + h // 2
                    mm = pe.matmul(ps[r, 2 + s // 4, (s % 4) * RV:(s % 4 + 1) * RV], kzm[:, b, h * RQ:(h + 1) * RQ], vrs[:, h * RV:(h + 1) * RV], start=True, stop=True)
            mm.then_inc(S("smp_state_sum"), 1)

            pe.wait_ge(s_lo, 2 * KB)
            pe.wait_ge(s_ev, chunks_before(U_OUT))
            units(U_OUT, 8, xhi, xlo)
            pe.wait_ge(s_lo, 3 * KB - 1)
            units(U_XQ, 8, yhi, ylo, last_block=(s_lo, 3 * KB), before=lambda c: norm_sum(2) if c == 1 else None)
            pe.wait_ge(s_root, 6)

            pe.wait_ge(s_xld, 32)

            def cross(n2):
                for p in range(2):
                    n = n2 * 2 + p
                    pe.wait_ge(s_xst, n + 1)
                    wait(pe, s_xe, 4 * n)
                    for h in range(XH):
                        for dd in range(2):
                            mm = pe.matmul(ps[:, 2 + h // 2, (h % 2) * NM:(h % 2) * NM + NM], stx[:, p, 2 * h + dd, :], mkT[:, 2 * h + dd, :], start=dd == 0, stop=dd == 1)
                    mm.then_inc(s_xs, 1)
                    pe.wait_ge(s_xp, 4 * n + 4)
                    wait(pe, s_xpe, n)
                    for a in range(2):
                        for h in range(XH):
                            mm = turn(ps[:, 4 + a, h * P:(h + 1) * P], xp[:, h, a * P:(a + 1) * P])
                    mm.then_inc(s_xpT, 1)
                    pe.wait_ge(s_xpe, n + 1)
                    wait(pe, s_xol, n)
                    for k in range(KB):
                        for a in range(2):
                            mm = pe.matmul(ps[:, 6 + k // 4, (k % 4) * P:(k % 4 + 1) * P], mv[:, a, k * P:(k + 1) * P], xpT[:, a, (k // 2) * P:(k // 2 + 1) * P], start=a == 0, stop=a == 1)
                    mm.then_inc(s_xo, 1)

            Steps(pe, s_act).loop(0, NQ // 2, cross)
            pe.wait_ge(s_xpe, NQ)
            pe.wait_ge(s_xe, 4 * NQ)
            pe.wait_ge(s_xol, NQ)

            def sxk(b):
                for kb in range(2):
                    t = b * 2 + kb
                    pe.wait_ge(s_kl[kb], b * 16 + 16)
                    wait(pe, s_kea, t - 1)
                    wait(pe, s_ked, t - 1)
                    for k in range(KB):
                        mm = turn(ps[:, 2 + 2 * kb + k // 4, (k % 4) * P:(k % 4 + 1) * P], kx[:, kb, k * P:(k + 1) * P])
                    mm.then_inc(s_kT, 1)
                for kb in range(2):
                    t = b * 2 + kb
                    pe.wait_ge(s_kea, t + 1)
                    pe.wait_ge(s_ked, t + 1)
                    for h in range(XH):
                        for dd in range(2):
                            mm = pe.matmul(ps[:, 6, ds(b * 16 + (kb * P + h * DT), DT)], kxT[:, kb, 2 * h + dd, :], xq[:, 2 * h + dd, ds(b * DT + TP, DT)], start=dd == 0, stop=dd == 1)
                    mm.then_inc(s_ksc, 1)

            Steps(pe, s_act).loop(0, NB, sxk)
            pe.wait_ge(S("sx_s_ready"), 1)
            for kb in range(2):
                mm = turn(ps[:, 7, kb * P:(kb + 1) * P], sxT[:, kb, :])
            mm.then_inc(S("sx_s_turned"), 1)
            pe.wait_ge(S("sx_probs"), 1)
            for kb in range(2):
                mm = turn(ps[:, 6, kb * P:(kb + 1) * P], sxp[:, kb * P:(kb + 1) * P])
            mm.then_inc(S("sx_p_turned"), 1)
            pe.wait_ge(S("sx_pT_ready"), 1)

            def sxv(b):
                for kb in range(2):
                    pe.wait_ge(s_kl[kb], b * 16 + 16 * (NB + 1))
                for k in range(KB):
                    for kb in range(2):
                        mm = pe.matmul(ps[:, 2, ds(b * DT + k * TS, DT)], kx[:, kb, k * P:(k + 1) * P], pxT[:, kb, ds(b * 16 + (k // 2) * DT, DT)], start=kb == 0, stop=kb == 1)
                mm.then_inc(s_vx, 1)

            Steps(pe, s_act).loop(0, NB, sxv)
            pe.wait_ge(s_xol, NQ + 1)
            units(U_XO, 8, yhi, ylo)
            pe.wait_ge(s_lo, 4 * KB - 1)
            for f in range(FC):
                u0 = U_MLP + 16 * f
                if f == 0:
                    units(u0, 8, xhi, xlo, last_block=(s_lo, 4 * KB), before=lambda c: norm_sum(3) if c == 1 else None)
                else:
                    units(u0, 8, xhi, xlo)
                units(u0 + 8, 8, yhi, ylo, before=lambda c: pe.wait_ge(s_hlo, 24 * f + 21 + c + 1))
            pe.wait_ge(s_root, 9)
            norm_sum(4)
            pe.wait_ge(s_yT, KB)
            for t in range(XT):
                w = P if t < NQ else TS
                if t >= 2:
                    pe.wait_ge(s_yea, t - 1)
                    pe.wait_ge(s_yed, t - 1)
                for k in range(KB):
                    mm = turn(ps[0:w, 2 + 2 * (t % 2) + k // 4, (k % 4) * P:(k % 4 + 1) * P], hT[:, k, t * P:t * P + w])
                mm.then_inc(s_yt, 1)

        @block.vector
        def _(dve):
            st = Steps(dve, s_dve)

            def prep_lo(m, n, hi, lo, g):
                dve.wait_ge(s_hi, n + 1)
                dve.scalar_tensor_tensor(row(lo, m), row(hT, m), gains[:, g, ds(m, 1)], row(hi, m).bitcast(F32), ALU.mult, ALU.subtract).then_inc(s_lo, 1)

            def invert(n, c):
                a, b = (c * CW, (c + 1) * CW) if n > 1 else (c * 4 * P, min((c + 1) * 4 * P, T))
                dve.wait_ge(s_root, 3 * (n - 1) + c + 1)
                dve.reciprocal(rstd[:, a:b], rstd[:, a:b]).then_inc(s_rstd, 1)
                dve.wait_ge(s_rstd, 3 * (n - 1) + c + 1)

            def evac(u, q, dst_of, last=False, before=None):
                if not last:
                    split_lo(dve, u + 1, 1 - q)
                for c in range(NCH):
                    if before is not None:
                        before(c)
                    dve.wait_ge(s_mm, chunks_before(u) + c + 1)
                    dst_of(u, q, c).then_inc(s_ev, 1)

            def scaled(t, m0):
                def f(u, q, c):
                    return dve.tensor_tensor(chunk(t, u - m0, c), ps[:, (q + c) % 2, 0:CW], rstd[:, c * CW:(c + 1) * CW], ALU.mult)
                return f

            def added(m0):
                def f(u, q, c):
                    return dve.tensor_tensor(chunk(hT, u - m0, c), ps[:, (q + c) % 2, 0:CW], chunk(hT, u - m0, c), ALU.add)
                return f

            def run(u0, n_units, f, after=None, last=False, before=None):
                def body(u):
                    for q in range(2):
                        evac(u + q, q, f, before=before if isinstance(u, int) and q == 0 else None)
                        if after is not None:
                            after(u + q)
                if not last:
                    pairs(dve, u0, n_units, body)
                    return
                pairs(dve, u0, n_units - 2, body)
                for q in range(2):
                    evac(u0 + n_units - 2 + q, q, f, last=q == 1)

            dve.memset(mhalf, -0.5).then_inc(S("dve_constants"), 1)
            dve.memset(small[:, 4:5], EPS_N).then_inc(S("dve_constants"), 1)
            dve.wait_ge(s_msq, 2)
            dve.wait_ge(S("dve_constants"), 2)
            dve.tensor_scalar(mvar, msq, 1.0 / D, EPS_N, ALU.mult, ALU.add).then_inc(s_mvar, 1)
            dve.wait_ge(s_mpow, 1)
            for t in range(2):
                dve.tensor_scalar(memx[:, t, :], memx[:, t, :], mrs[:, t:t + 1], None, ALU.mult).then_inc(s_mn, 1)
            dve.wait_ge(s_tab, 16 * N_TABS)
            st.did(dve.tensor_scalar(sink8[:], sink8[:], 8.0, None, ALU.mult))
            split_lo(dve, 0, 0)
            for k in range(KB):
                dve.wait_ge(s_mhi, k // 2 * 2 + 2)
                dve.scalar_tensor_tensor(mnlo[:, k, :], ps[:, 2 + k // 2, (k % 2) * NM:(k % 2) * NM + NM], gains[:, G_MEM, k:k + 1], mnhi[:, k, :].bitcast(F32),
                                         ALU.mult, ALU.subtract).then_inc(s_mlo, 1)

            def mem_body(i):
                for r in range(2):
                    for q in range(2):
                        u = i * 4 + 2 * r + q
                        split_lo(dve, u + 1, 1 - q)
                        dve.wait_ge(s_mm, u + 1)
                        dve.tensor_copy(mkvT[:, ds(u, 1), :].rearrange("p a t -> p (a t)"), ps[:, q, 0:NM]).then_inc(s_ev, 1)
                    t = i * 2 + r
                    dve.wait_ge(s_xT, t + 1)
                    dve.tensor_copy(hT[:, 4:8, ds(t * P, P)], ps[:, 3 + 2 * r, :].rearrange("p (k t) -> p k t", k=4)).then_inc(s_xed, 1)

            st.loop(0, 4, mem_body)
            dve.wait_ge(s_xT, XT)
            dve.tensor_copy(hT[:, 4:8, TP:T], ps[:, 3, :].rearrange("p (k t) -> p k t", k=4)[:, :, 0:TS]).then_inc(s_xed, 1)
            dve.wait_ge(s_sqx, XT)
            for t in range(XT):
                w = P if t < NQ else TS
                dve.tensor_scalar(diag[0:w, t, 0:w], ident[0:w, 0:w], sqx[0:w, t:t + 1], None, ALU.mult).then_inc(s_diag, 1)
            for k in range(KB):
                prep_lo(k, k, xhi, xlo, G_MIX)
            for s in range(1, 8, 2):
                dve.wait_ge(s_mt, s + 1)
                dve.tensor_copy(mkv[:, s // 4, (s % 4) * 512:(s % 4) * 512 + 512], ps[:, 2 + s % 4, :]).then_inc(s_mtd, 1)
            for c in range(NCH):
                invert(1, c)
            dve.wait_ge(s_mout, 48)
            run(U_IN, 6, scaled(za, U_IN))
            dve.wait_ge(s_spill, 16 * KB)

            def softmax_tail(c0, n, probs, exp_sem, exp_n, out_sem, sink=True):
                dve.wait_ge(exp_sem, exp_n)
                if sink:
                    st.did(dve.tensor_tensor(wsum[:, c0:c0 + n], wsum[:, c0:c0 + n], wsink[:, c0:c0 + n], ALU.add))
                    st.settle()
                st.did(dve.reciprocal(wrec[:, c0:c0 + n], wsum[:, c0:c0 + n]))
                st.settle()
                for g in range(n):
                    dve.tensor_scalar(probs(g), probs(g), wrec[:, c0 + g:c0 + g + 1], None, ALU.mult).then_inc(out_sem, 1)

            dist = table("dist").rearrange("p (v c) -> p v c", v=2)

            def win_max(n, kv):
                j, c0 = n * 2 + kv, kv * G
                dve.wait_ge(s_ws, j + 1)
                wait(dve, s_wpT, j - 1)
                which = 0 if isinstance(n, int) and n == 0 else 1
                for g in range(G):
                    dve.scalar_tensor_tensor(sc[:, kv, g, :], dist[:, which, :], 8.0 * SLOPES[c0 + g], ps[:, 2 + g // 2, (g % 2) * 256:(g % 2) * 256 + 256],
                                             ALU.mult, ALU.add).then_inc(s_wsb, 1)
                dve.wait_ge(s_wsb, j * 4 + 4)
                st.did(dve.tensor_reduce(wmax, sc[:, kv], AX.X, ALU.max))
                st.settle()
                st.did(dve.tensor_tensor(wmax, wmax, sink8[:, c0:c0 + G], ALU.max))
                st.settle()
                st.did(dve.tensor_scalar(wneg[:, c0:c0 + G], wmax, -0.125, None, ALU.mult))
                st.settle()
                dve.tensor_tensor(wdif[:, c0:c0 + G], sink8[:, c0:c0 + G], wmax, ALU.subtract).then_inc(s_wm, 1)

            def win_probs(n, kv):
                softmax_tail(kv * G, G, lambda g: sc[:, kv, g, :], s_we, n * 10 + 5 * kv + 5, s_wp)

            def win(n2):
                for p in range(2):
                    n = n2 * 2 + p
                    u = n + U_RET
                    end = isinstance(n, int) and n == NQ - 1

                    def evacuate(c):
                        dve.wait_ge(s_mm, chunks_before(u) + c + 1)
                        scaled(zb, U_RET)(u, p, c).then_inc(s_ev, 1)

                    win_max(n, 1)
                    if not end:
                        split_lo(dve, u + 1, 1 - p)
                    evacuate(0)
                    win_probs(n, 1)
                    if not end:
                        win_max(n + 1, 0)
                    evacuate(1)
                    if not end:
                        win_probs(n + 1, 0)
                    evacuate(2)

            win_max(0, 0)
            win_probs(0, 0)
            st.loop(0, NQ // 2 - 1, win)
            win(NQ // 2 - 1)

            dve.wait_ge(s_woe, NQ)
            dve.wait_ge(s_wpe, 2 * NQ)
            dve.memset(state[:], 0.0).then_inc(S("ret_state_zeroed"), 1)
            dve.wait_ge(S("ret_state_zeroed"), 1)
            gl = table("gl")
            decay = table("decay").rearrange("p (h t) -> p h t", h=RH)

            def by_half(t):
                return t.rearrange("p (j e) t -> p e j t", e=2)

            def stats(w, o_of, var_sem, meanwhile=None):
                for h in range(RH):
                    st.did(dve.bn_stats(gst[0:w, h * 6:(h + 1) * 6], o_of(h)))
                st.settle()
                if meanwhile is not None:
                    meanwhile()
                for h in range(RH):
                    st.did(dve.bn_aggr(gmv[0:w, h * 2:(h + 1) * 2], gst[0:w, h * 6:(h + 1) * 6]))
                st.settle()
                dve.tensor_scalar(gvar[0:w], gmv[0:w].rearrange("p (h m) -> p h m", m=2)[:, :, 1], EPS_G, None, ALU.add).then_inc(var_sem, 1)

            def ret_keys(n):
                dve.wait_ge(s_rT, n * 2 + 1)
                wait(dve, s_rs, n)
                dve.tensor_tensor(krz[:], ps[:, 2, 0:2 * P], table("zeta"), ALU.mult).then_inc(s_krz, 1)
                dve.wait_ge(s_ri, n + 1)
                for e, b in ((0, 4), (1, 7)):
                    dve.tensor_tensor(by_half(inner[:])[:, e], ps[:, b, 0:2 * P].rearrange("p (j t) -> p j t", j=2), by_half(decay)[:, e], ALU.mult).then_inc(s_rin, 1)

            def ret(n2):
                u = n2 + U_GATE
                for p in range(2):
                    n = n2 * 2 + p

                    def update():
                        dve.wait_ge(s_rs, n + 1)
                        for h in range(RH):
                            e, j = h % 2, h // 2
                            r = slice(e * RQ, (e + 1) * RQ)
                            dve.scalar_tensor_tensor(state[r, j, e, :], state[r, j, e, :], gl[r, j:j + 1], ps[r, 6, j * RV:(j + 1) * RV], ALU.mult, ALU.add).then_inc(s_rstate, 1)

                    dve.wait_ge(s_ro, n + 1)
                    stats(P, lambda h: ps[:, 5, h * RV:(h + 1) * RV], s_rvar, update)
                    if p == 0:
                        split_lo(dve, u, 0)
                    if not (isinstance(n, int) and n == NQ - 1):
                        ret_keys(n + 1)
                    dve.wait_ge(s_rrs, n + 1)
                    wait(dve, s_roT, n)
                    for h in range(RH):
                        dve.tensor_scalar(onrm[:, h, :], ps[:, 5, h * RV:(h + 1) * RV], gmv[:, 2 * h:2 * h + 1], grs[:, h:h + 1], ALU.subtract, ALU.mult).then_inc(s_ron, 1)
                    for c in (0,) if p == 0 else (1, 2):
                        dve.wait_ge(s_mm, chunks_before(u) + c + 1)
                        scaled(za, U_IN + 8)(u, 0, c).then_inc(s_ev, 1)

            ret_keys(0)
            st.loop(0, NQ // 2 - 1, ret)
            ret(NQ // 2 - 1)
            split_lo(dve, U_OUT, 0)
            dve.wait_ge(s_silu, RH)
            dve.wait_ge(s_rf, RH * NQ)
            for h in range(RH):
                dve.tensor_tensor(zb[:, 4 + h, 0:TP], zb[:, 4 + h, 0:TP], za[:, 6 + h, 0:TP], ALU.mult).then_inc(s_rg, 1)

            def stable(n, w=P):
                a, k = _S[n]
                return stab[0:w, a:a + k]

            dve.wait_ge(S("smp_kv_turned"), 1)
            dve.tensor_copy(kvtok[:], ps[0:TS, 4, 0:2 * P]).then_inc(S("smp_kv_ready"), 1)
            dve.wait_ge(S("smp_scores"), 2)
            dve.tensor_copy(sT[:].rearrange("p (k r) -> p k r", k=NKV), ps[:, 5:7, 0:P]).then_inc(S("smp_s_ready"), 1)
            dve.tensor_copy(snT[:].rearrange("p (k r) -> p k r", k=NKV), ps[0:TS, 5:7, P:2 * P]).then_inc(S("smp_s_ready"), 1)
            for kv in range(NKV):
                st.did(dve.tensor_tensor(wdif[:, kv * G:kv * G + G], sink8[:, kv * G:kv * G + G], stable("sel"), ALU.mult))
            st.settle()
            st.did(dve.tensor_reduce(wrec[:, 4:6], wdif.rearrange("p (k g) -> p k g", g=G), AX.X, ALU.add))
            dve.wait_ge(S("smp_s_turned"), 1)
            st.did(dve.tensor_tensor(ssc[:].rearrange("p k c -> p (k c)"), ps[:, 7, 0:320], stable("bias"), ALU.add))
            st.settle()
            st.did(dve.tensor_reduce(wmax[:, 0:2], ssc[:], AX.X, ALU.max))
            st.settle()
            st.did(dve.tensor_tensor(wmax[:, 0:2], wmax[:, 0:2], wrec[:, 4:6], ALU.max))
            st.settle()
            st.did(dve.tensor_scalar(wneg[:, 0:2], wmax[:, 0:2], -0.125, None, ALU.mult))
            st.settle()
            dve.tensor_tensor(wdif[:, 0:2], wrec[:, 4:6], wmax[:, 0:2], ALU.subtract).then_inc(S("smp_max"), 1)
            softmax_tail(0, 2, lambda kv: ssc[:, kv, :], S("smp_exp"), 3, S("smp_probs"))
            dve.wait_ge(S("smp_p_turned"), 1)
            dve.tensor_copy(pnT[:], ps[0:TS, 6, 0:2 * P]).then_inc(S("smp_pn_ready"), 1)
            dve.tensor_tensor(qxs[:], zb[:, 0:2, TP:T], stable("xi").rearrange("p (j t) -> p j t", j=2), ALU.mult).then_inc(S("smp_qx"), 1)
            dve.wait_ge(S("smp_r_turned"), 1)
            dve.tensor_tensor(kzs[:], ps[0:TS, 2, 0:2 * P], stable("zeta", TS), ALU.mult).then_inc(S("smp_kz"), 1)
            dve.wait_ge(S("smp_inner"), 1)
            sdecay = stable("decay", TS).rearrange("p (h t) -> p h t", h=RH)
            for e in range(2):
                dve.tensor_tensor(by_half(ins_[:])[:, e], ps[0:TS, 7 - e, 0:2 * TS].rearrange("p (j t) -> p j t", j=2), by_half(sdecay)[:, e], ALU.mult).then_inc(S("smp_decayed"), 1)
            dve.wait_ge(S("smp_kz"), 1)
            for b in range(NB):
                dve.tensor_scalar(kzm[:, b, :], kzs[:], stable("own", TS)[:, b:b + 1], None, ALU.mult).then_inc(S("smp_kz_masked"), 1)
            dve.wait_ge(S("smp_o_turned"), 1)
            stats(TS, lambda h: ps[0:TS, 4, h * RV:(h + 1) * RV], S("smp_var"))
            dve.wait_ge(S("smp_rstd"), 1)
            for h in range(RH):
                dve.tensor_scalar(ons[:, h, :], ps[0:TS, 4, h * RV:(h + 1) * RV], gmv[0:TS, 2 * h:2 * h + 1], grs[0:TS, h:h + 1], ALU.subtract, ALU.mult).then_inc(S("smp_normed"), 1)
            dve.wait_ge(S("smp_state_sum"), 1)
            for j in range(2):
                dve.scalar_tensor_tensor(sst[:, :, j, :], sst[:, :, j, :], stable("gl")[:, j:j + 1], bank(2, 4).rearrange("p (b j e) -> p b j e", b=NB, j=2)[:, :, j, :],
                                         ALU.mult, ALU.add).then_inc(S("smp_state"), 1)

            for k in range(KB):
                dve.wait_ge(s_hi, KB + k + 1)
                dve.tensor_tensor(xlo[:, k, :], za[:, k, :] if k < 4 else zb[:, k, :], xhi[:, k, :].bitcast(F32), ALU.subtract).then_inc(s_lo, 1)
            dve.wait_ge(s_back[0], 64)

            def residual(u0, n0, hi, lo, g):
                return lambda u: prep_lo(u - u0, u - u0 + n0, hi, lo, g)

            run(U_OUT, 4, added(U_OUT), residual(U_OUT, 2 * KB, yhi, ylo, G_X))
            dve.wait_ge(s_back[1], 64)
            run(U_OUT + 4, 4, added(U_OUT), residual(U_OUT, 2 * KB, yhi, ylo, G_X))
            run(U_XQ, 8, scaled(xq, U_XQ), before=lambda c: invert(2, c))

            def cross(n2):
                for p in range(2):
                    n = n2 * 2 + p
                    dve.wait_ge(s_xs, n + 1)
                    st.did(dve.tensor_reduce(wmax, bank(2, 2).rearrange("p (h c) -> p h c", h=XH), AX.X, ALU.max))
                    st.settle()
                    dve.tensor_scalar(wneg[:, 0:XH], wmax, -1.0 / 16, None, ALU.mult).then_inc(s_xm, 1)
                    softmax_tail(0, XH, lambda h: xp[:, h, :], s_xe, 4 * n + 4, s_xp, sink=False)
                    dve.wait_ge(s_xoh, n + 1)
                    dve.tensor_tensor(cols(ylo, 0, KB, n), bank(6, 2).rearrange("p (k t) -> p k t", k=KB), cols(yhi, 0, KB, n).bitcast(F32), ALU.subtract).then_inc(s_xol, 1)

            st.loop(0, NQ // 2, cross)

            def kx_evac(b):
                for kb in range(2):
                    t = b * 2 + kb
                    dve.wait_ge(s_kT, t + 1)
                    wait(dve, s_ksc, t - 1)
                    dve.tensor_copy(kxT[:, kb, 4:8, :].rearrange("p k t -> p (k t)"), ps[:, 3 + 2 * kb, :]).then_inc(s_ked, 1)

            st.loop(0, NB, kx_evac)
            dve.wait_ge(s_ksc, 2 * NB)
            dve.tensor_copy(sxT[:].rearrange("p a r -> p (a r)"), ps[:, 6, 0:2 * P]).then_inc(S("sx_s_ready"), 1)
            dve.wait_ge(S("sx_s_turned"), 1)
            st.did(dve.tensor_reduce(wmax[:, 0:1], ps[:, 7, 0:NM], AX.X, ALU.max))
            st.settle()
            dve.tensor_scalar(wneg[:, 0:1], wmax[:, 0:1], -1.0 / 16, None, ALU.mult).then_inc(S("sx_max"), 1)
            softmax_tail(0, 1, lambda h: sxp[:], S("sx_exp"), 1, S("sx_probs"), sink=False)
            dve.wait_ge(s_xoh, NQ + 1)
            dve.tensor_tensor(ylo[:, :, TP:T], ps[:, 2, 0:KB * TS].rearrange("p (k t) -> p k t", k=KB), yhi[:, :, TP:T].bitcast(F32), ALU.subtract).then_inc(s_xol, 1)
            run(U_XO, 8, added(U_XO), residual(U_XO, 3 * KB, xhi, xlo, G_MLP))

            for f in range(FC):
                u0 = U_MLP + 16 * f

                def up(u):
                    for q in range(2):
                        split_lo(dve, u + q + 1, 1 - q)

                        def lo_part(c):
                            hc = (u - u0 + q + 8 * f) * 3 + c
                            dve.wait_ge(s_hhi, hc + 1)
                            dve.tensor_tensor(chunk(ylo, u - u0 + q, c), hsq[:, (q + c) % 2, :], chunk(yhi, u - u0 + q, c).bitcast(F32), ALU.subtract).then_inc(s_hlo, 1)

                        for c in range(NCH):
                            hc = (u - u0 + q + 8 * f) * 3 + c
                            if f == 0 and isinstance(u, int) and q == 0:
                                invert(3, c)
                            dve.wait_ge(s_mm, chunks_before(u + q) + c + 1)
                            wait(dve, s_sqr, hc - 1)
                            dve.scalar_tensor_tensor(relu[:, (q + c) % 2, :], ps[:, (q + c) % 2, 0:CW], 0.0, rstd[:, c * CW:(c + 1) * CW], ALU.max, ALU.mult).then_inc(s_relu, 1)
                            dve.wait_ge(s_relu, hc + 1)
                            dve.sem_inc(s_ev, 1)
                            if c:
                                lo_part(c - 1)
                        lo_part(NCH - 1)

                pairs(dve, u0, 8, up)
                run(u0 + 8, 8, added(u0 + 8), last=f == FC - 1)
            for c in range(NCH):
                invert(4, c)
            for k in range(KB):
                dve.scalar_tensor_tensor(hT[:, k, :], hT[:, k, :], gains[:, G_FIN, k:k + 1], rstd[:], ALU.mult, ALU.mult).then_inc(s_yT, 1)
            for t in range(XT):
                dve.wait_ge(s_yt, t + 1)
                if t >= 4:
                    dve.wait_ge(s_yout[t % 4], 16 * (t // 4))
                w = P if t < NQ else TS
                dve.tensor_copy(ytok[0:w, t % 4, 512:D], ps[0:w, 3 + 2 * (t % 2), :]).then_inc(s_yed, 1)


_INS = ["x_prompt", "x_sample", "mem_prompt", "cache_win_k", "cache_win_v", "state_ret", "cache_mem_k", "cache_mem_v", "g_mix", "w_in",
        "attn_sinks", "ret_gn_g", "ret_gn_b", "w_out", "g_xattn", "g_mem", "w_xq", "w_xk", "w_xv", "w_xo", "g_mlp", "w_up", "w_down", "g_final"]
_OUTS = [("y_prompt", (1, TP, D)), ("y_sample", (NB, DT, D)), ("p_win_k", (1, 1, WIN, NKV, HD)), ("p_win_v", (1, 1, WIN, NKV, HD)),
         ("p_ret", (1, 1, RH, RQ, RV)), ("p_mem_k", (1, 1, NM, XH, D // XH)), ("p_mem_v", (1, 1, NM, XH, D // XH)),
         ("s_win_k", (1, NB, WIN, NKV, HD)), ("s_win_v", (1, NB, WIN, NKV, HD)), ("s_ret", (1, NB, RH, RQ, RV))]


def kernel(**inputs):
    import concourse.bacc as bacc
    from concourse.bass_utils import run_bass_kernel_spmd

    nc = bacc.Bacc("TRN2", target_bir_lowering=False, num_devices=1)
    arrays, io = {}, {}
    given = {name: np.ascontiguousarray(inputs[name]) for name in _INS}
    given["tables"], given["sample_tables"] = tables()
    for name, a in given.items():
        arrays[f"in_{name}"] = a
        io[name] = nc.dram_tensor(f"in_{name}", a.shape, mybir.dt.from_np(a.dtype), kind="ExternalInput").ap()
    for name, shape in _OUTS:
        io[name] = nc.dram_tensor(f"out_{name}", shape, F32, kind="ExternalOutput").ap()
    layer(nc, io)
    r = run_bass_kernel_spmd(nc, [arrays], core_ids=[0])
    return tuple(r.results[0][f"out_{name}"] for name, _ in _OUTS)
```

```python
from contextlib import ExitStack

import numpy as np
import concourse.bass as bass
from concourse import mybir
from concourse.alu_op_type import AluOpType as ALU

ACT = mybir.ActivationFunctionType
AX = mybir.AxisListType
F32 = mybir.dt.float32
F32R = mybir.dt.float32r
ds = bass.ds

P = 128
D = 1024
KB = D // P
TP = 1024
NB = 8
DT = 4
TS = NB * DT
T = TP + TS
NCH = 3
CW = T // NCH
NQ = TP // P
WIN = 128
NH, NKV, G, HD = 8, 2, 4, 64
RH, RQ, RV = 4, 64, 128
NM = 256
XH = 4
DFF = 4096
FC = 4
RMS_EPS, GN_EPS = 1e-6, 1e-5
MASKED = -1e37

U_MEM = 0
U_IN = U_MEM + 16
U_RET = U_IN + 6
U_GATE = U_IN + 14
U_OUT = U_IN + 18
U_XQ = U_OUT + 8
U_XO = U_XQ + 8
U_XB = U_XO + 8
U_MLP = U_XB + 8
U_END = U_MLP + FC * 16
LOAD = 48

_T = {}
_at = 0
for _n, _w in (("ident", P), ("ones", P), ("dist", 2 * 256), ("decay", RH * P), ("xi", 2 * P), ("zeta", RH * RQ), ("gl", 2)):
    _T[_n] = (_at, _w)
    _at += _w
N_TAB = _at
_S = {}
_at = 0
for _n, _w in (("bias", NKV * 160), ("decay", RH * TS), ("xi", 2 * TS), ("zeta", RH * RQ), ("own", NB), ("sel", G), ("gl", 2)):
    _S[_n] = (_at, _w)
    _at += _w
N_STAB = _at

SLOPES = [2.0 ** (-8.0 * (i + 1) / NH) for i in range(NH)]


def tables():
    lg = np.log(1.0 - 2.0 ** (-5.0 - np.arange(RH))).astype(np.float32).astype(np.float64)
    t = np.zeros((P, N_TAB), np.float64)
    r = np.arange(P)

    def put(a, m, n, v):
        a[: v.shape[0], m[n][0]:m[n][0] + m[n][1]] = v.reshape(v.shape[0], -1)

    put(t, _T, "ident", np.eye(P))
    put(t, _T, "ones", np.ones((P, P)))
    dist = r[:, None] + WIN - np.arange(2 * WIN)[None]
    later = np.where((dist >= 0) & (dist < WIN), -dist, MASKED)
    first = np.where(np.arange(2 * WIN)[None] < WIN, MASKED, later)
    put(t, _T, "dist", np.stack([first, later], 1))
    d = r[None, :] - r[:, None]
    put(t, _T, "decay", np.stack([np.where(d >= 0, 0.125 * np.exp(lg[h] * np.maximum(d, 0)), 0.0) for h in range(RH)], 1))
    half = r // RQ
    put(t, _T, "xi", np.stack([np.exp((r[None, :] + 1.0) * lg[2 * j + half][:, None]) for j in range(2)], 1))
    put(t, _T, "zeta", np.repeat(0.125 * np.exp((P - 1.0 - r)[:, None] * lg[None]), RQ, 1))
    put(t, _T, "gl", np.stack([np.exp(P * lg[2 * j + half]) for j in range(2)], 1))

    s = np.zeros((P, N_STAB), np.float64)
    b, g, q = r // 16, (r // 4) % 4, r % 4
    bias = np.full((P, NKV, 160), MASKED)
    for kv in range(NKV):
        slope = 8.0 * np.array(SLOPES)[kv * G + g]
        c = np.arange(WIN)[None]
        dist = q[:, None] + WIN - c
        bias[:, kv, :WIN] = np.where((dist >= 0) & (dist < WIN), -slope[:, None] * dist, MASKED)
        c = np.arange(TS)[None]
        dist = q[:, None] - c % DT
        bias[:, kv, WIN:] = np.where((c // DT == b[:, None]) & (dist >= 0), -slope[:, None] * dist, MASKED)
    put(s, _S, "bias", bias)
    w = np.arange(TS)
    d = w[None, :] - w[:, None]
    same = (w[None, :] // DT == w[:, None] // DT) & (d >= 0)
    put(s, _S, "decay", np.stack([np.where(same, 0.125 * np.exp(lg[h] * np.maximum(d, 0)), 0.0) for h in range(RH)], 1))
    put(s, _S, "xi", np.stack([np.exp((w[None, :] % DT + 1.0) * lg[2 * j + half][:, None]) for j in range(2)], 1))
    put(s, _S, "zeta", np.repeat(0.125 * np.exp((DT - 1.0 - w % DT)[:, None] * lg[None]), RQ, 1))
    put(s, _S, "own", (w[:, None] // DT == np.arange(NB)[None]).astype(float))
    put(s, _S, "sel", (g[:, None] == np.arange(G)[None]).astype(float))
    put(s, _S, "gl", np.stack([np.exp(DT * lg[2 * j + half]) for j in range(2)], 1))
    return t.astype(np.float32), s.astype(np.float32)


def chunks_before(u, memory=False):
    if memory or (isinstance(u, int) and u <= U_IN):
        return u
    return u * 3 - 2 * U_IN


def wait(eng, sem, value):
    if isinstance(value, int) and value <= 0:
        return
    eng.wait_ge(sem, value)


class Steps:

    def __init__(self, eng, sem):
        self.eng, self.sem, self.n, self.more = eng, sem, 0, 0

    def did(self, ins):
        ins.then_inc(self.sem, 1)
        self.n += 1

    def settle(self):
        wait(self.eng, self.sem, self.n + self.more)

    def loop(self, first, last, body):
        before = self.n
        body(first)
        steps = self.n - before
        if last - first > 1:
            with self.eng.Fori(first + 1, last) as i:
                if steps:
                    self.more = i * steps - (first + 1) * steps
                body(i)
            self.more = 0
            self.n = before + steps * (last - first)


def layer(nc, io):
    with ExitStack() as ctx:
        start = (nc.sbuf_base + 31) // 32 * 32
        top = [start]

        def place(name, shape, dt=F32, at=None):
            size = 4 * int(np.prod(shape[1:]))
            if at is None:
                at = top[0]
                top[0] = at + (size + 31) // 32 * 32
            t = nc.alloc_sbuf_tensor_at(name, shape, dt, offset=at)
            return t, at

        BLK = T * 4
        hT, at_h = place("hT", [P, KB, T])
        xhi, at_x = place("xhi", [P, KB, T], F32R)
        xlo, at_xl = place("xlo", [P, KB, T], F32R)
        yhi, at_y = place("yhi", [P, KB, T], F32R)
        ylo, _ = place("ylo", [P, KB, T], F32R)
        raw, _ = place("raw", [P, 2, KB, P])
        whi, _ = place("whi", [P, 2, KB, P], F32R)
        wlo, _ = place("wlo", [P, 2, KB, P], F32R)
        tab, at_tab = place("tab", [P, N_TAB])
        ss, at_ss = place("ss", [P, T])
        sq, at_sq = place("sq", [P, T // 2])
        rstd, _ = place("rstd", [P, T])
        gains, _ = place("gains", [P, 5, KB])
        gn, _ = place("gn", [P, 2, RH])
        sink8, _ = place("sink8", [P, NH])
        small, _ = place("small", [P, 96])
        assert top[0] <= nc.sbuf_usable_end, top[0]

        ident = tab[:, _T["ident"][0]:_T["ident"][0] + P]
        ones = tab[:, _T["ones"][0]:_T["ones"][0] + P]

        def table(n):
            a, w = _T[n]
            return tab[:, a:a + w]

        G_MIX, G_X, G_MLP, G_FIN, G_MEM = range(5)

        memx, _ = place("memx", [P, 2, D], at=at_y)
        mnhi, _ = place("mnhi", [P, KB, NM], F32R, at=at_y + 8192)
        mnlo, _ = place("mnlo", [P, KB, NM], F32R, at=at_y + 16384)
        mkvT, _ = place("mkvT", [P, 16, NM], at=at_y + 24576)
        mkv, _ = place("mkv", [P, 2, 2 * D], at=at_y + 40960)
        xin, _ = place("xin", [P, 2, D], at=at_y + 57344)
        diag, _ = place("diag", [P, NQ + 1, P], at=at_y)

        za, _ = place("za", [P, 10, T], at=at_y)
        zb, _ = place("zb", [P, 8, T], at=at_h)
        at_m = at_y + 10 * BLK
        stq, _ = place("stq", [P, 2, G, P], at=at_m)
        stk, _ = place("stk", [P, 2, 2 * P], at=at_m + 4096)
        stv, _ = place("stv", [P, 2, 2 * P], at=at_m + 6144)
        sc, _ = place("sc", [P, 2, G, 2 * P], at=at_m + 8192)
        pT, _ = place("pT", [P, 2, G * P], at=at_m + 16384)
        vtok, _ = place("vtok", [P, 2, P], at=at_m + 20480)
        rq, _ = place("rq", [P, 2, 2, P], at=at_m)
        rqx, _ = place("rqx", [P, 2, 2, P], at=at_m + 2048)
        rk, _ = place("rk", [P, 2, 2, P], at=at_m + 4096)
        rv, _ = place("rv", [P, 2, RH, P], at=at_m + 6144)
        krz, _ = place("krz", [P, RH * RQ], at=at_m + 10240)
        vrt, _ = place("vrt", [P, RH * RV], at=at_m + 11264)
        inner, _ = place("inner", [P, RH, P], at=at_m + 13312)
        onrm, _ = place("onrm", [P, RH, RV], at=at_m + 15360)
        state, _ = place("state", [P, 2, 2, RV], at=at_m + 19456)
        smz, _ = place("smz", [P, 14, TS], at=at_m + 21504)
        pw, _ = place("pw", [P, 2 * P], at=at_m + 23296)
        kvtok, _ = place("kvtok", [TS, 2 * P], at=at_m + 24320)
        qxs, _ = place("qxs", [P, 2, NB, 2, DT], at=at_sq)
        stab, _ = place("stab", [P, N_STAB], at=at_ss)
        kc, _ = place("kc", [P, NB, P], at=at_y + 4 * BLK)
        vc, _ = place("vc", [P, NB, P], at=at_y + 4 * BLK + 4 * NB * P)
        sst, _ = place("sst", [P, NB, 2, RV], at=at_y)
        kzm, _ = place("kzm", [TS, NB, RH * RQ], at=at_y + 2 * BLK)
        off = [at_m]

        def scratch(name, shape):
            t, a = place(name, shape, at=off[0])
            off[0] += (4 * int(np.prod(shape[1:])) + 31) // 32 * 32
            return t

        kcT = scratch("kcT", [P, NB, P])
        sT = scratch("sT", [P, NKV * P])
        snT = scratch("snT", [TS, NKV * P])
        ssc = scratch("ssc", [P, NKV, 160])
        psT = scratch("psT", [P, NKV * P])
        pnT = scratch("pnT", [TS, NKV * P])
        kzs = scratch("kzs", [TS, RH * RQ])
        vrs = scratch("vrs", [TS, RH * RV])
        ins_ = scratch("ins_", [TS, RH, TS])
        oTs = scratch("oTs", [P, RH, TS])
        ons = scratch("ons", [TS, RH, RV])
        rfs = scratch("rfs", [P, RH, TS])
        assert off[0] <= at_m + 19456

        xq, _ = place("xq", [P, KB, T], at=at_x)
        mkT, _ = place("mkT", [P, KB, NM], at=at_xl)
        mv, _ = place("mv", [P, 2, D], at=at_xl + 8192)
        stx, _ = place("stx", [P, 2, KB, P], at=at_xl + 16384)
        xp, _ = place("xp", [P, XH, NM], at=at_xl + 24576)
        xpT, _ = place("xpT", [P, 2, XH * P], at=at_xl + 28672)
        kx, _ = place("kx", [P, 8, D], at=at_x)
        kxT, _ = place("kxT", [P, 2, KB, P], at=at_xl + 24576)
        sxT, _ = place("sxT", [P, 2, P], at=at_xl)
        sxp, _ = place("sxp", [P, NM], at=at_xl + 1024)
        pxT, _ = place("pxT", [P, 2, P], at=at_xl + 2048)
        xqs, _ = place("xqs", [P, KB, TS], at=at_xl + 32768)
        at_t = at_tab + 4 * 2 * P
        relu, _ = place("relu", [P, 2, CW], at=at_t)
        hsq, _ = place("hsq", [P, 2, CW], at=at_t + 2 * 4 * CW)
        hg, _ = place("hg", [P, KB, T], at=at_x)
        ytok, _ = place("ytok", [P, 4, D], at=at_y)

        ps = ctx.enter_context(nc.psum_tensor("ps", [P, 8, 512], F32))

        def bank(b, n=1):
            return ps[:, b:b + n, :].rearrange("p b c -> p (b c)")

        spill = nc.dram_tensor("spill", [KB, P, T], F32, kind="Internal").ap()
        mkT_d = nc.dram_tensor("mkT_d", [P, KB * NM], F32, kind="Internal").ap()

        sem = {}

        def S(name):
            if name not in sem:
                sem[name] = ctx.enter_context(nc.semaphore(name))
            return sem[name]

        block = ctx.enter_context(nc.Block())

        s_raw = [S("raw_loaded_even"), S("raw_loaded_odd")]
        s_raw1 = S("gate_raw_loaded")
        s_whi, s_wlo = S("w_hi_made"), S("w_lo_made")
        s_mm, s_ev = S("chunk_multiplied"), S("chunk_evacuated")

        def kpn(w):
            return w.rearrange("(k p) n -> p k n", p=P)

        def load_unit(sp, u, q, pieces):
            wait(sp, s_wlo, u - 1)
            for n, (dst, src) in enumerate(pieces):
                last = n == len(pieces) - 1
                sp.dma_start(dst, src).then_inc(s_raw[q], LOAD - 16 * n if last else 16)

        def split_hi(act, u, q, memory=False):
            act.wait_ge(s_raw[q], LOAD // 2 * (u - q) + LOAD)
            wait(act, s_mm, chunks_before(u - 1, memory))
            act.activation(whi[:, q], raw[:, q], ACT.Copy).then_inc(s_whi, 1)

        def load_single(sp, u, u0, loaded, src):
            wait(sp, s_wlo, u)
            sp.dma_start(raw[:, 0], src).then_inc(loaded, 16)

        def split_single(act, u, u0, loaded):
            act.wait_ge(loaded, (u - u0) * 16 + 16)
            act.wait_ge(s_mm, chunks_before(u))
            act.activation(whi[:, 0], raw[:, 0], ACT.Copy).then_inc(s_whi, 1)

        def split_lo(dve, u, q):
            dve.wait_ge(s_whi, u + 1)
            dve.tensor_tensor(wlo[:, q], raw[:, q], whi[:, q].bitcast(F32), ALU.subtract).then_inc(s_wlo, 1)

        def product(pe, u, q, c, hi, lo, w, memory=False, before=None, bank=None, count=1, last_block=None):
            wait(pe, s_ev, chunks_before(u, memory) + (c - 1 if before is None else before))
            out = ps[:, (q + c) % 2 if bank is None else bank, 0:w]
            for k in range(KB):
                if k == KB - 1 and last_block is not None:
                    pe.wait_ge(*last_block)
                x1, x2 = hi[:, k, c * w:c * w + w], lo[:, k, c * w:c * w + w]
                pe.matmul(out, whi[:, q, k, :], x1, start=k == 0, stop=False)
                pe.matmul(out, whi[:, q, k, :], x2, start=False, stop=False)
                mm = pe.matmul(out, wlo[:, q, k, :], x1, start=False, stop=k == KB - 1)
            mm.then_inc(s_mm, count)

        SPARE = 5

        def gemm_bank(u, q, c):
            after_norm = isinstance(u, int) and u in (U_XQ, U_MLP) and c == 2
            return SPARE if after_norm else (q + c) % 2

        def unit(pe, u, q, hi, lo, last_block=None, before=None, chunks=range(NCH)):
            pe.wait_ge(s_wlo, u + 1)
            for c in chunks:
                if before is not None:
                    before(c)
                bank = gemm_bank(u, q, c)
                product(pe, u, q, c, hi, lo, CW, last_block=last_block if c == 0 else None, bank=bank, before=0 if bank == SPARE else None)

        def pairs(eng, first, n_units, body):
            body(first)
            if n_units > 2:
                with eng.Fori(1, n_units // 2) as i:
                    body(i * 2 + first)

        def chunk(t, m, c):
            return t[:, ds(m, 1), c * CW:(c + 1) * CW].rearrange("p a t -> p (a t)")

        def row(t, m):
            return t[:, ds(m, 1), :].rearrange("p a t -> p (a t)")

        def cols(t, a, b, n):
            return t[:, a:b, ds(n * P, P)]

        s_tab, s_mem, s_x = S("tables_loaded"), S("memory_loaded"), [S("x_loaded_even"), S("x_loaded_odd")]
        s_msq, s_mvar, s_mpow, s_mn = S("memory_squares"), S("memory_variance"), S("memory_rstd"), S("memory_scaled")
        s_mnT, s_mhi, s_mlo = S("memory_turned"), S("memory_hi"), S("memory_lo")
        s_xT, s_xea, s_xed = S("x_turned"), S("x_evacuated_act"), S("x_evacuated_dve")
        s_mt, s_mta, s_mtd, s_mout = S("kv_turned"), S("kv_evacuated_act"), S("kv_evacuated_dve"), S("kv_stored")
        s_hi, s_lo, s_ss = S("operand_hi"), S("operand_lo"), S("squares_summed")
        s_nmm, s_rstd = S("norm_summed"), S("rstd_made")
        s_pool, s_dve, s_act = S("pool_steps"), S("dve_steps"), S("act_steps")
        s_spill, s_back = S("residual_spilled"), [S("residual_back_0"), S("residual_back_1")]
        s_silu = S("gate_silu")
        s_wst, s_vT, s_vt = S("win_staged"), S("win_v_turned"), S("win_v_ready")
        s_ws, s_wsb, s_wm, s_we = S("win_scores"), S("win_biased"), S("win_max"), S("win_exp")
        s_wp, s_wpT, s_wpe, s_wo, s_woe = S("win_probs"), S("win_p_turned"), S("win_pT_ready"), S("win_out"), S("win_out_kept")
        s_rst, s_rT, s_krz, s_vrt = S("ret_staged"), S("ret_turned"), S("ret_kz"), S("ret_v")
        s_ri, s_rin, s_ro, s_rs, s_rstate = S("ret_inner"), S("ret_decayed"), S("ret_out"), S("ret_state_sum"), S("ret_state")
        s_rvar, s_rrs, s_ron, s_roT, s_rf, s_rg = S("ret_var"), S("ret_rstd"), S("ret_normed"), S("ret_o_turned"), S("ret_affine"), S("ret_gated")
        s_sqx, s_diag, s_root = S("x_squared"), S("x_diagonals"), S("root_made")
        s_pwT, s_pwe, s_pret = S("last_window_turned"), S("last_window_ready"), S("ret_state_stored")
        s_sld, s_sst, s_out = S("sample_loaded"), S("sample_state_loaded"), S("stored")
        s_xld, s_xst = S("cross_kv_loaded"), S("cross_staged")
        s_xs, s_xm, s_xe, s_xp = S("cross_scores"), S("cross_max"), S("cross_exp"), S("cross_probs")
        s_xpT, s_xpe, s_xo, s_xoh, s_xol = S("cross_p_turned"), S("cross_pT_ready"), S("cross_out"), S("cross_hi"), S("cross_lo")
        s_kl = [S(f"sx_loaded_{i}") for i in range(8)]
        s_vl = [S(f"sx_values_loaded_{i}") for i in range(4)]
        s_kT, s_kea, s_ked, s_ksc, s_vx = S("sx_k_turned"), S("sx_k_act"), S("sx_k_dve"), S("sx_scores"), S("sx_values")
        s_relu, s_sqr, s_hhi, s_hlo = S("relu_made"), S("square_made"), S("hidden_hi"), S("hidden_lo")
        s_hg, s_yt, s_yea, s_yed = S("residual_gained"), S("y_turned"), S("y_evac_act"), S("y_evac_dve")
        s_yout = [S(f"y_stored_{i}") for i in range(4)]
        N_TABS = 9
        N_SLD = 3
        XT = NQ + 1
        N_OUT = 2 * (NB + 1) + 2

        half = T // 2
        EPS_N, EPS_G = RMS_EPS, GN_EPS
        msq, mvar, mrs, mhalf = small[:, 8:10], small[:, 10:12], small[:, 12:14], small[:, 16:24]
        sqx = small[:, 24:24 + NQ + 1]
        tok_rms = small[:, 24:24 + NQ + 1]
        wmax, wneg, wdif = small[:, 24:28], small[:, 28:36], small[:, 36:44]
        wsum, wsink, wrec = small[:, 44:52], small[:, 52:60], small[:, 60:68]
        gst, gmv = small[:, 68:92], small[:, 8:16]
        gvar, grs = small[:, 92:96], small[:, 0:4]

        def values_at(b):
            return (4 if b % 4 < 2 else 0) + b % 2 * 2

        def sx_load(eng, b, cache, slot0, loaded):
            for kb in range(2):
                eng.dma_start(kx[:, slot0 + kb, :], io[cache][0, b, kb * P:(kb + 1) * P].rearrange("k h d -> k (h d)")).then_inc(loaded(slot0 + kb), 16)

        @block.sync
        def _(sp):
            def stream(src, u0, n_units):
                def body(u):
                    for q in range(2):
                        load_unit(sp, u + q, q, [(raw[:, q], src[:, :, ds((u - u0 + q) * P, P)])])
                pairs(sp, u0, n_units, body)

            stream(kpn(io["w_xk"][0]), U_MEM, 8)
            stream(kpn(io["w_xv"][0]), U_MEM + 8, 8)
            wi = kpn(io["w_in"][0])

            def in_q(u):
                for q in range(2):
                    m = u - U_IN + q
                    load_unit(sp, u + q, q, [(raw[:, q, :, 0:HD], wi[:, :, ds(m * HD, HD)]),
                                             (raw[:, q, :, HD:P], wi[:, :, ds(m * HD + G * HD, HD)])])

            pairs(sp, U_IN, 4, in_q)
            stream(wi[:, :, 4 * P:], U_IN + 4, 10)

            def single(u0, n_units, loaded, src):
                def body(i):
                    load_single(sp, i + u0, u0, loaded, src[:, :, ds(i * P, P)])
                body(0)
                with sp.Fori(1, n_units) as i:
                    body(i)
                for q in range(2):
                    sp.sem_inc(s_raw[q], n_units // 2 * LOAD)
                sp.wait_ge(s_wlo, u0 + n_units)

            single(U_GATE, 4, s_raw1, wi[:, :, (U_GATE - U_IN) * P:])
            wo = io["w_out"][0]
            wo_0, wo_1 = (wo[j * G * HD:(j + 1) * G * HD, :].rearrange("(k p) n -> p k n", p=HD) for j in range(2))
            wo_r = kpn(wo[2 * G * HD:, :])

            def out_units(u):
                for q in range(2):
                    c = ds((u - U_OUT + q) * P, P)
                    load_unit(sp, u + q, q, [(raw[0:HD, q, 0:4, :], wo_0[:, :, c]), (raw[HD:P, q, 0:4, :], wo_1[:, :, c]),
                                             (raw[:, q, 4:8, :], wo_r[:, :, c])])

            pairs(sp, U_OUT, 8, out_units)
            stream(kpn(io["w_xq"][0]), U_XQ, 8)
            stream(kpn(io["w_xo"][0]), U_XO, 8)
            stream(kpn(io["w_xo"][0]), U_XB, 8)
            for c in range(FC):
                u0 = U_MLP + 16 * c
                stream(kpn(io["w_up"][0])[:, :, c * D:(c + 1) * D], u0, 8)
                stream(kpn(io["w_down"][0][c * D:(c + 1) * D, :]), u0 + 8, 8)
            yp, ys = io["y_prompt"][0], io["y_sample"].rearrange("b t d -> (b t) d")
            for t in range(XT):
                sp.wait_ge(s_yea, t + 1)
                sp.wait_ge(s_yed, t + 1)
                if t < NQ:
                    sp.dma_start(yp[t * P:(t + 1) * P, :], ytok[:, t % 4, :]).then_inc(s_yout[t % 4], 16)
                else:
                    sp.dma_start(ys, ytok[0:TS, t % 4, :]).then_inc(s_yout[t % 4], 16)
            for i in range(4):
                sp.wait_ge(s_yout[i], 16 * len(range(i, XT, 4)))
            sp.wait_ge(s_out, 16 * N_OUT)
            sp.wait_ge(s_pret, 32)
            sp.wait_ge(s_mout, 48)
            sp.wait_ge(S("smp_state_stored"), 16 * NB)

        @block.gpsimd
        def _(pool):
            st = Steps(pool, s_pool)

            def squares(m, parts):
                for n, (a, b, done) in enumerate(parts):
                    pool.wait_ge(*done)
                    h = row(hT, m)[:, a:b]
                    if isinstance(m, int) and m == 0:
                        last = pool.tensor_tensor(ss[:, a:b], h, h, ALU.mult)
                    else:
                        st.settle()
                        st.did(pool.tensor_tensor(sq[:, 0:b - a], h, h, ALU.mult))
                        st.settle()
                        last = pool.tensor_tensor(ss[:, a:b], ss[:, a:b], sq[:, 0:b - a], ALU.add)
                    if n < len(parts) - 1:
                        st.did(last)
                last.then_inc(s_ss, 1)

            def halves(done):
                return [(0, half, done), (half, T, done)]

            pool.dma_start(memx[:], io["mem_prompt"][0].rearrange("(t p) d -> p t d", p=P)).then_inc(s_mem, 16)
            pool.dma_start(tab[:], io["tables"]).then_inc(s_tab, 16)
            with nc.allow_non_contiguous_dma(reason="vectors of 1024 or 512 onto the partitions"):
                for n, g in ((G_MEM, io["g_mem"][0]), (G_MIX, io["g_mix"][0]), (G_X, io["g_xattn"][0]), (G_MLP, io["g_mlp"][0]), (G_FIN, io["g_final"])):
                    pool.dma_start(gains[:, n, :], g.rearrange("(k p) -> p k", p=P)).then_inc(s_tab, 16)
                pool.dma_start(gn[:, 0, :], io["ret_gn_g"][0].rearrange("h p -> p h")).then_inc(s_tab, 16)
                pool.dma_start(gn[:, 1, :], io["ret_gn_b"][0].rearrange("h p -> p h")).then_inc(s_tab, 16)
                pool.dma_start(sink8[:], io["attn_sinks"][0].partition_broadcast(P)).then_inc(s_tab, 16)
            pool.wait_ge(s_mvar, 1)
            pool.tensor_tensor(mrs, mvar, mhalf[:, 0:2], ALU.pow).then_inc(s_mpow, 1)

            for t in range(XT):
                wait(pool, s_xT, t - 1)
                wait(pool, s_sqx, t - 1)
                if t < NQ:
                    pool.dma_start(xin[:, t % 2, :], io["x_prompt"][0, t * P:(t + 1) * P, :]).then_inc(s_x[t % 2], 16)
                else:
                    pool.dma_start(xin[0:TS, t % 2, :], io["x_sample"].rearrange("b t d -> (b t) d")).then_inc(s_x[t % 2], 16)
            pool.wait_ge(s_xea, XT)
            pool.wait_ge(s_xed, XT)
            for k in range(KB):
                pool.dma_start(spill[k], hT[:, k, :]).then_inc(s_spill, 16)
            pool.wait_ge(s_ev, 16)
            pool.dma_start(mkT_d, mkvT[:, 0:KB, :].rearrange("p k t -> p (k t)")).then_inc(s_mout, 16)
            pool.wait_ge(s_mta, 4)
            pool.wait_ge(s_mtd, 4)
            pool.dma_start(io["p_mem_k"].rearrange("l b (t p) h d -> p (l b t) (h d)", p=P), mkv[:, :, 0:D]).then_inc(s_mout, 16)
            pool.dma_start(io["p_mem_v"].rearrange("l b (t p) h d -> p (l b t) (h d)", p=P), mkv[:, :, D:]).then_inc(s_mout, 16)

            pool.wait_ge(s_ev, chunks_before(U_IN + 6))

            def win_stage(n2):
                for p in range(2):
                    n = n2 * 2 + p
                    wait(pool, s_ws, n * 2 - 2)
                    prev = n if isinstance(n, int) and n == 0 else n - 1
                    pool.tensor_copy(stq[:, p], cols(za, 0, G, n)).then_inc(s_wst, 1)
                    for dst, b in ((stk, 4), (stv, 5)):
                        pool.tensor_copy(dst[:, p, 0:P], cols(za, b, b + 1, prev).rearrange("p a t -> p (a t)")).then_inc(s_wst, 1)
                        pool.tensor_copy(dst[:, p, P:2 * P], cols(za, b, b + 1, n).rearrange("p a t -> p (a t)")).then_inc(s_wst, 1)

            st.loop(0, NQ // 2, win_stage)

            pool.wait_ge(s_woe, NQ)
            pool.wait_ge(s_ev, chunks_before(U_GATE))

            def ret_stage(n, p):
                pool.tensor_copy(rk[:, p], cols(zb, 2, 4, n)).then_inc(s_rst, 1)
                pool.tensor_copy(rv[:, p], cols(zb, 4, 8, n)).then_inc(s_rst, 1)
                pool.tensor_copy(rq[:, p], cols(zb, 0, 2, n)).then_inc(s_rst, 1)
                pool.tensor_tensor(rqx[:, p], cols(zb, 0, 2, n), table("xi").rearrange("p (j t) -> p j t", j=2), ALU.mult).then_inc(s_rst, 1)

            def ret_norm(n2):
                for p in range(2):
                    n = n2 * 2 + p
                    pool.wait_ge(s_rvar, n + 1)
                    pool.tensor_tensor(grs, gvar, mhalf[:, 0:4], ALU.pow).then_inc(s_rrs, 1)
                    if not (isinstance(n2, int) and n2 == NQ // 2 - 1):
                        pool.wait_ge(s_ro, n + 1)
                        ret_stage(n + 2, p)

            ret_stage(0, 0)
            ret_stage(1, 1)
            pool.tensor_copy(smz[:, 0:6, :], za[:, 0:6, TP:T]).then_inc(S("smp_kept"), 1)
            pool.tensor_copy(smz[:, 6:14, :], zb[:, :, TP:T]).then_inc(S("smp_kept"), 1)
            pool.dma_start(stab[:], io["sample_tables"]).then_inc(s_sld, 16)
            pool.wait_ge(S("smp_kept"), 2)
            pool.wait_ge(s_pwT, 1)
            pool.dma_start(kc[:], io["cache_win_k"][0].rearrange("b k h d -> k b (h d)")).then_inc(s_sld, 16)
            pool.dma_start(vc[:], io["cache_win_v"][0].rearrange("b k h d -> k b (h d)")).then_inc(s_sld, 16)
            st.loop(0, NQ // 2 - 1, ret_norm)
            ret_norm(NQ // 2 - 1)
            pool.wait_ge(s_rstate, RH * NQ)
            for e in range(2):
                pool.dma_start(io["p_ret"][0, 0].rearrange("(j h) d e -> h d j e", h=2)[e], state[e * RQ:(e + 1) * RQ, :, e, :]).then_inc(s_pret, 16)

            pool.wait_ge(s_rst, 4 * NQ)
            pool.wait_ge(s_spill, 16 * KB)
            for k in range(4):
                pool.dma_start(hT[:, k, :], spill[k]).then_inc(s_back[0], 16)
            pool.wait_ge(s_lo, KB + 2)
            for b in range(NB):
                pool.dma_start(sst[:, b], io["state_ret"][0, b].rearrange("(j h) d e -> (h d) j e", h=2)).then_inc(s_sst, 16)
            pool.wait_ge(s_lo, 2 * KB)
            for k in range(4, KB):
                pool.dma_start(hT[:, k, :], spill[k]).then_inc(s_back[1], 16)
            pool.wait_ge(S("smp_var"), 1)
            pool.tensor_tensor(grs[0:TS], gvar[0:TS], mhalf[0:TS, 0:4], ALU.pow).then_inc(S("smp_rstd"), 1)
            pool.wait_ge(S("smp_affine"), 4)
            pool.wait_ge(s_silu, 4)
            pool.tensor_tensor(smz[:, 10:14, :], rfs[:], za[:, 6:10, TP:T], ALU.mult).then_inc(S("smp_gated"), 1)
            pool.wait_ge(S("smp_state"), 2)
            for b in range(NB):
                pool.dma_start(io["s_ret"][0, b].rearrange("(j h) d e -> (h d) j e", h=2), sst[:, b]).then_inc(S("smp_state_stored"), 16)
            pool.wait_ge(S("smp_kv_ready"), 1)
            pool.wait_ge(s_pwe, 1)
            for name, cache, j in (("s_win_k", "cache_win_k", 0), ("s_win_v", "cache_win_v", 1)):
                pool.dma_start(io[name][0, :, 0:WIN - DT].rearrange("b k h d -> b (k h d)"),
                               io[cache][0, :, DT:WIN].rearrange("b k h d -> b (k h d)")).then_inc(s_out, 16)
                for b in range(NB):
                    pool.dma_start(io[name][0, b, WIN - DT:WIN].rearrange("t h d -> t (h d)"),
                                   kvtok[b * DT:b * DT + DT, j * P:j * P + P]).then_inc(s_out, 16)
            pool.dma_start(io["p_win_k"].rearrange("l b k h d -> (l b k) (h d)"), pw[:, 0:P]).then_inc(s_out, 16)
            pool.dma_start(io["p_win_v"].rearrange("l b k h d -> (l b k) (h d)"), pw[:, P:2 * P]).then_inc(s_out, 16)
            def residual_squares(u0, before, last_chunk=False):
                def body(u):
                    for q in range(2):
                        if not (isinstance(u, int) and u == u0 and q == 0):
                            pool.wait_ge(s_ss, before + (u - u0) + q)
                        m = u - u0 + q
                        if last_chunk:
                            squares(m, [(2 * CW, T, (s_ev, chunks_before(u + q + 1)))])
                        elif isinstance(u, int) and u + q == U_END - 1:
                            squares(m, [(c * CW, (c + 1) * CW, (s_ev, chunks_before(u + q) + c + 1)) for c in range(2)])
                            pool.wait_ge(s_ss, before + m + 1)
                            squares(m, [(2 * CW, T, (s_ev, chunks_before(u + q + 1)))])
                        else:
                            squares(m, halves((s_ev, chunks_before(u + q + 1))))
                body(u0)
                st.loop(1, 3, lambda i: body(i * 2 + u0))
                body(u0 + 6)

            residual_squares(U_OUT, 0)

            def x_stage(n2):
                for p in range(2):
                    n = n2 * 2 + p
                    wait(pool, s_xs, n - 1)
                    pool.tensor_copy(stx[:, p], cols(xq, 0, KB, n)).then_inc(s_xst, 1)

            pool.wait_ge(s_mm, chunks_before(U_XQ))
            pool.wait_ge(s_mout, 48)
            pool.dma_start(mkT[:].rearrange("p k t -> p (k t)"), mkT_d).then_inc(s_xld, 16)
            pool.dma_start(mv[:], io["p_mem_v"].rearrange("l b (t p) h d -> p (l b t) (h d)", p=P)).then_inc(s_xld, 16)
            pool.wait_ge(s_ev, chunks_before(U_XO))
            st.loop(0, NQ // 2, x_stage)

            pool.tensor_copy(xqs[:], xq[:, :, TP:T]).then_inc(S("sx_q_kept"), 1)
            pool.wait_ge(S("sx_q_kept"), 1)
            pool.wait_ge(s_xst, NQ)

            def xo_squares(m):
                u = U_XO + m
                pool.wait_ge(s_ss, KB + m)
                squares(m, [(0, CW, (s_ev, chunks_before(u) + 2)), (CW, 2 * CW, (s_ev, chunks_before(u) + 3))])

            for b in range(2):
                sx_load(pool, b, "cache_mem_k", 2 * b, lambda slot: s_kl[slot])
            for b in range(2):
                sx_load(pool, b, "cache_mem_v", values_at(b), lambda slot: s_kl[slot])
            for b in range(2, NB):
                pool.wait_ge(s_kT, 2 * b - 2)
                sx_load(pool, b, "cache_mem_k", b % 2 * 2, lambda slot: s_kl[slot])
                if b in (4, 6):
                    xo_squares(b // 2 - 2)
            for b in range(2, 4):
                pool.wait_ge(s_kT, 2 * (NB - 3 + b))
                sx_load(pool, b, "cache_mem_v", values_at(b), lambda slot: s_kl[slot])
            for m in range(2, KB):
                xo_squares(m)
            residual_squares(U_XB, 2 * KB, last_chunk=True)
            residual_squares(U_END - 8, 3 * KB)

        @block.scalar
        def _(act):
            def copy(out, in_):
                return act.activation(out, in_, ACT.Copy)

            def prep_hi(m, dst, g, done):
                act.wait_ge(*done)
                act.activation(row(dst, m), row(hT, m), ACT.Copy, scale=gains[:, g, ds(m, 1)]).then_inc(s_hi, 1)

            def root(n):
                act.wait_ge(s_ev, chunks_before({2: U_OUT, 3: U_XO}[n]))
                for c in range(NCH):
                    act.wait_ge(s_nmm, 3 * (n - 1) + c + 1)
                    act.activation(rstd[:, c * CW:(c + 1) * CW], ps[:, 2 + c, 0:CW], ACT.Sqrt, scale=1.0 / D, bias=small[:, 4:5]).then_inc(s_root, 1)

            def ahead(u, q, memory=False):
                split_hi(act, u + q + 1, 1 - q, memory)

            act.wait_ge(s_mem, 16)
            for t in range(2):
                act.activation(mkv[:, t, 0:D], memx[:, t, :], ACT.Square, accum_out=msq[:, t:t + 1]).then_inc(s_msq, 1)
            split_hi(act, 0, 0)
            act.wait_ge(s_mnT, 1)
            for k in range(KB):
                act.activation(mnhi[:, k, :], ps[:, 2 + k // 2, (k % 2) * NM:(k % 2) * NM + NM], ACT.Copy, scale=gains[:, G_MEM, k:k + 1]).then_inc(s_mhi, 1)

            def square_x(t, r, w):
                act.wait_ge(s_x[r], (t - r) * 8 + 16)
                wait(act, s_sqx, t)
                act.activation(ss[0:w, 0:D], xin[0:w, r, :], ACT.Square, accum_out=sqx[0:w, ds(t, 1)]).then_inc(s_sqx, 1)

            def mem_body(i):
                for r in range(2):
                    for q in range(2):
                        ahead(i * 4 + 2 * r, q, memory=True)
                    t = i * 2 + r
                    square_x(t, r, P)
                    act.wait_ge(s_xT, t + 1)
                    copy(hT[:, 0:4, ds(t * P, P)], ps[:, 2 + 2 * r, :].rearrange("p (k t) -> p k t", k=4)).then_inc(s_xea, 1)

            Steps(act, s_act).loop(0, 4, mem_body)
            square_x(NQ, 0, TS)
            act.wait_ge(s_sqx, XT)
            for w, a, b in ((P, 0, NQ), (TS, NQ, XT)):
                act.activation(sqx[0:w, a:b], sqx[0:w, a:b], ACT.Sqrt, scale=1.0 / D, bias=small[0:w, 4:5]).then_inc(s_root, 1)
            act.wait_ge(s_xT, XT)
            copy(hT[:, 0:4, TP:T], ps[:, 2, :].rearrange("p (k t) -> p k t", k=4)[:, :, 0:TS]).then_inc(s_xea, 1)
            for c, b in enumerate((6, 7, 1)):
                act.wait_ge(s_nmm, c + 1)
                w = min((c + 1) * 4 * P, T) - c * 4 * P
                copy(rstd[:, c * 4 * P:c * 4 * P + w], ps[:, b, 0:w]).then_inc(s_rstd, 1)
            for k in range(KB):
                prep_hi(k, xhi, G_MIX, (s_xea, XT) if k < 4 else (s_xed, XT))
            for s in range(0, 8, 2):
                act.wait_ge(s_mt, s + 1)
                copy(mkv[:, s // 4, (s % 4) * 512:(s % 4) * 512 + 512], ps[:, 2 + s % 4, :]).then_inc(s_mta, 1)

            def plain_in(u):
                for q in range(2):
                    ahead(u, q)

            pairs(act, U_IN, 6, plain_in)

            def win_exp(n, kv):
                j = n * 2 + kv
                act.wait_ge(s_wm, j + 1)
                for g in range(G):
                    c = kv * G + g
                    act.activation(sc[:, kv, g, :], sc[:, kv, g, :], ACT.Exp, scale=0.125, bias=wneg[:, c:c + 1],
                                   accum_out=wsum[:, c:c + 1]).then_inc(s_we, 1)
                act.activation(wsink[:, kv * G:kv * G + G], wdif[:, kv * G:kv * G + G], ACT.Exp, scale=0.125).then_inc(s_we, 1)

            def win_v(n):
                act.wait_ge(s_vT, n + 1)
                copy(vtok[:].rearrange("p a d -> p (a d)"), ps[:, 7, 0:2 * P]).then_inc(s_vt, 1)

            def win_pT(n, kv):
                act.wait_ge(s_wpT, n * 2 + kv + 1)
                copy(pT[:].rearrange("p a t -> p (a t)"), bank(4, 2)).then_inc(s_wpe, 1)

            def win(n2):
                for p in range(2):
                    n = n2 * 2 + p
                    end = isinstance(n, int) and n == NQ - 1
                    if not end:
                        split_hi(act, n + U_RET + 1, 1 - p)
                    win_exp(n, 1)
                    win_pT(n, 0)
                    if not end:
                        win_exp(n + 1, 0)
                    win_pT(n, 1)
                    act.wait_ge(s_wo, n * 2 + 2)
                    copy(cols(za, 0, G, n), ps[:, 6, :].rearrange("p (g t) -> p g t", g=G)).then_inc(s_woe, 1)
                    if not end:
                        win_v(n + 1)

            win_v(0)
            win_exp(0, 0)
            Steps(act, s_act).loop(0, NQ // 2 - 1, win)
            win(NQ // 2 - 1)

            def ret_v(n):
                act.wait_ge(s_rT, n * 2 + 2)
                copy(vrt[:], ps[:, 3, :]).then_inc(s_vrt, 1)

            def silu(m):
                act.wait_ge(s_ev, chunks_before(m + U_GATE + 1))
                act.activation(row(za, m + 6), row(za, m + 6), ACT.Silu).then_inc(s_silu, 1)

            def ret(n2):
                for p in range(2):
                    n = n2 * 2 + p
                    if p == 0:
                        split_single(act, n2 + U_GATE, U_GATE, s_raw1)
                    if not (isinstance(n, int) and n == NQ - 1):
                        ret_v(n + 1)
                    if p == 0 and not (isinstance(n, int) and n == 0):
                        silu(n2 - 1)
                    act.wait_ge(s_roT, n + 1)
                    for h in range(RH):
                        act.activation(cols(zb, 4 + h, 5 + h, n).rearrange("p a t -> p (a t)"), ps[:, 7, h * P:(h + 1) * P], ACT.Identity,
                                       scale=gn[:, 0, h:h + 1], bias=gn[:, 1, h:h + 1]).then_inc(s_rf, 1)

            act.wait_ge(s_pwT, 1)
            copy(pw[:], ps[:, 2, 0:2 * P]).then_inc(s_pwe, 1)
            ret_v(0)
            Steps(act, s_act).loop(0, NQ // 2 - 1, ret)
            ret(NQ // 2 - 1)
            silu(RH - 1)
            act.wait_ge(s_mm, chunks_before(U_OUT))
            split_hi(act, U_OUT, 0)

            def mixed_hi(blocks):
                for k in blocks:
                    if k >= 4:
                        act.wait_ge(s_rg, k - 3)
                    copy(xhi[:, k, 0:TP], za[:, k, 0:TP] if k < 4 else zb[:, k, 0:TP]).then_inc(s_hi, 1)

            act.wait_ge(S("smp_windows_turned"), 1)
            copy(kcT[:].rearrange("p b k -> p (b k)"), bank(2, 2)).then_inc(S("smp_turned_ready"), 1)
            mixed_hi(range(6))
            act.wait_ge(S("smp_max"), 1)
            for kv in range(NKV):
                act.activation(ssc[:, kv, :], ssc[:, kv, :], ACT.Exp, scale=0.125, bias=wneg[:, kv:kv + 1], accum_out=wsum[:, kv:kv + 1]).then_inc(S("smp_exp"), 1)
            act.activation(wsink[:, 0:NKV], wdif[:, 0:NKV], ACT.Exp, scale=0.125).then_inc(S("smp_exp"), 1)
            act.wait_ge(S("smp_p_turned"), 1)
            copy(psT[:], ps[:, 5, 0:2 * P]).then_inc(S("smp_turned_ready"), 1)
            mixed_hi(range(6, KB))
            act.wait_ge(S("smp_out"), 1)
            copy(smz[:, 0:G, :].rearrange("p g (b t) -> p b g t", t=DT), ps[:, 4, 0:P].rearrange("p (b g t) -> p b g t", g=G, t=DT)).then_inc(S("smp_out_kept"), 1)
            act.wait_ge(S("smp_ret_steps"), 1)
            copy(vrs[:], ps[0:TS, 3, :]).then_inc(S("smp_ret_ready"), 1)
            act.wait_ge(S("smp_ret_out"), 1)
            for e in range(2):
                copy(oTs[:].rearrange("p (j e) (b t) -> p e j b t", e=2, t=DT)[:, e],
                     ps[:, 5, 0:4 * TS].rearrange("p (j b e t) -> p e j b t", j=2, e=2, t=DT)[:, e]).then_inc(S("smp_ret_ready"), 1)
            act.wait_ge(S("smp_o_turned"), 2)
            for h in range(RH):
                act.activation(rfs[:, h, :], ps[:, 7, h * TS:(h + 1) * TS], ACT.Identity, scale=gn[:, 0, h:h + 1], bias=gn[:, 1, h:h + 1]).then_inc(S("smp_affine"), 1)

            for i, m in ((0, 0), (4, 10)):
                if i:
                    act.wait_ge(S("smp_gated"), 1)
                else:
                    act.wait_ge(S("smp_out_kept"), 1)
                copy(xhi[:, i:i + 4, TP:T], smz[:, m:m + 4, :]).then_inc(S("smp_hi"), 1)
            def residual(u0, dst, g):
                def body(u):
                    for q in range(2):
                        ahead(u, q)
                        if isinstance(u, int) and u == U_OUT and q == 0:
                            act.wait_ge(S("smp_state_stored"), 16 * NB)
                        prep_hi(u - u0 + q, dst, g, (s_ev, chunks_before(u + q + 1)))
                pairs(act, u0, 8, body)

            residual(U_OUT, yhi, G_X)
            root(2)
            pairs(act, U_XQ, 6, plain_in)
            ahead(U_XQ + 6, 0)

            def cross_exp(n):
                act.wait_ge(s_xm, n + 1)
                wait(act, s_xpT, n)
                for h in range(XH):
                    act.activation(xp[:, h, :], ps[:, 2 + h // 2, (h % 2) * NM:(h % 2) * NM + NM], ACT.Exp, scale=1.0 / 16, bias=wneg[:, h:h + 1],
                                   accum_out=wsum[:, h:h + 1]).then_inc(s_xe, 1)

            def cross(n2):
                for p in range(2):
                    n = n2 * 2 + p
                    act.wait_ge(s_xpT, n + 1)
                    wait(act, s_xo, n)
                    copy(xpT[:].rearrange("p a t -> p (a t)"), bank(4, 2)).then_inc(s_xpe, 1)
                    if not (isinstance(n, int) and n == NQ - 1):
                        cross_exp(n + 1)
                    act.wait_ge(s_xo, n + 1)
                    copy(cols(yhi, 0, KB, n), bank(6, 2).rearrange("p (k t) -> p k t", k=KB)).then_inc(s_xoh, 1)

            split_hi(act, U_XO, 0)
            cross_exp(0)
            Steps(act, s_act).loop(0, NQ // 2 - 1, cross)
            cross(NQ // 2 - 1)

            def kx_evac(i):
                for r in range(2):
                    for kb in range(2):
                        t = i * 4 + (2 * r + kb)
                        act.wait_ge(s_kT, t + 1)
                        wait(act, s_ksc, t - 1)
                        copy(kxT[:, kb, 0:4, :].rearrange("p k t -> p (k t)"), ps[:, 2 + 2 * kb, :]).then_inc(s_kea, 1)

            def sx_keys(i):
                kx_evac(i)
                split_hi(act, i + U_XO + 1, (i + 1) % 2)

            for i in range(NB // 2):
                sx_keys(i)
            act.wait_ge(S("sx_max"), 1)
            act.activation(sxp[:], ps[:, 7, 0:NM], ACT.Exp, scale=1.0 / 16, bias=wneg[:, 0:1], accum_out=wsum[:, 0:1]).then_inc(S("sx_exp"), 1)
            act.wait_ge(S("sx_p_turned"), 1)
            copy(pxT[:].rearrange("p a r -> p (a r)"), ps[:, 6, 0:2 * P]).then_inc(S("sx_pT_ready"), 1)
            split_hi(act, U_XO + 5, 1)
            for b in range(4, NB):
                act.wait_ge(s_vx, b - 3)
                sx_load(act, b, "cache_mem_v", values_at(b), lambda slot: s_vl[slot // 2])
                if b % 2 == 1:
                    split_hi(act, U_XO + 4 + b // 2, b // 2 % 2)
            split_hi(act, U_XB, 0)
            act.wait_ge(s_vx, NB)
            copy(yhi[:, :, TP:T], ps[:, 2, 0:KB * TS].rearrange("p (k t) -> p k t", k=KB)).then_inc(s_xoh, 1)

            def last_chunk(u):
                for q in range(2):
                    ahead(u, q)
                    m = u - U_XB + q - 1
                    if not (isinstance(m, int) and m < 0):
                        prep_hi(m, xhi, G_MLP, (s_ev, chunks_before(u + q)))

            pairs(act, U_XB, 8, last_chunk)
            prep_hi(KB - 1, xhi, G_MLP, (s_ev, chunks_before(U_MLP)))
            root(3)

            for f in range(FC):
                u0 = U_MLP + 16 * f

                def up(u):
                    for q in range(2):
                        ahead(u, q)
                        for c in range(NCH):
                            b = (q + c) % 2
                            hc = (u - u0 + q + 8 * f) * 3 + c
                            act.wait_ge(s_relu, hc + 1)
                            wait(act, s_hlo, hc - 1)
                            act.activation(hsq[:, b, :], relu[:, b, :], ACT.Square).then_inc(s_sqr, 1)
                            act.wait_ge(s_sqr, hc + 1)
                            copy(chunk(yhi, u - u0 + q, c), hsq[:, b, :]).then_inc(s_hhi, 1)

                pairs(act, u0, 8, up)
                if f < FC - 1:
                    pairs(act, u0 + 8, 8, plain_in)

            def gained(m, a, b, done):
                act.wait_ge(s_ev, done)
                act.activation(row(hg, m)[:, a:b], row(hT, m)[:, a:b], ACT.Copy, scale=gains[:, G_FIN, ds(m, 1)]).then_inc(s_hg, 1)

            def down(u):
                for q in range(2):
                    ahead(u, q)
                    gained(u - (U_END - 8) + q, 0, T, chunks_before(u + q + 1))

            pairs(act, U_END - 8, 6, down)
            ahead(U_END - 2, 0)
            gained(KB - 2, 0, T, chunks_before(U_END - 1))
            for c in range(NCH):
                gained(KB - 1, c * CW, (c + 1) * CW, chunks_before(U_END - 1) + c + 1)
            for i in range(2):
                act.wait_ge(s_nmm, 3 * 3 + i + 1)
                a, b = ((0, 5), (5, NQ))[i]
                act.activation(tok_rms[:, a:b], ps[:, 6 + i, a:b], ACT.Sqrt, scale=1.0 / D, bias=small[:, 4:5]).then_inc(s_root, 1)
                if i == 1:
                    act.activation(tok_rms[0:TS, NQ:XT], ps[0:TS, 7, NQ:XT], ACT.Sqrt, scale=1.0 / D, bias=small[0:TS, 4:5]).then_inc(s_root, 1)
            for t in range(XT):
                act.wait_ge(s_yt, t + 1)
                act.wait_ge(s_rstd, 9 + (1 if t < 5 else 3))
                if t >= 4:
                    act.wait_ge(s_yout[t % 4], 16 * (t // 4))
                w = P if t < NQ else TS
                act.activation(ytok[0:w, t % 4, 0:512], ps[0:w, 2 + 2 * (t % 2), :], ACT.Copy, scale=tok_rms[0:w, t:t + 1]).then_inc(s_yea, 1)

        @block.tensor
        def _(pe):
            def norm_sum(n):
                pe.wait_ge(s_ss, KB if n == 2 else 3 * KB)
                for c in range(NCH):
                    pe.matmul(ps[:, 2 + c, 0:CW], ones, ss[:, c * CW:(c + 1) * CW], start=True, stop=True).then_inc(s_nmm, 1)

            def units(u0, n_units, hi, lo, last_block=None, before=None, chunks=range(NCH)):
                def body(u):
                    for q in range(2):
                        first = isinstance(u, int) and q == 0
                        unit(pe, u + q, q, hi, lo, last_block if first else None, before if first else None, chunks if first else range(NCH))
                pairs(pe, u0, n_units, body)

            def turn(out, in_):
                n = in_.shape[0]
                return pe.transpose(out, in_, ident[0:n, 0:n])

            pe.wait_ge(s_tab, 16 * N_TABS)
            pe.wait_ge(s_mn, 2)
            for k in range(KB):
                for t in range(2):
                    mm = turn(ps[:, 2 + k // 2, (k % 2) * NM + t * P:(k % 2) * NM + (t + 1) * P], memx[:, t, k * P:(k + 1) * P])
            mm.then_inc(s_mnT, 1)
            pe.wait_ge(s_mlo, KB)

            def turn_x(t, r, w):
                wait(pe, s_xea, t - 1)
                wait(pe, s_xed, t - 1)
                pe.wait_ge(s_x[r], (t - r) * 8 + 16)
                for k in range(KB):
                    mm = turn(ps[:, 2 + 2 * r + k // 4, (k % 4) * P:(k % 4) * P + w], xin[0:w, r, k * P:(k + 1) * P])
                mm.then_inc(s_xT, 1)

            def mem_body(i):
                for r in range(2):
                    for q in range(2):
                        u = i * 4 + 2 * r + q
                        pe.wait_ge(s_wlo, u + 1)
                        product(pe, u, q, 0, mnhi, mnlo, NM, memory=True)
                    turn_x(i * 2 + r, r, P)

            Steps(pe, s_act).loop(0, 4, mem_body)
            turn_x(NQ, 0, TS)
            pe.wait_ge(s_ev, 16)
            pe.wait_ge(s_diag, XT)
            for t in range(XT):
                w = P if t < NQ else TS
                mm = pe.matmul(ps[:, (6, 7, 1)[t // 4], (t % 4) * P:(t % 4) * P + w], ones[0:w, :], diag[0:w, t, 0:w], start=True, stop=True)
                if t % 4 == 3 or t == NQ:
                    mm.then_inc(s_nmm, 1)
            pe.wait_ge(s_xea, XT)
            pe.wait_ge(s_xed, XT)
            for s in range(8):
                if s >= 4:
                    pe.wait_ge(s_mta if s % 2 == 0 else s_mtd, (s - 4) // 2 + 1)
                for j in range(4):
                    mm = turn(ps[:, 2 + s % 4, j * P:(j + 1) * P], mkvT[:, (s % 4) * 4 + j, (s // 4) * P:(s // 4 + 1) * P])
                mm.then_inc(s_mt, 1)
            pe.wait_ge(s_rstd, 3)
            pe.wait_ge(s_lo, KB - 1)
            units(U_IN, 6, xhi, xlo, last_block=(s_lo, KB))
            pe.wait_ge(s_mta, 4)
            pe.wait_ge(s_mtd, 4)

            def win_turn_v(n, p):
                pe.wait_ge(s_wst, n * 5 + 5)
                wait(pe, s_vt, n)
                for a in range(2):
                    mm = turn(ps[:, 7, a * P:(a + 1) * P], stv[:, p, a * P:(a + 1) * P])
                mm.then_inc(s_vT, 1)

            def win_scores(n, p, kv):
                r = slice(kv * HD, (kv + 1) * HD)
                pe.wait_ge(s_wst, n * 5 + 5)
                wait(pe, s_wsb, n * 8 + 4 * kv)
                for g in range(G):
                    mm = pe.matmul(ps[:, 2 + g // 2, (g % 2) * 256:(g % 2) * 256 + 256], stq[r, p, g, :], stk[r, p, :], start=True, stop=True)
                mm.then_inc(s_ws, 1)

            def win_turn_p(n, kv):
                pe.wait_ge(s_wp, n * 8 + 4 * kv + 4)
                wait(pe, s_wpe, n * 2 + kv)
                for a in range(2):
                    for g in range(G):
                        mm = turn(ps[:, 4 + a, g * P:(g + 1) * P], sc[:, kv, g, a * P:(a + 1) * P])
                mm.then_inc(s_wpT, 1)

            def win_values(n, kv):
                r = slice(kv * HD, (kv + 1) * HD)
                pe.wait_ge(s_wpe, n * 2 + kv + 1)
                pe.wait_ge(s_vt, n + 1)
                wait(pe, s_woe, n)
                for a in range(2):
                    mm = pe.matmul(ps[r, 6, :], vtok[:, a, r], pT[:, a, :], start=a == 0, stop=a == 1)
                mm.then_inc(s_wo, 1)

            def win(n2):
                for p in range(2):
                    n = n2 * 2 + p
                    u = n + U_RET
                    end = isinstance(n, int) and n == NQ - 1
                    win_scores(n, p, 1)
                    pe.wait_ge(s_wlo, u + 1)
                    product(pe, u, p, 0, xhi, xlo, CW)
                    win_turn_p(n, 0)
                    if not end:
                        win_scores(n + 1, 1 - p, 0)
                    win_values(n, 0)
                    product(pe, u, p, 1, xhi, xlo, CW)
                    win_turn_p(n, 1)
                    product(pe, u, p, 2, xhi, xlo, CW)
                    win_values(n, 1)
                    if not end:
                        win_turn_v(n + 1, 1 - p)

            win_turn_v(0, 0)
            win_scores(0, 0, 0)
            Steps(pe, s_act).loop(0, NQ // 2 - 1, win)
            win(NQ // 2 - 1)

            def ret_turn(n, p):
                pe.wait_ge(s_rst, n * 4 + 4)
                wait(pe, s_krz, n)
                wait(pe, s_vrt, n)
                for a in range(2):
                    mm = turn(ps[:, 2, a * P:(a + 1) * P], rk[:, p, a, :])
                mm.then_inc(s_rT, 1)
                for h in range(RH):
                    mm = turn(ps[:, 3, h * P:(h + 1) * P], rv[:, p, h, :])
                mm.then_inc(s_rT, 1)

            def ret_inner(n, p):
                wait(pe, s_rin, n * 2)
                wait(pe, s_rf, n * 4 - 4)
                for h in range(RH):
                    r = slice((h % 2) * RQ, (h % 2 + 1) * RQ)
                    mm = pe.matmul(ps[:, 4 if h % 2 == 0 else 7, (h // 2) * P:(h // 2 + 1) * P], rk[r, p, h // 2, :], rq[r, p, h // 2, :], start=True, stop=True)
                mm.then_inc(s_ri, 1)

            def ret(n2):
                u = n2 + U_GATE
                for p in range(2):
                    n = n2 * 2 + p
                    end = isinstance(n, int) and n == NQ - 1
                    pe.wait_ge(s_rin, n * 2 + 2)
                    pe.wait_ge(s_vrt, n + 1)
                    wait(pe, s_rstate, n * RH)
                    pe.wait_ge(S("ret_state_zeroed"), 1)
                    wait(pe, s_ron, n * 4)
                    for j in range(2):
                        pe.matmul(ps[:, 5, j * 2 * RV:(j + 1) * 2 * RV], rqx[:, p, j, :], state[:, j].rearrange("p e v -> p (e v)"), start=True, stop=False, skip_group_check=True)
                        for h in (2 * j, 2 * j + 1):
                            mm = pe.matmul(ps[:, 5, h * RV:(h + 1) * RV], inner[:, h, :], vrt[:, h * RV:(h + 1) * RV], start=False, stop=True, skip_group_check=True)
                    mm.then_inc(s_ro, 1)
                    pe.wait_ge(s_krz, n + 1)
                    for h in range(RH):
                        r = slice((h % 2) * RQ, (h % 2 + 1) * RQ)
                        mm = pe.matmul(ps[r, 6, (h // 2) * RV:(h // 2 + 1) * RV], krz[:, h * RQ:(h + 1) * RQ], vrt[:, h * RV:(h + 1) * RV], start=True, stop=True)
                    mm.then_inc(s_rs, 1)
                    if not end:
                        ret_turn(n + 1, 1 - p)
                        ret_inner(n + 1, 1 - p)
                    if p == 0:
                        pe.wait_ge(s_wlo, u + 1)
                    product(pe, u, 0, p, xhi, xlo, CW, before=0)
                    pe.wait_ge(s_ron, n * 4 + 4)
                    wait(pe, s_rin, n * 2 + (2 if end else 4))
                    wait(pe, s_rf, n * 4)
                    for h in range(RH):
                        mm = turn(ps[:, 7, h * P:(h + 1) * P], onrm[:, h, :])
                    mm.then_inc(s_roT, 1)
                product(pe, u, 0, 2, xhi, xlo, CW)

            pe.wait_ge(s_woe, NQ)
            pe.wait_ge(s_vt, NQ)
            for a in range(2):
                mm = turn(ps[:, 2, a * P:(a + 1) * P], za[:, 4 + a, TP - WIN:TP])
            mm.then_inc(s_pwT, 1)
            pe.wait_ge(s_pwe, 1)
            ret_turn(0, 0)
            ret_inner(0, 0)
            Steps(pe, s_act).loop(0, NQ // 2 - 1, ret)
            ret(NQ // 2 - 1)
            pe.wait_ge(s_rf, 4 * NQ)
            pe.wait_ge(s_rstate, RH * NQ)
            pe.wait_ge(s_sld, 16 * N_SLD)
            for b in range(NB):
                mm = turn(ps[:, 2 + b // 4, (b % 4) * P:(b % 4 + 1) * P], kc[:, b, :])
            mm.then_inc(S("smp_windows_turned"), 1)
            for a in range(2):
                mm = turn(ps[0:TS, 4, a * P:(a + 1) * P], smz[:, 4 + a, :])
            mm.then_inc(S("smp_windows_turned"), 1)
            pe.wait_ge(S("smp_turned_ready"), 1)
            for kv in range(NKV):
                r = slice(kv * HD, (kv + 1) * HD)
                for b in range(NB):
                    mm = pe.matmul(ps[:, 5 + kv, b * 16:b * 16 + 16].rearrange("p (g t) -> p g t", t=DT), kcT[r, b, :],
                                   smz[r, 0:G, b * DT:b * DT + DT], start=True, stop=True)
            mm.then_inc(S("smp_scores"), 1)
            for kv in range(NKV):
                r = slice(kv * HD, (kv + 1) * HD)
                mm = pe.matmul(ps[0:TS, 5 + kv, P:2 * P].rearrange("p (b g t) -> p b g t", g=G, t=DT), smz[r, 4, :],
                               smz[r, 0:G, :].rearrange("p g (b t) -> p b g t", t=DT), start=True, stop=True)
            mm.then_inc(S("smp_scores"), 1)
            pe.wait_ge(S("smp_s_ready"), 2)
            for kv in range(NKV):
                turn(ps[:, 7, kv * 160:kv * 160 + WIN], sT[:, kv * P:(kv + 1) * P])
                mm = turn(ps[:, 7, kv * 160 + WIN:kv * 160 + 160], snT[:, kv * P:(kv + 1) * P])
            mm.then_inc(S("smp_s_turned"), 1)
            pe.wait_ge(S("smp_probs"), 2)
            for kv in range(NKV):
                turn(ps[:, 5, kv * P:(kv + 1) * P], ssc[:, kv, 0:WIN])
                mm = turn(ps[0:TS, 6, kv * P:(kv + 1) * P], ssc[:, kv, WIN:160])
            mm.then_inc(S("smp_p_turned"), 1)
            pe.wait_ge(S("smp_turned_ready"), 2)
            pe.wait_ge(S("smp_pn_ready"), 1)
            pe.wait_ge(S("smp_kv_ready"), 1)
            for kv in range(NKV):
                r = slice(kv * HD, (kv + 1) * HD)
                pe.matmul(ps[r, 4, 0:P], kvtok[:, P + kv * HD:P + (kv + 1) * HD], pnT[:, kv * P:(kv + 1) * P], start=True, stop=False, skip_group_check=True)
                for b in range(NB):
                    mm = pe.matmul(ps[r, 4, b * 16:(b + 1) * 16], vc[:, b, r], psT[:, kv * P + b * 16:kv * P + (b + 1) * 16],
                                   start=False, stop=b == NB - 1, skip_group_check=True)
            mm.then_inc(S("smp_out"), 1)
            for a in range(2):
                turn(ps[0:TS, 2, a * P:(a + 1) * P], smz[:, 8 + a, :])
            for h in range(RH):
                mm = turn(ps[0:TS, 3, h * P:(h + 1) * P], smz[:, 10 + h, :])
            mm.then_inc(S("smp_ret_steps"), 1)
            for h in range(RH):
                r = slice((h % 2) * RQ, (h % 2 + 1) * RQ)
                mm = pe.matmul(ps[0:TS, 7 - h % 2, (h // 2) * TS:(h // 2 + 1) * TS], smz[r, 8 + h // 2, :], smz[r, 6 + h // 2, :], start=True, stop=True)
            mm.then_inc(S("smp_ret_steps"), 1)
            pe.wait_ge(S("smp_decayed"), 2)
            pe.wait_ge(S("smp_ret_ready"), 1)
            pe.wait_ge(S("smp_qx"), 3)
            pe.wait_ge(s_sst, 16 * NB)
            for j in range(2):
                o = ps[:, 5, j * 2 * TS:(j + 1) * 2 * TS]
                for e in range(2):
                    h = 2 * j + e
                    pe.matmul(o.rearrange("p (b e t) -> p b e t", e=2, t=DT)[:, :, e, :], vrs[:, h * RV:(h + 1) * RV], ins_[:, h, :].rearrange("p (b t) -> p b t", t=DT),
                              start=j == 0 and e == 0, stop=False, skip_group_check=True)
                for b in range(NB):
                    mm = pe.matmul(o[:, b * 2 * DT:(b + 1) * 2 * DT], sst[:, b, j, :], qxs[:, j, b].rearrange("p e t -> p (e t)"),
                                   start=False, stop=b == NB - 1, skip_group_check=True)
            mm.then_inc(S("smp_ret_out"), 1)
            pe.wait_ge(S("smp_ret_ready"), 3)
            pe.wait_ge(S("smp_out_kept"), 1)
            for h in range(RH):
                mm = turn(ps[0:TS, 4, h * RV:(h + 1) * RV], oTs[:, h, :])
            mm.then_inc(S("smp_o_turned"), 1)
            pe.wait_ge(s_lo, 2 * KB)
            pe.wait_ge(s_ev, chunks_before(U_OUT))
            pe.wait_ge(s_wlo, U_OUT + 1)
            product(pe, U_OUT, 0, 0, xhi, xlo, CW)
            pe.wait_ge(S("smp_normed"), RH)
            for h in range(RH):
                mm = turn(ps[:, 7, h * TS:(h + 1) * TS], ons[:, h, :])
            mm.then_inc(S("smp_o_turned"), 1)
            pe.wait_ge(S("smp_kz_masked"), NB)
            pe.wait_ge(S("smp_out_kept"), 1)
            for b in range(NB):
                for h in range(RH):
                    r, s = slice((h % 2) * RQ, (h % 2 + 1) * RQ), b * 2 + h // 2
                    mm = pe.matmul(ps[r, 2 + s // 4, (s % 4) * RV:(s % 4 + 1) * RV], kzm[:, b, h * RQ:(h + 1) * RQ], vrs[:, h * RV:(h + 1) * RV], start=True, stop=True)
            mm.then_inc(S("smp_state_sum"), 1)

            pe.wait_ge(S("smp_lo"), 2)
            units(U_OUT, 8, xhi, xlo, chunks=range(1, NCH))
            pe.wait_ge(s_lo, 3 * KB - 1)
            units(U_XQ, 8, yhi, ylo, last_block=(s_lo, 3 * KB), before=lambda c: norm_sum(2) if c == 1 else None)
            pe.wait_ge(s_root, 2 + 3)

            pe.wait_ge(s_xld, 32)

            def cross_scores(n, p):
                pe.wait_ge(s_xst, n + 1)
                wait(pe, s_xe, n * 4)
                for h in range(XH):
                    for dd in range(2):
                        mm = pe.matmul(ps[:, 2 + h // 2, (h % 2) * NM:(h % 2) * NM + NM], stx[:, p, 2 * h + dd, :], mkT[:, 2 * h + dd, :], start=dd == 0, stop=dd == 1)
                mm.then_inc(s_xs, 1)

            def cross(n2):
                for p in range(2):
                    n = n2 * 2 + p
                    if not (isinstance(n, int) and n == NQ - 1):
                        cross_scores(n + 1, 1 - p)
                    pe.wait_ge(s_xp, n * 4 + 4)
                    wait(pe, s_xpe, n)
                    for a in range(2):
                        for h in range(XH):
                            mm = turn(ps[:, 4 + a, h * P:(h + 1) * P], xp[:, h, a * P:(a + 1) * P])
                    mm.then_inc(s_xpT, 1)
                    pe.wait_ge(s_xpe, n + 1)
                    wait(pe, s_xol, n)
                    for k in range(KB):
                        for a in range(2):
                            mm = pe.matmul(ps[:, 6 + k // 4, (k % 4) * P:(k % 4 + 1) * P], mv[:, a, k * P:(k + 1) * P], xpT[:, a, (k // 2) * P:(k // 2 + 1) * P], start=a == 0, stop=a == 1)
                    mm.then_inc(s_xo, 1)

            cross_scores(0, 0)
            Steps(pe, s_act).loop(0, NQ // 2 - 1, cross)
            cross(NQ // 2 - 1)
            pe.wait_ge(s_xpe, NQ)
            pe.wait_ge(s_xe, 4 * NQ)
            pe.wait_ge(s_xol, NQ)

            def xo_product(u, c):
                product(pe, u, u % 2, c, yhi, ylo, CW, bank=c, count=2 - c)

            def sx_turn(b):
                for kb in range(2):
                    slot = b % 2 * 2 + kb
                    pe.wait_ge(s_kl[slot], b // 2 * 16 + 16)
                    wait(pe, s_kea, 2 * b + kb - 1)
                    wait(pe, s_ked, 2 * b + kb - 1)
                    for k in range(KB):
                        mm = turn(ps[:, 2 + 2 * kb + k // 4, (k % 4) * P:(k % 4 + 1) * P], kx[:, slot, k * P:(k + 1) * P])
                    mm.then_inc(s_kT, 1)

            def sx_scores(b):
                for kb in range(2):
                    pe.wait_ge(s_kea, 2 * b + kb + 1)
                    pe.wait_ge(s_ked, 2 * b + kb + 1)
                    for h in range(XH):
                        o = kb * P + b * 16 + h * DT
                        for dd in range(2):
                            mm = pe.matmul(ps[:, 6, o:o + DT], kxT[:, kb, 2 * h + dd, :], xqs[:, 2 * h + dd, b * DT:(b + 1) * DT], start=dd == 0, stop=dd == 1)
                    mm.then_inc(s_ksc, 1)

            def sx_values(b):
                for kb in range(2):
                    slot = values_at(b) + kb
                    if b < 4:
                        pe.wait_ge(s_kl[slot], 16 * ((NB // 2 if slot < 4 else 0) + 1))
                    else:
                        pe.wait_ge(s_vl[slot // 2], 32)
                for k in range(KB):
                    for kb in range(2):
                        mm = pe.matmul(ps[:, 2, k * TS + b * DT:k * TS + (b + 1) * DT], kx[:, values_at(b) + kb, k * P:(k + 1) * P],
                                       pxT[:, kb, b * 16 + (k // 2) * DT:b * 16 + (k // 2 + 1) * DT], start=kb == 0, stop=kb == 1)
                mm.then_inc(s_vx, 1)

            pe.wait_ge(S("sx_q_kept"), 1)
            for b in range(NB):
                u, c = U_XO + b // 2, b % 2
                sx_turn(b)
                if c == 0:
                    pe.wait_ge(s_wlo, u + 1)
                xo_product(u, c)
                sx_scores(b)
            pe.wait_ge(S("sx_s_ready"), 1)
            for kb in range(2):
                mm = turn(ps[:, 7, kb * P:(kb + 1) * P], sxT[:, kb, :])
            mm.then_inc(S("sx_s_turned"), 1)
            pe.wait_ge(s_wlo, U_XO + 5)
            xo_product(U_XO + 4, 0)
            xo_product(U_XO + 4, 1)
            pe.wait_ge(S("sx_probs"), 1)
            for kb in range(2):
                mm = turn(ps[:, 6, kb * P:(kb + 1) * P], sxp[:, kb * P:(kb + 1) * P])
            mm.then_inc(S("sx_p_turned"), 1)
            pe.wait_ge(S("sx_pT_ready"), 1)
            for i in range(NB // 2):
                sx_values(2 * i)
                sx_values(2 * i + 1)
                if i < NB // 2 - 1:
                    u = U_XO + 5 + i
                    pe.wait_ge(s_wlo, u + 1)
                    xo_product(u, 0)
                    xo_product(u, 1)
            pe.wait_ge(s_xol, NQ + 1)

            def xb(u):
                for q in range(2):
                    pe.wait_ge(s_wlo, u + q + 1)
                    first = isinstance(u, int) and q == 0
                    product(pe, u + q, q, 2, yhi, ylo, CW, before=-1 if first else -3, bank=q, count=3)

            pairs(pe, U_XB, 8, xb)
            pe.wait_ge(s_lo, 4 * KB - 1)
            for f in range(FC):
                u0 = U_MLP + 16 * f
                if f == 0:
                    units(u0, 8, xhi, xlo, last_block=(s_lo, 4 * KB), before=lambda c: norm_sum(3) if c == 1 else None)
                else:
                    units(u0, 8, xhi, xlo)
                units(u0 + 8, 8, yhi, ylo, before=lambda c: pe.wait_ge(s_hlo, 24 * f + 21 + c + 1))
            pe.wait_ge(s_root, 2 + 6)

            def token_sums(tiles, b, n_squares):
                pe.wait_ge(s_ss, n_squares)
                for t in tiles:
                    w = P if t < NQ else TS
                    mm = pe.matmul(ps[0:w, b, t:t + 1], ss[:, t * P:t * P + w], ones[:, 0:1], start=True, stop=True)
                mm.then_inc(s_nmm, 1)

            token_sums(range(5), 6, 4 * KB)
            for t in range(XT):
                w = P if t < NQ else TS
                if t == 2:
                    token_sums(range(5, XT), 7, 4 * KB + 1)
                pe.wait_ge(s_hg, KB - 1 + (t * P + w - 1) // CW + 1)
                if t >= 2:
                    pe.wait_ge(s_yea, t - 1)
                    pe.wait_ge(s_yed, t - 1)
                for k in range(KB):
                    mm = turn(ps[0:w, 2 + 2 * (t % 2) + k // 4, (k % 4) * P:(k % 4 + 1) * P], hg[:, k, t * P:t * P + w])
                mm.then_inc(s_yt, 1)

        @block.vector
        def _(dve):
            st = Steps(dve, s_dve)

            def prep_lo(m, n, hi, lo, g):
                dve.wait_ge(s_hi, n + 1)
                dve.scalar_tensor_tensor(row(lo, m), row(hT, m), gains[:, g, ds(m, 1)], row(hi, m).bitcast(F32), ALU.mult, ALU.subtract).then_inc(s_lo, 1)

            def invert(n, c):
                dve.wait_ge(s_root, 2 + 3 * (n - 2) + c + 1)
                dve.reciprocal(rstd[:, c * CW:(c + 1) * CW], rstd[:, c * CW:(c + 1) * CW]).then_inc(s_rstd, 1)
                dve.wait_ge(s_rstd, 3 * (n - 1) + c + 1)

            def evac(u, q, dst_of, last=False, before=None):
                if not last:
                    split_lo(dve, u + 1, 1 - q)
                for c in range(NCH):
                    if before is not None:
                        before(c)
                    dve.wait_ge(s_mm, chunks_before(u) + c + 1)
                    dst_of(u, q, c).then_inc(s_ev, 1)

            def scaled(t, m0):
                def f(u, q, c):
                    return dve.tensor_tensor(chunk(t, u - m0, c), ps[:, gemm_bank(u, q, c), 0:CW], rstd[:, c * CW:(c + 1) * CW], ALU.mult)
                return f

            def added(m0):
                def f(u, q, c):
                    return dve.tensor_tensor(chunk(hT, u - m0, c), ps[:, (q + c) % 2, 0:CW], chunk(hT, u - m0, c), ALU.add)
                return f

            def run(u0, n_units, f, after=None, last=False, before=None):
                def body(u):
                    for q in range(2):
                        evac(u + q, q, f, before=before if isinstance(u, int) and q == 0 else None)
                        if after is not None:
                            after(u + q)
                if not last:
                    pairs(dve, u0, n_units, body)
                    return
                pairs(dve, u0, n_units - 2, body)
                for q in range(2):
                    evac(u0 + n_units - 2 + q, q, f, last=q == 1)

            dve.memset(mhalf, -0.5).then_inc(S("dve_constants"), 1)
            dve.memset(small[:, 4:5], EPS_N).then_inc(S("dve_constants"), 1)
            dve.wait_ge(s_msq, 2)
            dve.wait_ge(S("dve_constants"), 2)
            dve.tensor_scalar(mvar, msq, 1.0 / D, EPS_N, ALU.mult, ALU.add).then_inc(s_mvar, 1)
            dve.wait_ge(s_mpow, 1)
            for t in range(2):
                dve.tensor_scalar(memx[:, t, :], memx[:, t, :], mrs[:, t:t + 1], None, ALU.mult).then_inc(s_mn, 1)
            dve.wait_ge(s_tab, 16 * N_TABS)
            st.did(dve.tensor_scalar(sink8[:], sink8[:], 8.0, None, ALU.mult))
            split_lo(dve, 0, 0)
            for k in range(KB):
                dve.wait_ge(s_mhi, k // 2 * 2 + 2)
                dve.scalar_tensor_tensor(mnlo[:, k, :], ps[:, 2 + k // 2, (k % 2) * NM:(k % 2) * NM + NM], gains[:, G_MEM, k:k + 1], mnhi[:, k, :].bitcast(F32),
                                         ALU.mult, ALU.subtract).then_inc(s_mlo, 1)

            def mem_body(i):
                for r in range(2):
                    for q in range(2):
                        u = i * 4 + 2 * r + q
                        split_lo(dve, u + 1, 1 - q)
                        dve.wait_ge(s_mm, u + 1)
                        dve.tensor_copy(mkvT[:, ds(u, 1), :].rearrange("p a t -> p (a t)"), ps[:, q, 0:NM]).then_inc(s_ev, 1)
                    t = i * 2 + r
                    dve.wait_ge(s_xT, t + 1)
                    dve.tensor_copy(hT[:, 4:8, ds(t * P, P)], ps[:, 3 + 2 * r, :].rearrange("p (k t) -> p k t", k=4)).then_inc(s_xed, 1)

            st.loop(0, 4, mem_body)
            dve.wait_ge(s_xT, XT)
            dve.tensor_copy(hT[:, 4:8, TP:T], ps[:, 3, :].rearrange("p (k t) -> p k t", k=4)[:, :, 0:TS]).then_inc(s_xed, 1)
            for i, (w, a, b) in enumerate(((P, 0, NQ), (TS, NQ, XT))):
                dve.wait_ge(s_root, i + 1)
                st.did(dve.reciprocal(sqx[0:w, a:b], sqx[0:w, a:b]))
            st.settle()
            for t in range(XT):
                w = P if t < NQ else TS
                dve.tensor_scalar(diag[0:w, t, 0:w], ident[0:w, 0:w], sqx[0:w, t:t + 1], None, ALU.mult).then_inc(s_diag, 1)
            for k in range(KB):
                prep_lo(k, k, xhi, xlo, G_MIX)
            for s in range(1, 8, 2):
                dve.wait_ge(s_mt, s + 1)
                dve.tensor_copy(mkv[:, s // 4, (s % 4) * 512:(s % 4) * 512 + 512], ps[:, 2 + s % 4, :]).then_inc(s_mtd, 1)
            dve.wait_ge(s_rstd, 3)
            dve.wait_ge(s_mout, 48)
            run(U_IN, 6, scaled(za, U_IN))
            dve.wait_ge(s_spill, 16 * KB)

            def softmax_tail(c0, n, probs, exp_sem, exp_n, out_sem, sink=True):
                dve.wait_ge(exp_sem, exp_n)
                if sink:
                    st.did(dve.tensor_tensor(wsum[:, c0:c0 + n], wsum[:, c0:c0 + n], wsink[:, c0:c0 + n], ALU.add))
                    st.settle()
                st.did(dve.reciprocal(wrec[:, c0:c0 + n], wsum[:, c0:c0 + n]))
                st.settle()
                for g in range(n):
                    dve.tensor_scalar(probs(g), probs(g), wrec[:, c0 + g:c0 + g + 1], None, ALU.mult).then_inc(out_sem, 1)

            dist = table("dist").rearrange("p (v c) -> p v c", v=2)

            def win_max(n, kv):
                j, c0 = n * 2 + kv, kv * G
                dve.wait_ge(s_ws, j + 1)
                wait(dve, s_wpT, j - 1)
                which = 0 if isinstance(n, int) and n == 0 else 1
                for g in range(G):
                    dve.scalar_tensor_tensor(sc[:, kv, g, :], dist[:, which, :], 8.0 * SLOPES[c0 + g], ps[:, 2 + g // 2, (g % 2) * 256:(g % 2) * 256 + 256],
                                             ALU.mult, ALU.add).then_inc(s_wsb, 1)
                dve.wait_ge(s_wsb, j * 4 + 4)
                st.did(dve.tensor_reduce(wmax, sc[:, kv], AX.X, ALU.max))
                st.settle()
                st.did(dve.tensor_tensor(wmax, wmax, sink8[:, c0:c0 + G], ALU.max))
                st.settle()
                st.did(dve.tensor_scalar(wneg[:, c0:c0 + G], wmax, -0.125, None, ALU.mult))
                st.settle()
                dve.tensor_tensor(wdif[:, c0:c0 + G], sink8[:, c0:c0 + G], wmax, ALU.subtract).then_inc(s_wm, 1)

            def win_probs(n, kv):
                softmax_tail(kv * G, G, lambda g: sc[:, kv, g, :], s_we, n * 10 + 5 * kv + 5, s_wp)

            def win(n2):
                for p in range(2):
                    n = n2 * 2 + p
                    u = n + U_RET
                    end = isinstance(n, int) and n == NQ - 1

                    def evacuate(c):
                        dve.wait_ge(s_mm, chunks_before(u) + c + 1)
                        scaled(zb, U_RET)(u, p, c).then_inc(s_ev, 1)

                    win_max(n, 1)
                    if not end:
                        split_lo(dve, u + 1, 1 - p)
                    evacuate(0)
                    win_probs(n, 1)
                    if not end:
                        win_max(n + 1, 0)
                    evacuate(1)
                    if not end:
                        win_probs(n + 1, 0)
                    evacuate(2)

            win_max(0, 0)
            win_probs(0, 0)
            st.loop(0, NQ // 2 - 1, win)
            win(NQ // 2 - 1)

            dve.wait_ge(s_woe, NQ)
            dve.wait_ge(s_wpe, 2 * NQ)
            dve.memset(qxs[:], 0.0).then_inc(S("smp_qx"), 1)
            dve.memset(state[:], 0.0).then_inc(S("ret_state_zeroed"), 1)
            dve.wait_ge(S("ret_state_zeroed"), 1)
            gl = table("gl")
            decay = table("decay").rearrange("p (h t) -> p h t", h=RH)

            def by_half(t):
                return t.rearrange("p (j e) t -> p e j t", e=2)

            def stats(w, o_of, var_sem, meanwhile=None):
                for h in range(RH):
                    st.did(dve.bn_stats(gst[0:w, h * 6:(h + 1) * 6], o_of(h)))
                st.settle()
                if meanwhile is not None:
                    meanwhile()
                for h in range(RH):
                    st.did(dve.bn_aggr(gmv[0:w, h * 2:(h + 1) * 2], gst[0:w, h * 6:(h + 1) * 6]))
                st.settle()
                dve.tensor_scalar(gvar[0:w], gmv[0:w].rearrange("p (h m) -> p h m", m=2)[:, :, 1], EPS_G, None, ALU.add).then_inc(var_sem, 1)

            def ret_keys(n):
                dve.wait_ge(s_rT, n * 2 + 1)
                wait(dve, s_rs, n)
                dve.tensor_tensor(krz[:], ps[:, 2, 0:2 * P], table("zeta"), ALU.mult).then_inc(s_krz, 1)
                dve.wait_ge(s_ri, n + 1)
                for e, b in ((0, 4), (1, 7)):
                    dve.tensor_tensor(by_half(inner[:])[:, e], ps[:, b, 0:2 * P].rearrange("p (j t) -> p j t", j=2), by_half(decay)[:, e], ALU.mult).then_inc(s_rin, 1)

            def ret(n2):
                u = n2 + U_GATE
                for p in range(2):
                    n = n2 * 2 + p

                    def update():
                        dve.wait_ge(s_rs, n + 1)
                        for h in range(RH):
                            e, j = h % 2, h // 2
                            r = slice(e * RQ, (e + 1) * RQ)
                            dve.scalar_tensor_tensor(state[r, j, e, :], state[r, j, e, :], gl[r, j:j + 1], ps[r, 6, j * RV:(j + 1) * RV], ALU.mult, ALU.add).then_inc(s_rstate, 1)

                    dve.wait_ge(s_ro, n + 1)
                    stats(P, lambda h: ps[:, 5, h * RV:(h + 1) * RV], s_rvar, update)
                    if p == 0:
                        split_lo(dve, u, 0)
                    if not (isinstance(n, int) and n == NQ - 1):
                        ret_keys(n + 1)
                    dve.wait_ge(s_rrs, n + 1)
                    wait(dve, s_roT, n)
                    for h in range(RH):
                        dve.tensor_scalar(onrm[:, h, :], ps[:, 5, h * RV:(h + 1) * RV], gmv[:, 2 * h:2 * h + 1], grs[:, h:h + 1], ALU.subtract, ALU.mult).then_inc(s_ron, 1)
                    for c in (0,) if p == 0 else (1, 2):
                        dve.wait_ge(s_mm, chunks_before(u) + c + 1)
                        scaled(za, U_IN + 8)(u, 0, c).then_inc(s_ev, 1)

            ret_keys(0)
            st.loop(0, NQ // 2 - 1, ret)
            ret(NQ // 2 - 1)
            split_lo(dve, U_OUT, 0)
            dve.wait_ge(S("smp_windows_turned"), 2)
            dve.tensor_copy(kvtok[:], ps[0:TS, 4, 0:2 * P]).then_inc(S("smp_kv_ready"), 1)
            dve.wait_ge(s_rf, RH * NQ)
            for h in range(RH):
                dve.wait_ge(s_silu, h + 1)
                dve.tensor_tensor(zb[:, 4 + h, 0:TP], zb[:, 4 + h, 0:TP], za[:, 6 + h, 0:TP], ALU.mult).then_inc(s_rg, 1)

            def stable(n, w=P):
                a, k = _S[n]
                return stab[0:w, a:a + k]

            def mixed_lo(blocks):
                for k in blocks:
                    dve.wait_ge(s_hi, KB + k + 1)
                    dve.tensor_tensor(xlo[:, k, 0:TP], za[:, k, 0:TP] if k < 4 else zb[:, k, 0:TP], xhi[:, k, 0:TP].bitcast(F32), ALU.subtract).then_inc(s_lo, 1)

            mixed_lo(range(4))
            dve.wait_ge(S("smp_scores"), 2)
            dve.tensor_copy(sT[:].rearrange("p (k r) -> p k r", k=NKV), ps[:, 5:7, 0:P]).then_inc(S("smp_s_ready"), 1)
            dve.tensor_copy(snT[:].rearrange("p (k r) -> p k r", k=NKV), ps[0:TS, 5:7, P:2 * P]).then_inc(S("smp_s_ready"), 1)
            for kv in range(NKV):
                st.did(dve.tensor_tensor(wdif[:, kv * G:kv * G + G], sink8[:, kv * G:kv * G + G], stable("sel"), ALU.mult))
            st.settle()
            st.did(dve.tensor_reduce(wrec[:, 4:6], wdif.rearrange("p (k g) -> p k g", g=G), AX.X, ALU.add))
            dve.wait_ge(S("smp_s_turned"), 1)
            st.did(dve.tensor_tensor(ssc[:].rearrange("p k c -> p (k c)"), ps[:, 7, 0:320], stable("bias"), ALU.add))
            st.settle()
            st.did(dve.tensor_reduce(wmax[:, 0:2], ssc[:], AX.X, ALU.max))
            st.settle()
            st.did(dve.tensor_tensor(wmax[:, 0:2], wmax[:, 0:2], wrec[:, 4:6], ALU.max))
            st.settle()
            st.did(dve.tensor_scalar(wneg[:, 0:2], wmax[:, 0:2], -0.125, None, ALU.mult))
            st.settle()
            dve.tensor_tensor(wdif[:, 0:2], wrec[:, 4:6], wmax[:, 0:2], ALU.subtract).then_inc(S("smp_max"), 1)
            softmax_tail(0, 2, lambda kv: ssc[:, kv, :], S("smp_exp"), 3, S("smp_probs"))
            mixed_lo(range(4, 6))
            dve.wait_ge(S("smp_p_turned"), 1)
            dve.tensor_copy(pnT[:], ps[0:TS, 6, 0:2 * P]).then_inc(S("smp_pn_ready"), 1)
            dve.wait_ge(S("smp_qx"), 1)
            for e in range(2):
                r = slice(e * RQ, (e + 1) * RQ)
                dve.tensor_tensor(qxs[r, :, :, e, :], smz[r, 6:8, :].rearrange("p j (b t) -> p j b t", t=DT),
                                  stable("xi")[r].rearrange("p (j b t) -> p j b t", j=2, t=DT), ALU.mult).then_inc(S("smp_qx"), 1)
            dve.wait_ge(S("smp_ret_steps"), 1)
            dve.tensor_tensor(kzs[:], ps[0:TS, 2, 0:2 * P], stable("zeta", TS), ALU.mult).then_inc(S("smp_kz"), 1)
            dve.wait_ge(S("smp_ret_steps"), 2)
            sdecay = stable("decay", TS).rearrange("p (h t) -> p h t", h=RH)
            for e in range(2):
                dve.tensor_tensor(by_half(ins_[:])[:, e], ps[0:TS, 7 - e, 0:2 * TS].rearrange("p (j t) -> p j t", j=2), by_half(sdecay)[:, e], ALU.mult).then_inc(S("smp_decayed"), 1)
            dve.wait_ge(S("smp_kz"), 1)
            for b in range(NB):
                dve.tensor_scalar(kzm[:, b, :], kzs[:], stable("own", TS)[:, b:b + 1], None, ALU.mult).then_inc(S("smp_kz_masked"), 1)
            mixed_lo(range(6, KB))
            dve.wait_ge(S("smp_o_turned"), 1)
            stats(TS, lambda h: ps[0:TS, 4, h * RV:(h + 1) * RV], S("smp_var"))
            dve.wait_ge(S("smp_rstd"), 1)
            for h in range(RH):
                dve.tensor_scalar(ons[:, h, :], ps[0:TS, 4, h * RV:(h + 1) * RV], gmv[0:TS, 2 * h:2 * h + 1], grs[0:TS, h:h + 1], ALU.subtract, ALU.mult).then_inc(S("smp_normed"), 1)
            for i, m in ((0, 0), (4, 10)):
                dve.wait_ge(S("smp_hi"), i // 4 + 1)
                dve.tensor_tensor(xlo[:, i:i + 4, TP:T], smz[:, m:m + 4, :], xhi[:, i:i + 4, TP:T].bitcast(F32), ALU.subtract).then_inc(S("smp_lo"), 1)
            dve.wait_ge(S("smp_state_sum"), 1)
            for j in range(2):
                dve.scalar_tensor_tensor(sst[:, :, j, :], sst[:, :, j, :], stable("gl")[:, j:j + 1], bank(2, 4).rearrange("p (b j e) -> p b j e", b=NB, j=2)[:, :, j, :],
                                         ALU.mult, ALU.add).then_inc(S("smp_state"), 1)

            dve.wait_ge(s_back[0], 64)

            def residual(u0, n0, hi, lo, g):
                return lambda u: prep_lo(u - u0, u - u0 + n0, hi, lo, g)

            run(U_OUT, 4, added(U_OUT), residual(U_OUT, 2 * KB, yhi, ylo, G_X))
            dve.wait_ge(s_back[1], 64)
            dve.wait_ge(s_out, 16 * N_OUT)
            run(U_OUT + 4, 4, added(U_OUT), residual(U_OUT, 2 * KB, yhi, ylo, G_X))
            run(U_XQ, 8, scaled(xq, U_XQ), before=lambda c: invert(2, c), last=True)
            split_lo(dve, U_XO, 0)

            def cross_max(n):
                dve.wait_ge(s_xs, n + 1)
                st.did(dve.tensor_reduce(wmax, bank(2, 2).rearrange("p (h c) -> p h c", h=XH), AX.X, ALU.max))
                st.settle()
                dve.tensor_scalar(wneg[:, 0:XH], wmax, -1.0 / 16, None, ALU.mult).then_inc(s_xm, 1)

            def cross_probs(n):
                softmax_tail(0, XH, lambda h: xp[:, h, :], s_xe, n * 4 + 4, s_xp, sink=False)

            def cross(n2):
                for p in range(2):
                    n = n2 * 2 + p
                    end = isinstance(n, int) and n == NQ - 1
                    if not end:
                        cross_max(n + 1)
                        cross_probs(n + 1)
                    dve.wait_ge(s_xoh, n + 1)
                    dve.tensor_tensor(cols(ylo, 0, KB, n), bank(6, 2).rearrange("p (k t) -> p k t", k=KB), cols(yhi, 0, KB, n).bitcast(F32), ALU.subtract).then_inc(s_xol, 1)

            cross_max(0)
            cross_probs(0)
            st.loop(0, NQ // 2 - 1, cross)
            cross(NQ // 2 - 1)

            def xo_evacuate(u, c):
                dve.wait_ge(s_mm, chunks_before(u) + 2 + c)
                dve.tensor_tensor(chunk(hT, u - U_XO, c), ps[:, c, 0:CW], chunk(hT, u - U_XO, c), ALU.add).then_inc(s_ev, 2 - c)

            def sx_keys(i):
                for r in range(2):
                    for kb in range(2):
                        t = i * 4 + (2 * r + kb)
                        dve.wait_ge(s_kT, t + 1)
                        wait(dve, s_ksc, t - 1)
                        dve.tensor_copy(kxT[:, kb, 4:8, :].rearrange("p k t -> p (k t)"), ps[:, 3 + 2 * kb, :]).then_inc(s_ked, 1)
                    xo_evacuate(i + U_XO, r)
                split_lo(dve, i + U_XO + 1, (i + 1) % 2)

            for i in range(NB // 2):
                sx_keys(i)
            dve.wait_ge(s_ksc, 2 * NB)
            dve.tensor_copy(sxT[:].rearrange("p a r -> p (a r)"), ps[:, 6, 0:2 * P]).then_inc(S("sx_s_ready"), 1)
            dve.wait_ge(S("sx_s_turned"), 1)
            st.did(dve.tensor_reduce(wmax[:, 0:1], ps[:, 7, 0:NM], AX.X, ALU.max))
            st.settle()
            dve.tensor_scalar(wneg[:, 0:1], wmax[:, 0:1], -1.0 / 16, None, ALU.mult).then_inc(S("sx_max"), 1)
            softmax_tail(0, 1, lambda h: sxp[:], S("sx_exp"), 1, S("sx_probs"), sink=False)
            for c in range(2):
                xo_evacuate(U_XO + 4, c)

            def sx_values(i):
                split_lo(dve, i + U_XO + 5, (i + 1) % 2)
                for c in range(2):
                    xo_evacuate(i + U_XO + 5, c)

            for i in range(NB // 2 - 1):
                sx_values(i)
            split_lo(dve, U_XB, 0)
            dve.wait_ge(s_xoh, NQ + 1)
            dve.tensor_tensor(ylo[:, :, TP:T], ps[:, 2, 0:KB * TS].rearrange("p (k t) -> p k t", k=KB), yhi[:, :, TP:T].bitcast(F32), ALU.subtract).then_inc(s_xol, 1)

            def last_chunk(u0, n0, hi, lo, g):
                def body(u):
                    for q in range(2):
                        m = u - u0 + q
                        split_lo(dve, u + q + 1, 1 - q)
                        if not (isinstance(m, int) and m == 0):
                            prep_lo(m - 1, m + (n0 - 1), hi, lo, g)
                        dve.wait_ge(s_mm, chunks_before(u + q + 1))
                        dve.tensor_tensor(chunk(hT, m, 2), ps[:, q, 0:CW], chunk(hT, m, 2), ALU.add).then_inc(s_ev, 3)
                pairs(dve, u0, 8, body)
                prep_lo(KB - 1, KB - 1 + n0, hi, lo, g)

            last_chunk(U_XB, 3 * KB, xhi, xlo, G_MLP)

            for f in range(FC):
                u0 = U_MLP + 16 * f

                def up(u):
                    for q in range(2):
                        split_lo(dve, u + q + 1, 1 - q)

                        def lo_part(c):
                            hc = (u - u0 + q + 8 * f) * 3 + c
                            dve.wait_ge(s_hhi, hc + 1)
                            dve.tensor_tensor(chunk(ylo, u - u0 + q, c), hsq[:, (q + c) % 2, :], chunk(yhi, u - u0 + q, c).bitcast(F32), ALU.subtract).then_inc(s_hlo, 1)

                        for c in range(NCH):
                            hc = (u - u0 + q + 8 * f) * 3 + c
                            if f == 0 and isinstance(u, int) and q == 0:
                                invert(3, c)
                            dve.wait_ge(s_mm, chunks_before(u + q) + c + 1)
                            wait(dve, s_sqr, hc - 1)
                            dve.scalar_tensor_tensor(relu[:, (q + c) % 2, :], ps[:, gemm_bank(u + q, q, c) if q == 0 else (q + c) % 2, 0:CW], 0.0, rstd[:, c * CW:(c + 1) * CW], ALU.max, ALU.mult).then_inc(s_relu, 1)
                            dve.wait_ge(s_relu, hc + 1)
                            dve.sem_inc(s_ev, 1)
                            if c:
                                lo_part(c - 1)
                        lo_part(NCH - 1)

                pairs(dve, u0, 8, up)
                run(u0 + 8, 8, added(u0 + 8), last=f == FC - 1)
            for i, (a, b, w) in enumerate(((0, 5, P), (5, NQ, P), (NQ, XT, TS))):
                dve.wait_ge(s_root, 2 + 6 + i + 1)
                dve.reciprocal(tok_rms[0:w, a:b], tok_rms[0:w, a:b]).then_inc(s_rstd, 1)
            for t in range(XT):
                dve.wait_ge(s_yt, t + 1)
                dve.wait_ge(s_rstd, 9 + (1 if t < 5 else 3))
                if t >= 4:
                    dve.wait_ge(s_yout[t % 4], 16 * (t // 4))
                w = P if t < NQ else TS
                dve.tensor_scalar(ytok[0:w, t % 4, 512:D], ps[0:w, 3 + 2 * (t % 2), :], tok_rms[0:w, t:t + 1], None, ALU.mult).then_inc(s_yed, 1)


_INS = ["x_prompt", "x_sample", "mem_prompt", "cache_win_k", "cache_win_v", "state_ret", "cache_mem_k", "cache_mem_v", "g_mix", "w_in",
        "attn_sinks", "ret_gn_g", "ret_gn_b", "w_out", "g_xattn", "g_mem", "w_xq", "w_xk", "w_xv", "w_xo", "g_mlp", "w_up", "w_down", "g_final"]
_OUTS = [("y_prompt", (1, TP, D)), ("y_sample", (NB, DT, D)), ("p_win_k", (1, 1, WIN, NKV, HD)), ("p_win_v", (1, 1, WIN, NKV, HD)),
         ("p_ret", (1, 1, RH, RQ, RV)), ("p_mem_k", (1, 1, NM, XH, D // XH)), ("p_mem_v", (1, 1, NM, XH, D // XH)),
         ("s_win_k", (1, NB, WIN, NKV, HD)), ("s_win_v", (1, NB, WIN, NKV, HD)), ("s_ret", (1, NB, RH, RQ, RV))]


def kernel(**inputs):
    import concourse.bacc as bacc
    from concourse.bass_utils import run_bass_kernel_spmd

    nc = bacc.Bacc("TRN2", target_bir_lowering=False, num_devices=1)
    arrays, io = {}, {}
    given = {name: np.ascontiguousarray(inputs[name]) for name in _INS}
    given["tables"], given["sample_tables"] = tables()
    for name, a in given.items():
        arrays[f"in_{name}"] = a
        io[name] = nc.dram_tensor(f"in_{name}", a.shape, mybir.dt.from_np(a.dtype), kind="ExternalInput").ap()
    for name, shape in _OUTS:
        io[name] = nc.dram_tensor(f"out_{name}", shape, F32, kind="ExternalOutput").ap()
    layer(nc, io)
    r = run_bass_kernel_spmd(nc, [arrays], core_ids=[0])
    return tuple(r.results[0][f"out_{name}"] for name, _ in _OUTS)
```
